# Optimizing a Trainium2 kernel written in Bass

```python
import math
import jax, jax.numpy as jnp
from jax import lax
import numpy as np

D_MODEL = 1024
BATCH = 1
SEQ = 512
DEPTH = 2

CHUNK = 64
ROPE_THETA = 10000.0
EPS = 1e-6
HEAD_DIM = 64
Q_BLOCK = 128

A_Q_HEADS = 4
A_KV_HEADS = 2
WINDOW = 128
WIN_CHUNKS = WINDOW // CHUNK

B_Q_HEADS = 4
B_KV_RANK = 128
IDX_HEADS = 4
IDX_DIM = 32
TOPK_MAX = 256

C_HEADS = 4
C_VDIM = 2 * HEAD_DIM

A_WIDTH = A_Q_HEADS * HEAD_DIM
B_WIDTH = B_Q_HEADS * HEAD_DIM
C_WIDTH = C_HEADS * C_VDIM
D_MIX = A_WIDTH + B_WIDTH + C_WIDTH

IN_SIZES = (
    A_Q_HEADS * HEAD_DIM, A_KV_HEADS * HEAD_DIM, A_KV_HEADS * HEAD_DIM,
    B_Q_HEADS * HEAD_DIM, B_KV_RANK,
    IDX_HEADS * IDX_DIM, IDX_DIM, IDX_HEADS,
    C_HEADS * 2 * HEAD_DIM, C_HEADS * 2 * HEAD_DIM, C_HEADS * C_VDIM,
)
D_IN = sum(IN_SIZES)

D_FF = 2816
N_MOD = 9

kernel_name = "hymba_style_chunk_causal_hybrid_encoder"

def rms_norm(x, g):
    xf = x.astype(jnp.float32)
    y = xf * lax.rsqrt(jnp.mean(xf * xf, axis=-1, keepdims=True) + EPS)
    return (y * g.astype(jnp.float32)).astype(x.dtype)

def modulate(x, g, shift, scale):
    return rms_norm(x, g) * (1.0 + scale[:, None, :]) + shift[:, None, :]

def rope_tables(positions, dim):
    inv = ROPE_THETA ** (-jnp.arange(0, dim, 2, dtype=jnp.float32) / dim)
    ang = positions.astype(jnp.float32)[..., None] * inv
    return jnp.cos(ang)[:, :, None, :], jnp.sin(ang)[:, :, None, :]

def apply_rope(x, cos, sin):
    half = x.shape[-1] // 2
    xf = x.astype(jnp.float32)
    x1, x2 = xf[..., :half], xf[..., half:]
    return jnp.concatenate([x1 * cos - x2 * sin, x2 * cos + x1 * sin], axis=-1).astype(x.dtype)

def swiglu(h, w_in, w_out):
    g, u = jnp.split(h @ w_in, 2, axis=-1)
    return (jax.nn.silu(g) * u) @ w_out

def to_blocks(t, nb):
    return jnp.moveaxis(t.reshape((t.shape[0], nb, Q_BLOCK) + t.shape[2:]), 1, 0)

def from_blocks(t):
    nb, b, qb = t.shape[:3]
    return jnp.moveaxis(t, 0, 1).reshape((b, nb * qb) + t.shape[3:])

def shift_chunks(t, j):
    if j == 0:
        return t
    pad = [(0, 0)] * t.ndim
    pad[1] = (j, 0)
    return jnp.pad(t[:, :t.shape[1] - j], pad)

def swa_sink_attention(q, k, v, sinks):
    b, s, hq, d = q.shape
    g = k.shape[2]
    r = hq // g
    nc = s // CHUNK
    qc = q.reshape(b, nc, CHUNK, g, r, d)
    kc = k.reshape(b, nc, CHUNK, g, d)
    vc = v.reshape(b, nc, CHUNK, g, d)
    kb = jnp.concatenate([shift_chunks(kc, j) for j in range(WIN_CHUNKS - 1, -1, -1)], axis=2)
    vb = jnp.concatenate([shift_chunks(vc, j) for j in range(WIN_CHUNKS - 1, -1, -1)], axis=2)
    offs = WIN_CHUNKS - 1 - jnp.arange(WIN_CHUNKS * CHUNK) // CHUNK
    valid = jnp.arange(nc)[:, None] >= offs[None, :]
    logits = jnp.einsum('bnqgrd,bnkgd->bngrqk', qc, kb).astype(jnp.float32) * (d ** -0.5)
    logits = jnp.where(valid[None, :, None, None, None, :], logits, -jnp.inf)
    sink = jnp.broadcast_to(sinks.astype(jnp.float32).reshape(g, r)[None, None, :, :, None, None],
                            logits.shape[:-1] + (1,))
    p = jax.nn.softmax(jnp.concatenate([logits, sink], axis=-1), axis=-1)[..., :-1]
    out = jnp.einsum('bngrqk,bnkgd->bnqgrd', p.astype(v.dtype), vb)
    return out.reshape(b, s, hq * d)

def dsa_sparse_attention(q, k, v, q_idx, k_idx, w_idx):
    b, s, h, d = q.shape
    nb = s // Q_BLOCK
    topk = min(TOPK_MAX, s // 4)
    key_chunk = jnp.arange(s) // CHUNK

    def block(args):
        qb, qib, wb, blk = args
        q_chunk = (blk * Q_BLOCK + jnp.arange(Q_BLOCK)) // CHUNK
        adm = key_chunk[None, :] <= q_chunk[:, None]
        sc = jax.nn.relu(jnp.einsum('bqhe,bse->bqhs', qib, k_idx).astype(jnp.float32))
        score = jnp.einsum('bqh,bqhs->bqs', wb.astype(jnp.float32), sc)
        score = jnp.where(adm[None], score, -jnp.inf)
        _, idx = lax.top_k(score, topk)
        sel_valid = key_chunk[idx] <= q_chunk[None, :, None]
        k_sel = jax.vmap(lambda kk, ii: kk[ii])(k, idx)
        v_sel = jax.vmap(lambda vv, ii: vv[ii])(v, idx)
        logits = jnp.einsum('bqhd,bqkd->bqhk', qb, k_sel).astype(jnp.float32) * (d ** -0.5)
        logits = jnp.where(sel_valid[:, :, None, :], logits, -jnp.inf)
        p = jax.nn.softmax(logits, axis=-1)
        return jnp.einsum('bqhk,bqkd->bqhd', p.astype(v.dtype), v_sel)

    out = lax.map(block, (to_blocks(q, nb), to_blocks(q_idx, nb), to_blocks(w_idx, nb), jnp.arange(nb)))
    return from_blocks(out).reshape(b, s, h * d)

def diff_attention(q, k, v, lam, subln_g, lam_init):
    b, s, h, _, d = q.shape
    nb = s // Q_BLOCK
    key_chunk = jnp.arange(s) // CHUNK

    def block(args):
        qb, blk = args
        q_chunk = (blk * Q_BLOCK + jnp.arange(Q_BLOCK)) // CHUNK
        adm = key_chunk[None, :] <= q_chunk[:, None]
        logits = jnp.einsum('bqhjd,bshjd->bhjqs', qb, k).astype(jnp.float32) * (d ** -0.5)
        logits = jnp.where(adm[None, None, None], logits, -jnp.inf)
        p = jax.nn.softmax(logits, axis=-1)
        a = p[:, :, 0] - lam * p[:, :, 1]
        return jnp.einsum('bhqs,bshe->bqhe', a.astype(v.dtype), v)

    out = from_blocks(lax.map(block, (to_blocks(q, nb), jnp.arange(nb))))
    out = rms_norm(out, subln_g) * (1.0 - lam_init)
    return out.reshape(b, s, h * v.shape[-1])

def setup_inputs(seed: int = 0) -> dict:
    key = jax.random.key(seed)
    ks = jax.random.split(key, 24)
    f32 = jnp.float32

    def nrm(k, shape, scale):
        return jax.random.normal(k, shape, f32) * scale

    def gain(k, shape):
        return 1.0 + 0.02 * jax.random.normal(k, shape, f32)

    offs = jax.random.randint(ks[2], (BATCH, 1), 0, 4096, dtype=jnp.int32)
    positions = offs + jnp.arange(SEQ, dtype=jnp.int32)[None, :]
    return {
        "x": jax.random.normal(ks[0], (BATCH, SEQ, D_MODEL), f32),
        "c": jax.random.normal(ks[1], (BATCH, D_MODEL), f32),
        "positions": positions,
        "w_mod": nrm(ks[3], (DEPTH, D_MODEL, N_MOD * D_MODEL), D_MODEL ** -0.5),
        "b_mod": nrm(ks[4], (DEPTH, N_MOD * D_MODEL), 0.01),
        "norm_ffn1": gain(ks[5], (DEPTH, D_MODEL)),
        "w_ffn1_in": nrm(ks[6], (DEPTH, D_MODEL, 2 * D_FF), D_MODEL ** -0.5),
        "w_ffn1_out": nrm(ks[7], (DEPTH, D_FF, D_MODEL), D_FF ** -0.5),
        "norm_mix": gain(ks[8], (DEPTH, D_MODEL)),
        "w_in": nrm(ks[9], (DEPTH, D_MODEL, D_IN), D_MODEL ** -0.5),
        "a_sinks": nrm(ks[10], (DEPTH, A_Q_HEADS), 0.5),
        "b_kv_norm": gain(ks[11], (DEPTH, B_KV_RANK)),
        "w_kv_up": nrm(ks[12], (DEPTH, B_KV_RANK, 2 * HEAD_DIM), B_KV_RANK ** -0.5),
        "c_lambda_q1": nrm(ks[13], (DEPTH, HEAD_DIM), 0.1),
        "c_lambda_k1": nrm(ks[14], (DEPTH, HEAD_DIM), 0.1),
        "c_lambda_q2": nrm(ks[15], (DEPTH, HEAD_DIM), 0.1),
        "c_lambda_k2": nrm(ks[16], (DEPTH, HEAD_DIM), 0.1),
        "c_subln": gain(ks[17], (DEPTH, C_VDIM)),
        "w_out": nrm(ks[18], (DEPTH, D_MIX, D_MODEL), D_MIX ** -0.5),
        "norm_ffn2": gain(ks[19], (DEPTH, D_MODEL)),
        "w_ffn2_in": nrm(ks[20], (DEPTH, D_MODEL, 2 * D_FF), D_MODEL ** -0.5),
        "w_ffn2_out": nrm(ks[21], (DEPTH, D_FF, D_MODEL), D_FF ** -0.5),
        "final_norm": gain(ks[22], (D_MODEL,)),
    }

def reference(x, c, positions, w_mod, b_mod, norm_ffn1, w_ffn1_in, w_ffn1_out, norm_mix,
              w_in, a_sinks, b_kv_norm, w_kv_up, c_lambda_q1, c_lambda_k1, c_lambda_q2,
              c_lambda_k2, c_subln, w_out, norm_ffn2, w_ffn2_in, w_ffn2_out, final_norm):
    b, s, _ = x.shape
    cos64, sin64 = rope_tables(positions, HEAD_DIM)
    cos32, sin32 = rope_tables(positions, IDX_DIM)
    splits = np.cumsum(IN_SIZES)[:-1].tolist()
    c_act = jax.nn.silu(c)

    for l in range(DEPTH):
        mods = (c_act @ w_mod[l] + b_mod[l]).reshape(b, N_MOD, D_MODEL)

        h = modulate(x, norm_ffn1[l], mods[:, 0], mods[:, 1])
        x = x + 0.5 * mods[:, 2][:, None, :] * swiglu(h, w_ffn1_in[l], w_ffn1_out[l])

        h = modulate(x, norm_mix[l], mods[:, 3], mods[:, 4])
        (aq, ak, av, bq, bkv, iq, ik, iw, cq, ck, cv) = jnp.split(h @ w_in[l], splits, axis=-1)

        aq = apply_rope(aq.reshape(b, s, A_Q_HEADS, HEAD_DIM), cos64, sin64)
        ak = apply_rope(ak.reshape(b, s, A_KV_HEADS, HEAD_DIM), cos64, sin64)
        av = av.reshape(b, s, A_KV_HEADS, HEAD_DIM)
        y_a = swa_sink_attention(aq, ak, av, a_sinks[l])

        bq = apply_rope(bq.reshape(b, s, B_Q_HEADS, HEAD_DIM), cos64, sin64)
        kv = rms_norm(bkv, b_kv_norm[l]) @ w_kv_up[l]
        bk = apply_rope(kv[..., :HEAD_DIM].reshape(b, s, 1, HEAD_DIM), cos64, sin64)[:, :, 0]
        bv = kv[..., HEAD_DIM:]
        iq = apply_rope(iq.reshape(b, s, IDX_HEADS, IDX_DIM), cos32, sin32)
        ik = apply_rope(ik.reshape(b, s, 1, IDX_DIM), cos32, sin32)[:, :, 0]
        y_b = dsa_sparse_attention(bq, bk, bv, iq, ik, iw)

        cq = apply_rope(cq.reshape(b, s, 2 * C_HEADS, HEAD_DIM), cos64, sin64).reshape(b, s, C_HEADS, 2, HEAD_DIM)
        ck = apply_rope(ck.reshape(b, s, 2 * C_HEADS, HEAD_DIM), cos64, sin64).reshape(b, s, C_HEADS, 2, HEAD_DIM)
        cv = cv.reshape(b, s, C_HEADS, C_VDIM)
        lam_init = 0.8 - 0.6 * math.exp(-0.3 * l)
        lam = (jnp.exp(jnp.sum(c_lambda_q1[l].astype(jnp.float32) * c_lambda_k1[l].astype(jnp.float32)))
               - jnp.exp(jnp.sum(c_lambda_q2[l].astype(jnp.float32) * c_lambda_k2[l].astype(jnp.float32)))
               + lam_init)
        y_c = diff_attention(cq, ck, cv, lam, c_subln[l], lam_init)

        y = jnp.concatenate([y_a, y_b, y_c], axis=-1) @ w_out[l]
        x = x + mods[:, 5][:, None, :] * y

        h = modulate(x, norm_ffn2[l], mods[:, 6], mods[:, 7])
        x = x + 0.5 * mods[:, 8][:, None, :] * swiglu(h, w_ffn2_in[l], w_ffn2_out[l])

    return rms_norm(x, final_norm)


_drawn_inputs = setup_inputs


def setup_inputs(seed=0):
    import zlib

    import numpy as np

    out = dict(_drawn_inputs(seed))
    spreads = {}
    factors = {'b_mod': 2.915,
     'norm_ffn1': 4.269,
     'norm_mix': 4.792,
     'a_sinks': 8.0,
     'b_kv_norm': 8.0,
     'c_lambda_q1': 5.646,
     'c_lambda_k1': 5.63,
     'c_lambda_q2': 4.497,
     'c_lambda_k2': 5.32,
     'c_subln': 7.376,
     'norm_ffn2': 5.64,
     'final_norm': 2.815}
    for name, (base, spread) in spreads.items():
        noise = np.random.default_rng([zlib.crc32(name.encode()), seed]).standard_normal(out[name].shape)
        drawn = base * np.exp(spread * noise) if base else spread * noise
        out[name] = __import__('jax').numpy.asarray(drawn.astype(out[name].dtype))
    for name, factor in factors.items():
        out[name] = (out[name] * factor).astype(out[name].dtype)
    return out
```

```python
import math
from contextlib import ExitStack

import numpy as np
import concourse.bass as bass
from concourse import mybir
from concourse.alu_op_type import AluOpType as ALU

F32 = mybir.dt.float32
F32R = mybir.dt.float32r
BF16 = mybir.dt.bfloat16
I32 = mybir.dt.int32
ACT = mybir.ActivationFunctionType
AX = mybir.AxisListType

P = 128
S, D, DEPTH = 512, 1024, 2
KD = D // P
NT = S // P
D_FF = 2816
N_MOD = 9
HALVES = ((0, 12), (12, 10))
HD, CH, IDX = 64, 64, 32
TOPK = min(256, S // 4)
EPS = 1e-6
BIG = 1e30

A_Q, A_K, A_V, B_Q, B_KV, I_Q, I_K, I_W, C_Q, C_K, C_V, D_IN = (
    0, 256, 384, 512, 768, 896, 1024, 1056, 1060, 1572, 2084, 2596)

FFN_BLOCKS = sum(n for _, n in HALVES) + KD * len(HALVES)
MIX_BLOCKS = 12
FFN1_0 = 0
MIX_0 = FFN_BLOCKS
OUT_0 = MIX_0 + MIX_BLOCKS
FFN2_0 = OUT_0 + KD
BLOCKS = FFN2_0 + FFN_BLOCKS
F_TILES = D_FF // P
CREDIT = 2

C_ID, C_P64, C_P32, C_ONE, C_MASK, C_INV, C_EPS, C_HPI, C_LI, C_1LI = (
    0, 128, 256, 384, 512, 768, 770, 771, 772, 774)
N_CONST = 776
V_B, V_N1, V_NM, V_N2, V_FIN, V_KV, V_SUB, V_C = 0, 72, 80, 88, 96, 104, 105, 106
N_VEC = 114
V_SINK, V_NSINK, V_NLAM, V_SUBG, N_LAY = 114, 118, 122, 123, 124

TWO_PI = 2 * math.pi
PI_A = 6.28125
PI_B = float(np.float32(np.round((TWO_PI - PI_A) * 2 ** 17) / 2 ** 17))
PI_C = float(np.float32(TWO_PI - PI_A - PI_B))
ROUND = 12582912.0
PI_LO = 3.1415925


def constants():
    c = np.zeros((P, N_CONST), np.float32)
    c[:, C_ID:C_ID + P] = np.eye(P)
    for at, half in ((C_P64, HD // 2), (C_P32, IDX // 2)):
        for m in range(P):
            low = m % (2 * half) < half
            c[m + half if low else m - half, at + m] = -1.0 if low else 1.0
    c[:, C_ONE:C_ONE + P] = 1.0
    c[:, C_MASK:C_MASK + 64] = -BIG
    c[64:, C_MASK + 64:C_MASK + 128] = -BIG
    c[:64, C_MASK + 192:C_MASK + 256] = -BIG
    for n, dim in enumerate((HD, IDX)):
        inv = (10000.0 ** (-np.arange(0, dim, 2, dtype=np.float64) / dim)).astype(np.float32)
        c[:, C_INV + n] = np.tile(inv, P // (dim // 2))
    c[:, C_EPS] = EPS
    c[:, C_HPI] = math.pi / 2
    for l in range(DEPTH):
        li = 0.8 - 0.6 * math.exp(-0.3 * l)
        c[:, C_LI + l] = li
        c[:, C_1LI + l] = 1.0 - li
    return c


def trunk(nc, a, out):
    ctx = ExitStack()
    base = nc.sbuf_base
    top = [(base + 63) // 64 * 64]

    def place(name, shape, dt, at=None):
        n = int(np.prod(shape[1:])) * (2 if dt == BF16 else 4)
        where = top[0] if at is None else at
        if at is None:
            top[0] += (n + 31) // 32 * 32
        return nc.alloc_sbuf_tensor_at(name, list(shape), dt, offset=where), where

    def sb(name, shape, dt=F32, at=None):
        return place(name, shape, dt, at)[0]

    x_t = sb("x_t", [P, KD, S])
    h_at = top[0]
    h_hi = sb("h_hi", [P, KD, S], F32R)
    h_lo = sb("h_lo", [P, KD, S], F32R)
    region = top[0]
    nf_max = HALVES[0][1]
    a_hi = sb("a_hi", [P, nf_max, S], F32R)
    a_lo = sb("a_lo", [P, nf_max, S], F32R)
    region_end = top[0]
    w_raw = [sb(f"w_raw{p}", [P, 2048]) for p in range(2)]
    w_at = [top[0] + 4 * 2048 * n for n in range(4)]
    w_hi = [sb(f"w_hi{p}", [P, 2048], F32R) for p in range(2)]
    w_lo = [sb(f"w_lo{p}", [P, 2048], F32R) for p in range(2)]
    rot = sb("rot", [P, 4, S])
    wm = [sb(f"wm{p}", [P, D]) for p in range(2)]
    macc_at = top[0]
    macc = [sb(f"macc{p}", [P, D]) for p in range(2)]
    const = sb("const", [P, N_CONST])
    id_bf = sb("id_bf", [P, P], BF16)
    mask_bf = sb("mask_bf", [P, 256], BF16)
    lay = sb("lay", [P, DEPTH, N_LAY])
    cur = sb("cur", [P, N_LAY])
    c_act = sb("c_act", [P, KD])
    modc = sb("modc", [P, N_MOD, KD])
    coef = sb("coef", [P, 3, KD])
    gate = sb("gate", [P, 3, KD])
    temps = top[0]
    sil = [sb(f"sil{p}", [P, S]) for p in range(2)]
    a_f = [sb(f"a_f{p}", [P, S]) for p in range(2)]
    sq = [sb(f"sq{p}", [P, S]) for p in range(2)]
    sq_sum = sb("sq_sum", [P, S])
    sd = sb("sd", [P, NT])
    rstd = sb("rstd", [P, NT])
    diag = sb("diag", [P, NT, P])
    xn = [sb(f"xn{p}", [P, S]) for p in range(3)]
    temps_end = top[0]

    top[0] = region
    aq = sb("aq", [P, 2, S])
    ak = sb("ak", [P, S])
    akx = sb("akx", [P, S])
    bq = sb("bq", [P, 2, S])
    bk = sb("bk", [P, S])
    iq = sb("iq", [P, S])
    ik = sb("ik", [P, S])
    cq = sb("cq", [P, 4, S])
    ck = sb("ck", [P, 4, S])
    cv = sb("cv", [P, NT, S])
    av = sb("av", [P, NT, P])
    bv = sb("bv", [P, NT, HD])
    iw = sb("iw", [P, NT, 4])
    assert top[0] <= region_end
    top[0] = temps
    q_raw = [sb(f"q_raw{p}", [P, S]) for p in range(2)]
    t_cos = [sb(f"t_cos{p}", [P, S]) for p in range(2)]
    t_sin = [sb(f"t_sin{p}", [P, S]) for p in range(2)]
    kv_raw = sb("kv_raw", [P, S])
    kvn_hi = sb("kvn_hi", [P, S], F32R)
    kvn_lo = sb("kvn_lo", [P, S], F32R)
    rel = [sb(f"rel{p}", [P, S]) for p in range(2)]
    iw_raw = rel[0]
    mix_proj_end = top[0]
    score_at = [0, 0, 256, 640]
    score = sb("score", [P, 1152])
    sel_bf = sb("sel_bf", [P, 1152], BF16)
    top8 = sb("top8", [P, 8])
    stats_n = sb("stats_n", [P, 16])
    stats_s = sb("stats_s", [P, 16])
    stats_e = sb("stats_e", [P, 4])
    stats_r = sb("stats_r", [P, 16])
    stats_f = sb("stats_f", [P, 16])
    c_ss = sb("c_ss", [P, 16])
    c_rs = sb("c_rs", [P, 16])
    mixer_top = top[0]
    top[0] = temps
    e_buf = [sb(f"e_buf{p}", [P, S]) for p in range(4)] + [iq, ik]
    p_t = [sb(f"p_t{p}", [P, S]) for p in range(2)]
    c_sq = sb("c_sq", [P, S])
    y_c = sb("y_c", [P, NT, S])
    assert top[0] <= mix_proj_end
    y_ab = sb("y_ab", [P, NT, S], at=macc_at)
    high = max(temps_end, mixer_top)
    assert high <= nc.sbuf_usable_end, (high, nc.sbuf_usable_end)
    top[0] = region
    x_nat = sb("x_nat", [P, NT, D])
    vec_rows = sb("vec_rows", [P, DEPTH, P])
    pos_i = sb("pos_i", [P, S], I32)
    pos_f = sb("pos_f", [P, S])
    ang = [sb(f"ang{n}", [P, S]) for n in range(2)]
    lam_v = sb("lam_v", [P, 4, DEPTH, HD])
    lam_p = sb("lam_p", [P, 2, DEPTH, HD])
    lam_s = sb("lam_s", [P, 2, DEPTH])
    boot_wm = [sb(f"boot_wm{j}", [P, 2, D], at=h_at + 8 * D * j) for j in range(4)]
    boot_wm += [sb(f"boot_wm{j}", [P, 2, D]) for j in (4, 5)]
    assert top[0] <= region_end
    boot_wm += [sb(f"boot_wm{j}", [P, 2, D], at=at) for j, at in ((6, w_at[1]), (7, w_at[3]))]
    out_nat = sb("out_nat", [P, NT, D], at=region)

    ps = [ctx.enter_context(nc.psum_tensor(f"ps{b}", [P, S], F32)) for b in range(8)]
    SUM, MISC = 4, (5, 7)

    ident = const[:, C_ID:C_ID + P]
    ones = const[:, C_ONE:C_ONE + P]

    def sem(name):
        return ctx.enter_context(nc.semaphore(name))

    const_in = sem("const_in")
    vec_in = sem("vec_in")
    boot_in = [sem(f"boot_in{j}") for j in range(KD)]
    lam_in = sem("lam_in")
    x_in = sem("x_in")
    pos_in = sem("pos_in")
    raw_in = [sem(f"raw_in{p}") for p in range(2)]
    hi_done = sem("hi_done")
    lo_done = sem("lo_done")
    blk_done = sem("blk_done")
    wm_in = [sem(f"wm_in{p}") for p in range(2)]
    wm_used = sem("wm_used")
    acc_zero = sem("acc_zero")
    mod_sum = sem("mod_sum")
    mod_out = sem("mod_out")
    silu_done = sem("silu_done")
    mul_done = sem("mul_done")
    ahi_done = sem("ahi_done")
    alo_done = sem("alo_done")
    x_done = sem("x_done")
    sq_done = sem("sq_done")
    sq_added = sem("sq_added")
    sum_done = sem("sum_done")
    sd_done = sem("sd_done")
    rstd_done = sem("rstd_done")
    diag_done = sem("diag_done")
    spread_done = sem("spread_done")
    xn_done = sem("xn_done")
    hhi_done = sem("hhi_done")
    hlo_done = sem("hlo_done")
    cur_done = sem("cur_done")
    mod_step = sem("mod_step")
    passed = sem("passed")
    tr_done = sem("tr_done")
    boot_step = sem("boot_step")
    start_act = sem("start_act")
    start_dve = sem("start_dve")
    unit_done = sem("unit_done")
    unit_out = sem("unit_out")
    swap_done = sem("swap_done")
    rope_done = sem("rope_done")
    kv_act = sem("kv_act")
    kv_sum = sem("kv_sum")
    kvn_done = sem("kvn_done")
    kvn_hi_done = sem("kvn_hi_done")
    kvn_lo_done = sem("kvn_lo_done")
    akx_done = sem("akx_done")
    iw_turned = sem("iw_turned")
    iw_done = sem("iw_done")
    idx_done = sem("idx_done")
    relu_done = sem("relu_done")
    idx_acc = sem("idx_acc")
    dve_step = sem("dve_step")
    sel_done = sem("sel_done")
    sc_done = sem("sc_done")
    max_done = sem("max_done")
    exp_done = sem("exp_done")
    sink_done = sem("sink_done")
    comb_done = sem("comb_done")
    pt_psum = sem("pt_psum")
    pt_done = sem("pt_done")
    pv_done = sem("pv_done")
    y_out = sem("y_out")
    css_done = sem("css_done")
    csd_done = sem("csd_done")
    cn_done = sem("cn_done")
    yt_done = sem("yt_done")
    yhi_done = sem("yhi_done")
    ylo_done = sem("ylo_done")
    fin_done = sem("fin_done")
    ftr_done = sem("ftr_done")
    fout_a = sem("fout_a")
    fout_b = sem("fout_b")
    stored = sem("stored")

    FFN1 = [("in", 0, [(2, 2), (2, 3), (2, None)]), ("out", 0, [(2, 4), (2, None)]),
            ("in", 1, [(2, 5), (2, 6), (1, None)]), ("out", 1, [(2, 7), (2, None)])]
    FFN2 = [("in", 0, [(2, 8), (4, None)]), ("out", 0, [(4, None)]),
            ("in", 1, [(2, 9), (2, 10), (1, None)]), ("out", 1, [(4, None)])]

    def walk(which):
        s, f = (FFN1_0, FFN2_0)[which], F_TILES * which
        for kind, half, segments in (FFN1, FFN2)[which]:
            step = 0
            for pairs, module in segments:
                yield kind, half, pairs, module, s, step, f
                s += 2 * pairs
                step += 2 * pairs
                if kind == "in":
                    f += 2 * pairs

    MIX = [(B_KV, 256), (I_K, 36), (A_Q, 256), (A_K, 256), (B_Q, 256), None,
           (C_Q, 256), (C_Q + 256, 256), (C_K, 256), (C_K + 256, 256), (C_V, 256), (C_V + 256, 256)]
    KV_UP, INDEX_KEYS = 5, 1
    UNITS = [(0, "kv", kv_raw[:]), (0, "i32", iq[:]), (1, "i32", ik[:]),
             (2, "q64", aq[:, 0]), (2, "q64", aq[:, 1]), (3, "k64", ak[:]), (3, "turn", av[:]),
             (4, "q64", bq[:, 0]), (4, "q64", bq[:, 1]), (5, "k64", bk[:]), (5, "nat", bv),
             (6, "q64", cq[:, 0]), (6, "q64", cq[:, 1]), (7, "q64", cq[:, 2]), (7, "q64", cq[:, 3]),
             (8, "k64", ck[:, 0]), (8, "k64", ck[:, 1]), (9, "k64", ck[:, 2]), (9, "k64", ck[:, 3]),
             *[(10 + h // 2, "turn", cv[:, :, h * P:(h + 1) * P]) for h in range(4)]]
    ROPED = [u for u, (_, kind, _) in enumerate(UNITS) if kind in ("i32", "q64", "k64", "turn")]
    MOVED = [u for u in ROPED if UNITS[u][1] in ("i32", "turn")]
    UNIT_IK, UNIT_AK = 2, 5
    N_U, N_R, N_M = len(UNITS), len(ROPED), len(MOVED)
    IDX_ITEMS = [(b, h) for b in (1, 2, 3) for h in range(4)]
    N_I = len(IDX_ITEMS)
    IDX_AFTER = {u: (2 * j, 2 * j + 1) for j, u in enumerate(range(5, 5 + N_I // 2))}
    TK = TOPK // 8
    TOPK_PLAN = {4: [(1, 0, 3)], 5: [(1, 3, 6)], 6: [(1, 6, 9)], 7: [(1, 9, 12)],
                 8: [(1, 12, 15)], 9: [(1, 15, 16), (2, 0, 1)], 10: [(2, 1, 6)], 11: [(2, 6, 11)]}
    LATE_ROUNDS = {2 + j: (b, r, r + 1) for j, (b, r) in enumerate(
        [(2, r) for r in range(11, TK)] + [(3, r) for r in range(TK)])}
    SEL_ORDER = [1, 2, 3]
    ITEMS = [(b, i) for b in range(NT) for i in range(12)]
    N_IT, N_SU = len(ITEMS), 16 * NT

    def unit_col(i, j=0):
        return i if i < 8 else 8 + 2 * (i - 8) + j

    def keys_of(b, i):
        return (max(b - 1, 0) * P, P * min(b + 1, 2)) if i < 4 else (0, P * (b + 1))

    NORMS = 3
    VEC_DMAS = 8
    CHAIN = N_R - sum(kind == "turn" for _, kind, _ in UNITS) + 1 + 3 + 3 * 2 * TK + 4 * NT + 8 * NT + 2 * NT + 2 * NT + 1

    def used(l, s):
        return (BLOCKS - MIX_BLOCKS) * l + (s if s <= MIX_0 + 1 else s - MIX_BLOCKS)

    def units_through(n):
        return sum(unit[0] <= n for unit in UNITS)

    def fence(eng):
        eng.sem_inc(passed, 1)

    def at_col(t, k):
        return t[:, bass.ds(k, 1)].rearrange("p a s -> p (a s)")

    def block_len(s):
        if MIX_0 <= s < OUT_0:
            cols = MIX[s - MIX_0]
            return KD * cols[1] if cols else P
        if OUT_0 <= s < FFN2_0:
            return KD * P
        r = s - FFN1_0 if s < MIX_0 else s - FFN2_0
        for _, nf in HALVES:
            if r < nf:
                return 2 * KD * P
            if r < nf + KD:
                return nf * P
            r -= nf + KD
        return None

    def split_views(s, p):
        if s == MIX_0 + INDEX_KEYS:
            raw = w_raw[p][:, 0:KD * 36].rearrange("p (k n) -> p k n", n=36)
            hi, lo = (w[p][:, 0:KD * 100].rearrange("p (k n) -> p k n", n=100) for w in (w_hi, w_lo))
            return [(raw[:, :, 0:n], hi[:, :, at:at + n], lo[:, :, at:at + n])
                    for at, n in ((0, IDX), (IDX, IDX), (2 * IDX, IDX + 4))]
        if s == MIX_0 + KV_UP:
            return [(w_raw[p][:, 0:64], w_hi[p][:, 0:64], w_lo[p][:, 0:64]),
                    (w_raw[p][:, 0:128], w_hi[p][:, 64:192], w_lo[p][:, 64:192])]
        n = block_len(s)
        return [(w_raw[p][:, 0:n], w_hi[p][:, 0:n], w_lo[p][:, 0:n])]

    def run_segment(eng, s0, pairs, body):
        sizes = [block_len(s0 + 1 + j) for j in range(2 * pairs)]
        whole = pairs if len(set(sizes)) == 1 and s0 + 2 * pairs not in (MIX_0, BLOCKS) else pairs - 1
        if whole:
            with eng.Fori(0, whole) as i:
                for p in range(2):
                    body(i, p, s0 + p + 1)
        if whole < pairs:
            body(pairs - 1, 0, s0 + 1)
            nxt = s0 + 2 * pairs
            body(pairs - 1, 1, None if nxt == BLOCKS else nxt - 2 * (pairs - 1))

    w_mod = a["w_mod"].rearrange("l (k p) n -> l p k n", p=P)

    def load_chunk(eng, source_l, l, q, k, p):
        eng.wait_ge(wm_used, 72 * l + 8 * q + k + 1)
        fence(eng)
        m = q % N_MOD
        eng.dma_start(wm[p][:], w_mod[source_l, :, bass.ds(k, 1), m * D:(m + 1) * D]
                      .rearrange("p a n -> p (a n)")).then_inc(wm_in[p], 16)

    def vec_src(name):
        return a[name].rearrange("l (r c) -> r l c", c=P)

    def load_vec(eng, row, src):
        eng.dma_start(vec_rows[row:row + src.shape[0]], src).then_inc(vec_in, 16)

    block = ctx.enter_context(nc.Block())

    @block.sync
    def _(sp):
        sp.dma_start(const[:], a["consts"]).then_inc(const_in, 16)
        load_vec(sp, V_B, vec_src("b_mod"))
        load_vec(sp, V_N1, vec_src("norm_ffn1"))
        load_vec(sp, V_FIN, a["final_norm"].rearrange("(r c) -> r c", c=P).unsqueeze(1)
                 .broadcast_to([KD, DEPTH, P]))
        for n, name in enumerate(("c_lambda_q1", "c_lambda_k1", "c_lambda_q2", "c_lambda_k2")):
            sp.dma_start(lam_v[:, n], a[name].unsqueeze(0).broadcast_to([P, DEPTH, HD])
                         ).then_inc(lam_in, 16)
        load_vec(sp, V_C, a["c"].rearrange("b (r c) -> (b r) c", c=P).unsqueeze(1)
                 .broadcast_to([KD, DEPTH, P]))
        x_rows = a["x"].rearrange("b (t p) d -> (b p) t d", p=P)
        w_in_r = a["w_in"].rearrange("l (k p) n -> l p k n", p=P)
        w_out_r = a["w_out"].rearrange("l (k p) n -> l p k n", p=P)

        def load_block(s, p, parts):
            sp.wait_ge(lo_done, s + 1)
            fence(sp)
            for dst, src in parts:
                sp.dma_start(dst, src).then_inc(raw_in[p], 16)

        def slot(p, n):
            return lambda tiles: w_raw[p][:, 0:tiles * n].rearrange("p (k n) -> p k n", n=n)

        def ffn(l, which):
            w_up, w_down = (("w_ffn1_in", "w_ffn1_out"), ("w_ffn2_in", "w_ffn2_out"))[which]
            up = a[w_up].rearrange("l (k p) (g f) -> l p k g f", p=P, g=2)
            down = a[w_down].rearrange("l (f p) n -> l p f n", p=P)
            for kind, half, pairs, module, s0, step, _ in walk(which):
                f0, nf = HALVES[half]
                with sp.Fori(0, pairs) as i:
                    for p in range(2):
                        s = BLOCKS * l + s0 + p + 2 * i
                        if kind == "in":
                            dst = w_raw[p][:].rearrange("p (k g f) -> p k g f", k=KD, g=2)
                            col = bass.ds(i * 2 * P + (f0 + step + p) * P, P)
                            load_block(s, p, [(dst[:, :, g], up[l, :, :, g, col]) for g in range(2)])
                        else:
                            dst = slot(p, P)(nf)
                            col = bass.ds(i * 2 * P + (step + p) * P, P)
                            cut = (slice(0, nf // 2), slice(nf // 2, nf))
                            load_block(s, p, [(dst[:, c], down[l, :, f0 + c.start:f0 + c.stop, col])
                                              for c in cut])

        sp.wait_ge(vec_in, 16 * VEC_DMAS)
        for q in range(2):
            for j in range(4):
                sp.dma_start(boot_wm[4 * q + j][:], w_mod[0, :, 2 * j:2 * j + 2, q * D:(q + 1) * D]
                             ).then_inc(boot_in[4 * q + j], 16)
            if q == 0:
                for t in (0, 2):
                    sp.dma_start(x_nat[:, t:t + 2], x_rows[:, t:t + 2]).then_inc(x_in, 16)
        with sp.Fori(0, DEPTH) as l:
            ffn(l, 0)
            for n, cols in enumerate(MIX):
                p = n % 2
                if cols is None:
                    parts = [(w_raw[p][:, g:g + 64], a["w_kv_up"][l, :, g:g + 64]) for g in (0, 64)]
                else:
                    dst = slot(p, cols[1])(KD)
                    parts = [(dst[:, g:g + 4], w_in_r[l, :, g:g + 4, cols[0]:sum(cols)])
                             for g in (0, 4)]
                load_block(BLOCKS * l + MIX_0 + n, p, parts)
            with sp.Fori(0, KD // 2) as i:
                for p in range(2):
                    dst = slot(p, P)(KD)
                    load_block(BLOCKS * l + OUT_0 + p + 2 * i, p,
                               [(dst[:, g:g + 4], w_out_r[l, :, g:g + 4, bass.ds(i * 2 * P + p * P, P)])
                                for g in (0, 4)])
            ffn(l, 1)

        o_rows = out.rearrange("b (t p) d -> (b p) t d", p=P)
        for t in range(NT):
            sp.wait_ge(fout_a, t + 1)
            sp.wait_ge(fout_b, t + 1)
            sp.dma_start(o_rows[:, t], out_nat[:, t]).then_inc(stored, 16)
        sp.wait_ge(stored, 16 * NT)

    @block.scalar
    def _(act):
        def split_hi(l, s, i=0):
            p = s % 2
            act.wait_ge(raw_in[p], 32 * (BLOCKS // 2) * l + 32 * (s // 2) + 32 * i + 32)
            if MIX_0 + 2 <= s <= OUT_0:
                act.wait_ge(unit_done, N_U * l + units_through(s - 2 - MIX_0))
            else:
                act.wait_ge(blk_done, used(l, s) + 2 * i + 1)
            for raw, hi, _ in split_views(s + 2 * i if isinstance(i, int) else s, p):
                ins = nc.scalar.activation(hi, raw, ACT.Copy)
            ins.then_inc(hi_done, 1)

        def square(x_n, l, m, i, j, p):
            k = 2 * i + j
            act.wait_ge(x_done, x_n + 1)
            act.wait_ge(sq_added, (KD - 1) * NORMS * l + 2 * i + ((KD - 1) * m + j - 1))
            nc.scalar.activation(sq[p][:], at_col(x_t, k), ACT.Square).then_inc(sq_done, 1)

        def root_of_mean(dst, src, n):
            return nc.scalar.activation(dst, src, ACT.Sqrt, scale=1.0 / n,
                                        bias=const[:, C_EPS:C_EPS + 1])

        def norm(l, n):
            v = NORMS * l + n
            act.wait_ge(sum_done, v + 1)
            root_of_mean(sd[:], ps[SUM][:, 0:NT], D).then_inc(sd_done, 1)
            act.wait_ge(mod_out, N_MOD * l + 3 * n + 2)
            for k in range(KD):
                act.wait_ge(xn_done, KD * v + k + 1)
                nc.scalar.activation(h_hi[:, k], xn[k % 3][:], ACT.Identity,
                                     bias=modc[:, 3 * n, k:k + 1]).then_inc(hhi_done, 1)

        def ffn(l, which):
            for kind, half, pairs, module, s0, step, f0 in walk(which):
                def body(i, p, prepared):
                    if module is not None:
                        for c in range(2):
                            load_chunk(act, l if module < N_MOD else 1 - l, l, module,
                                       4 * i + (2 * p + c), c)
                    if prepared is not None:
                        split_hi(l, prepared, i)
                    if kind == "in":
                        f = 2 * F_TILES * l + f0 + p + 2 * i
                        act.wait_ge(blk_done, used(l, s0 + p) + 2 * i + 1 + CREDIT)
                        nc.scalar.activation(sil[p][:], ps[2 * p][:], ACT.Silu).then_inc(silu_done, 1)
                        act.wait_ge(mul_done, f + 1)
                        nc.scalar.activation(at_col(a_hi, 2 * i + (step + p)), a_f[p][:], ACT.Copy
                                             ).then_inc(ahi_done, 1)
                    elif half == 1:
                        square(KD + 40 * l + (24 * which + KD + step + p) + 2 * i, l,
                               1 + 2 * which, i, step + p, p)

                run_segment(act, s0, pairs, body)

        for row, name in ((V_NM, "norm_mix"), (V_N2, "norm_ffn2"), (V_KV, "b_kv_norm"),
                          (V_SUB, "c_subln")):
            load_vec(act, row, vec_src(name))
        act.dma_start(pos_i[:], a["positions"].broadcast_to([P, S])).then_inc(pos_in, 16)
        act.dma_start(lay[:, :, V_SINK:V_SINK + 4],
                      a["a_sinks"].unsqueeze(0).broadcast_to([P, DEPTH, 4])).then_inc(lam_in, 16)
        act.wait_ge(const_in, 16)
        act.wait_ge(tr_done, 2)
        for l in range(DEPTH):
            nc.scalar.activation(lay[:, l, 0:N_VEC], ps[6 + l][:, 0:N_VEC], ACT.Copy
                                 ).then_inc(start_act, 1)
        nc.scalar.activation(c_act[:], ps[6][:, V_C:V_C + KD], ACT.Silu).then_inc(start_act, 1)
        act.wait_ge(start_dve, 1)
        nc.scalar.activation(lam_s[:], lam_s[:], ACT.Exp).then_inc(start_act, 1)
        for n in range(2):
            act.wait_ge(start_dve, 2 + n)
            nc.scalar.activation(rot[:, 2 * n + 1], ang[n][:], ACT.Sin).then_inc(start_act, 1)
            nc.scalar.activation(rot[:, 2 * n], rot[:, 2 * n], ACT.Sin, scale=-1.0,
                                 bias=const[:, C_HPI:C_HPI + 1]).then_inc(start_act, 1)
        for k in range(KD):
            if k >= 2:
                act.wait_ge(sq_added, k - 1)
            act.wait_ge(x_done, k + 1)
            nc.scalar.activation(sq[k % 2][:], x_t[:, k], ACT.Square).then_inc(sq_done, 1)

        def evac(l, u):
            _, kind, dst = UNITS[u]
            act.wait_ge(unit_done, N_U * l + u + 1)
            src = ps[u % 4][:]
            if kind == "kv":
                nc.scalar.activation(dst, src, ACT.Copy).then_inc(unit_out, 1)
                nc.scalar.activation(rel[0][:], src, ACT.Square).then_inc(kv_act, 1)
                act.wait_ge(kv_sum, l + 1)
                root_of_mean(rel[1][:], ps[SUM][:], P).then_inc(kv_act, 1)
            elif u in ROPED:
                r = ROPED.index(u)
                scale = HD ** -0.5 if kind == "q64" else 1.0
                if r >= 2:
                    act.wait_ge(rope_done, N_R * l + r - 1)
                rows = 96 if u == UNIT_IK else P
                ins = nc.scalar.activation(q_raw[r % 2][0:rows, :], src[0:rows], ACT.Copy, scale=scale)
                if u == UNIT_IK:
                    nc.scalar.activation(q_raw[r % 2][96:128, :], src[0:IDX], ACT.Copy)
                    ins = nc.scalar.activation(iw_raw[96:100, :], src[96:100], ACT.Copy)
                if kind in ("q64", "k64"):
                    for g in range(4):
                        ins = nc.scalar.activation(t_sin[r % 2][32 * g:32 * g + 32, :],
                                                   src[32 * (g ^ 1):32 * (g ^ 1) + 32], ACT.Copy,
                                                   scale=scale if g % 2 else -scale)
                ins.then_inc(unit_out, 1)
            else:
                n = dst.shape[2]
                nc.scalar.activation(dst[:], src[:, 0:NT * n].rearrange("p (t n) -> p t n", n=n),
                                     ACT.Copy).then_inc(unit_out, 1)

        def mixer_projections(l):
            def outs(n, last):
                for u in [u for u in range(N_U) if UNITS[u][0] == n][slice(1, 9) if last else slice(1)]:
                    evac(l, u)
                    for x in IDX_AFTER.get(u, ()):
                        nn = P * (IDX_ITEMS[x][0] + 1)
                        act.wait_ge(idx_done, N_I * l + x + 1)
                        if x >= 2:
                            act.wait_ge(idx_acc, N_I * l + x - 1)
                        nc.scalar.activation(rel[x % 2][:, 0:nn], ps[4 + x % 2][:, 0:nn], ACT.Relu
                                             ).then_inc(relu_done, 1)

            for n in range(MIX_BLOCKS):
                split_hi(l, MIX_0 + n + 1)
                outs(n - 1, True)
                outs(n, False)
                if n == 3:
                    act.wait_ge(kvn_done, l + 1)
                    nc.scalar.activation(kvn_hi[:], kv_raw[:], ACT.Copy).then_inc(kvn_hi_done, 1)
                if n == 4:
                    act.wait_ge(rope_done, N_R * l + ROPED.index(UNIT_AK) + 1)
                    nc.scalar.activation(akx[0:64, :], ak[64:128, :], ACT.Copy).then_inc(akx_done, 1)
                    nc.scalar.activation(akx[64:128, :], ak[0:64, :], ACT.Copy).then_inc(akx_done, 1)
            outs(MIX_BLOCKS - 1, True)

        def exps(l, it):
            b, i = ITEMS[it]
            nn = keys_of(b, i)[1]
            for j in range(2 if i >= 8 else 1):
                c = unit_col(i, j)
                su = 16 * b + c
                act.wait_ge(max_done, N_SU * l + su + 1)
                nc.scalar.activation(e_buf[su % 6][:, 0:nn], ps[su % 4][:, 0:nn], ACT.Exp,
                                     bias=stats_n[:, c:c + 1], accum_out=stats_s[:, c:c + 1]
                                     ).then_inc(exp_done, 1)
            if i == 3:
                for h in range(4):
                    nc.scalar.activation(stats_e[:, h:h + 1], cur[:, V_SINK + h:V_SINK + h + 1],
                                         ACT.Exp, bias=stats_n[:, h:h + 1]).then_inc(sink_done, 1)

        def evac_p(l, it):
            b, i = ITEMS[it]
            nn = keys_of(b, i)[1]
            act.wait_ge(pt_psum, N_IT * l + it + 1)
            if it >= 2:
                act.wait_ge(pv_done, N_IT * l + it - 1)
            nc.scalar.activation(p_t[it % 2][:, 0:nn], ps[6 + it % 2][:, 0:nn], ACT.Copy
                                 ).then_inc(pt_done, 1)

        def attention(l):
            act.wait_ge(rope_done, N_R * (l + 1))
            act.wait_ge(kvn_lo_done, l + 1)
            for it, (b, i) in enumerate(ITEMS):
                if b and i in (0, 8):
                    act.wait_ge(y_out, 2 * NT * l + 2 * (b - 1) + (1 if i == 0 else 2))
                exps(l, it)
                if it >= 2:
                    evac_p(l, it - 2)
            for it in (N_IT - 2, N_IT - 1):
                evac_p(l, it)
            act.wait_ge(css_done, l + 1)
            nc.scalar.activation(c_rs[:], c_ss[:], ACT.Sqrt, scale=1.0 / P,
                                 bias=const[:, C_EPS:C_EPS + 1]).then_inc(csd_done, 1)
            for n in range(2 * NT):
                b, c = n // 2, n % 2
                act.wait_ge(yt_done, 2 * NT * l + n + 1)
                nc.scalar.activation(h_hi[:, 4 * c:4 * c + 4, b * P:(b + 1) * P],
                                     ps[n][:].rearrange("p (t s) -> p t s", s=P), ACT.Copy,
                                     scale=cur[:, V_SUBG:V_SUBG + 1] if c else 1.0
                                     ).then_inc(yhi_done, 1)

        with act.Fori(0, DEPTH) as l:
            split_hi(l, 0)
            norm(l, 0)
            ffn(l, 0)
            norm(l, 1)
            mixer_projections(l)
            attention(l)

            def out_step(i, p, prepared):
                split_hi(l, prepared, i)
                square(KD + 40 * l + 2 * KD + p + 2 * i, l, 2, i, p, p)

            run_segment(act, OUT_0, KD // 2, out_step)
            norm(l, 2)
            ffn(l, 1)

        act.wait_ge(sum_done, NORMS * DEPTH + 1)
        root_of_mean(sd[:], ps[SUM][:, 0:NT], D).then_inc(sd_done, 1)
        act.wait_ge(rstd_done, NORMS * DEPTH + 1)
        for n in range(0, 2 * NT, 2):
            act.wait_ge(ftr_done, n + 1)
            nc.scalar.activation(out_nat[:, n // 2, 0:S], ps[n % 4][:], ACT.Copy,
                                 scale=rstd[:, n // 2:n // 2 + 1]).then_inc(fout_a, 1)

    @block.vector
    def _(dve):
        def split_lo(l, s, i=0):
            dve.wait_ge(hi_done, BLOCKS * l + s + 2 * i + 1)
            for raw, hi, lo in split_views(s + 2 * i if isinstance(i, int) else s, s % 2):
                ins = nc.vector.tensor_tensor(lo, raw, hi.bitcast(F32), ALU.subtract)
            ins.then_inc(lo_done, 1)

        def clear(l, q):
            nc.vector.memset(macc[q % N_MOD % 2][:], 0.0).then_inc(acc_zero, 1)
            dve.wait_ge(acc_zero, N_MOD * l + q - 1)
            fence(dve)

        def chunk(l, q, k, p):
            acc = macc[q % N_MOD % 2][:]
            dve.wait_ge(wm_in[p], 16 * 36 * l + 16 * 4 * (q - 2) + 8 * (k - p) + 16)
            dve.wait_ge(wm_used, 72 * l + 8 * q + k + CREDIT)
            nc.vector.scalar_tensor_tensor(acc, wm[p][:], c_act[:, bass.ds(k, 1)], acc,
                                           ALU.mult, ALU.add).then_inc(wm_used, 1)

        def module_out(l, q, src):
            m = q % N_MOD
            n, par = m // 3, m % 2
            dve.wait_ge(mod_sum, N_MOD * l + q + 1)
            fence(dve)
            ins = nc.vector.tensor_tensor(modc[:, m], ps[MISC[par]][:, 0:8],
                                          src[:, V_B + 8 * m:V_B + 8 * m + 8], ALU.add)
            if m % 3:
                ins.then_inc(mod_step, 1)
                dve.wait_ge(mod_step, 6 * l + q - q // 3)
                if m % 3 == 1:
                    g = (V_N1, V_NM, V_N2)[n]
                    ins = nc.vector.scalar_tensor_tensor(coef[:, n], modc[:, m], 1.0,
                                                         src[:, g:g + KD], ALU.add, ALU.mult)
                else:
                    ins = nc.vector.tensor_scalar(gate[:, n], modc[:, m], 1.0 if n == 1 else 0.5,
                                                  None, ALU.mult)
            ins.then_inc(mod_out, 1)
            dve.wait_ge(mod_out, N_MOD * l + q + 1)
            fence(dve)

        def norm(l, n):
            v = NORMS * l + n
            dve.wait_ge(sd_done, v + 1)
            nc.vector.reciprocal(rstd[:], sd[:]).then_inc(rstd_done, 1)
            dve.wait_ge(rstd_done, v + 1)
            for t in range(NT):
                fence(dve)
                nc.vector.tensor_scalar(diag[:, t], ident, rstd[:, t:t + 1], None, ALU.mult
                                        ).then_inc(diag_done, 1)

            def rest(k):
                dve.wait_ge(hhi_done, KD * v + k + 1)
                nc.vector.scalar_tensor_tensor(h_lo[:, k], xn[k % 3][:], modc[:, 3 * n, k:k + 1],
                                               h_hi[:, k].bitcast(F32), ALU.add, ALU.subtract
                                               ).then_inc(hlo_done, 1)

            dve.wait_ge(spread_done, v + 1)
            for k in range(KD):
                if k >= 3:
                    dve.wait_ge(hlo_done, KD * v + k - 2)
                nc.vector.scalar_tensor_tensor(xn[k % 3][:], x_t[:, k], coef[:, n, k:k + 1],
                                               ps[SUM][:], ALU.mult, ALU.mult).then_inc(xn_done, 1)
                if k:
                    rest(k - 1)
            rest(KD - 1)

        def x_update(s, p, k, g):
            dve.wait_ge(blk_done, s + 1 + CREDIT)
            xk = at_col(x_t, k)
            nc.vector.scalar_tensor_tensor(xk, ps[2 * p][:], gate[:, g, bass.ds(k, 1)], xk,
                                           ALU.mult, ALU.add).then_inc(x_done, 1)

        def ffn(l, which):
            for kind, half, pairs, module, s0, step, f0 in walk(which):
                if module is not None:
                    clear(l, module)

                def body(i, p, prepared):
                    if prepared is not None:
                        split_lo(l, prepared, i)
                    if module is not None:
                        for c in range(2):
                            chunk(l, module, 4 * i + (2 * p + c), c)
                    if kind == "in":
                        f = 2 * F_TILES * l + f0 + p + 2 * i
                        dve.wait_ge(silu_done, f + 1)
                        nc.vector.tensor_tensor(a_f[p][:], ps[2 * p + 1][:], sil[p][:], ALU.mult
                                                ).then_inc(mul_done, 1)
                        dve.wait_ge(ahi_done, f + 1)
                        k = 2 * i + (step + p)
                        nc.vector.tensor_tensor(at_col(a_lo, k), a_f[p][:],
                                                at_col(a_hi, k).bitcast(F32), ALU.subtract
                                                ).then_inc(alo_done, 1)
                    else:
                        x_update(used(l, s0 + p) + 2 * i, p, 2 * i + (step + p), 2 * which)

                run_segment(dve, s0, pairs, body)
                if module is not None:
                    src = cur if module < N_MOD else lay[:, bass.ds(1 - l, 1)].rearrange(
                        "p a n -> p (a n)")
                    module_out(l, module, src)

        boots = [0]

        def boot(ins):
            boots[0] += 1
            ins.then_inc(boot_step, 1)
            dve.wait_ge(boot_step, boots[0])

        dve.sem_inc(lo_done, CREDIT)
        dve.sem_inc(wm_used, CREDIT)
        dve.wait_ge(const_in, 16)
        nc.vector.tensor_copy(id_bf[:], ident)
        nc.vector.tensor_copy(mask_bf[:], const[:, C_MASK:C_MASK + 256])
        dve.wait_ge(lam_in, 16 * 5)
        boot(nc.vector.tensor_tensor(lam_p[:], lam_v[:, 0:4:2], lam_v[:, 1:4:2], ALU.mult))
        nc.vector.tensor_reduce(lam_s[:], lam_p[:], AX.X, ALU.add).then_inc(start_dve, 1)
        dve.wait_ge(pos_in, 16)
        boot(nc.vector.tensor_copy(pos_f[:], pos_i[:]))
        for n in range(2):
            turn = rot[:, 2 * n]
            boot(nc.vector.tensor_scalar(ang[n][:], pos_f[:], const[:, C_INV + n:C_INV + n + 1], None,
                                         ALU.mult))
            boot(nc.vector.tensor_scalar(turn, ang[n][:], 1.0 / TWO_PI, ROUND, ALU.mult, ALU.add))
            boot(nc.vector.tensor_scalar(turn, turn, ROUND, None, ALU.subtract))
            for part in (PI_A, PI_B, PI_C):
                boot(nc.vector.scalar_tensor_tensor(ang[n][:], turn, -part, ang[n][:],
                                                    ALU.mult, ALU.add))
            boot(nc.vector.tensor_scalar(ang[n][:], ang[n][:], PI_LO, -PI_LO, ALU.min, ALU.max))
            nc.vector.scalar_tensor_tensor(turn, ang[n][:], -1.0, ang[n][:], ALU.mult, ALU.max
                                           ).then_inc(start_dve, 1)
        dve.wait_ge(start_act, 4)
        nc.vector.tensor_scalar(lay[:, :, V_NSINK:V_NSINK + 4], lay[:, :, V_SINK:V_SINK + 4], -1.0,
                                None, ALU.mult)
        boot(nc.vector.tensor_tensor(lam_s[:, 0], lam_s[:, 1], lam_s[:, 0], ALU.subtract))
        nc.vector.tensor_tensor(lay[:, :, V_NLAM], lam_s[:, 0], const[:, C_LI:C_LI + DEPTH],
                                ALU.subtract)
        boot(nc.vector.tensor_tensor(lay[:, :, V_SUBG], lay[:, :, V_SUB],
                                     const[:, C_1LI:C_1LI + DEPTH], ALU.mult))
        for q in range(2):
            for k in range(KD):
                src = boot_wm[4 * q + k // 2][:, k % 2]
                dve.wait_ge(boot_in[4 * q + k // 2], 16)
                if k == 0:
                    ins = nc.vector.tensor_scalar(macc[q][:], src, c_act[:, k:k + 1], None, ALU.mult)
                else:
                    dve.wait_ge(wm_used, 8 * q + k + CREDIT)
                    ins = nc.vector.scalar_tensor_tensor(macc[q][:], src, c_act[:, k:k + 1],
                                                         macc[q][:], ALU.mult, ALU.add)
                ins.then_inc(wm_used, 1)
            if q == 0:
                for k in range(KD):
                    dve.wait_ge(tr_done, 3 + k)
                    nc.vector.tensor_copy(x_t[:, k], ps[k % 4][:]).then_inc(x_done, 1)
        for q in range(2):
            module_out(0, q, lay[:, 0])

        chain = [0]

        def link(l, ins):
            chain[0] += 1
            ins.then_inc(dve_step, 1)
            dve.wait_ge(dve_step, CHAIN * l + chain[0])

        def rope(l, u):
            kind, dst = UNITS[u][1:]
            r = ROPED.index(u)
            if u in MOVED:
                dve.wait_ge(swap_done, N_M * l + MOVED.index(u) + 1)
            if kind == "turn":
                nc.vector.tensor_copy(dst, ps[6 + r % 2][:].rearrange("p (t n) -> p t n", n=P)
                                      ).then_inc(rope_done, 1)
                return
            t = 2 if kind == "i32" else 0
            dve.wait_ge(unit_out, N_U * l + u + 1)
            nc.vector.tensor_tensor(t_cos[r % 2][:], q_raw[r % 2][:], rot[:, t], ALU.mult)
            swapped = ps[6 + r % 2][:] if kind == "i32" else t_sin[r % 2][:]
            link(l, nc.vector.tensor_tensor(t_sin[r % 2][:], swapped, rot[:, t + 1], ALU.mult))
            nc.vector.tensor_tensor(dst, t_cos[r % 2][:], t_sin[r % 2][:], ALU.add
                                    ).then_inc(rope_done, 1)

        def index_score(l, x):
            b, h = IDX_ITEMS[x]
            nn = P * (b + 1)
            dst = score[:, score_at[b]:score_at[b] + nn]
            dve.wait_ge(relu_done, N_I * l + x + 1)
            w = iw[:, b, h:h + 1]
            if h:
                ins = nc.vector.scalar_tensor_tensor(dst, rel[x % 2][:, 0:nn], w, dst,
                                                     ALU.mult, ALU.add)
            else:
                ins = nc.vector.tensor_scalar(dst, rel[x % 2][:, 0:nn], w, 0.0, ALU.mult, ALU.add)
            ins.then_inc(idx_acc, 1)
            dve.wait_ge(idx_acc, N_I * l + x + 1)
            if h == 3:
                link(l, nc.vector.memset(score[0:64, score_at[b] + nn - 64:score_at[b] + nn], -BIG))

        def topk(l, b, r0, r1):
            nn = P * (b + 1)
            work = score[:, score_at[b]:score_at[b] + nn]
            for r in range(r0, r1):
                fence(dve)
                link(l, nc.vector.max(top8[:], work))
                fence(dve)
                link(l, nc.vector.match_replace(work, top8[:], work, -3e38))
            if r1 == TK:
                nc.vector.tensor_scalar(sel_bf[:, score_at[b]:score_at[b] + nn], work, -2e38, -BIG,
                                        ALU.is_gt, ALU.mult).then_inc(sel_done, 1)

        def mixer_projections(l):
            def outs(n, last):
                for u in [u for u in range(N_U) if UNITS[u][0] == n][slice(1, 9) if last else slice(1)]:
                    if u in ROPED:
                        rope(l, u)
                    for x in IDX_AFTER.get(u, ()):
                        index_score(l, x)

            for n in range(MIX_BLOCKS):
                split_lo(l, MIX_0 + n + 1)
                outs(n - 1, True)
                if n == 2:
                    dve.wait_ge(iw_turned, l + 1)
                    nc.vector.tensor_copy(iw[:], ps[5][:, 0:NT * 4].rearrange("p (t n) -> p t n", n=4)
                                          ).then_inc(iw_done, 1)
                    dve.wait_ge(kv_act, 2 * l + 2)
                    link(l, nc.vector.reciprocal(rel[1][:], rel[1][:]))
                    nc.vector.scalar_tensor_tensor(kv_raw[:], kv_raw[:], cur[:, V_KV:V_KV + 1],
                                                   rel[1][:], ALU.mult, ALU.mult).then_inc(kvn_done, 1)
                    dve.wait_ge(iw_done, l + 1)
                    fence(dve)
                if n == 4:
                    dve.wait_ge(kvn_hi_done, l + 1)
                    nc.vector.tensor_tensor(kvn_lo[:], kv_raw[:], kvn_hi[:].bitcast(F32),
                                            ALU.subtract).then_inc(kvn_lo_done, 1)
                for part in TOPK_PLAN.get(n, []):
                    topk(l, *part)
                outs(n, False)
            outs(MIX_BLOCKS - 1, True)

        def maxima(l, it):
            b, i = ITEMS[it]
            nn = keys_of(b, i)[1]
            for j in range(2 if i >= 8 else 1):
                c = unit_col(i, j)
                su = 16 * b + c
                dve.wait_ge(sc_done, N_SU * l + su + 1)
                ins = nc.vector.tensor_reduce(stats_n[:, c:c + 1], ps[su % 4][:, 0:nn], AX.X, ALU.max,
                                              negate=True)
                if i < 4:
                    link(l, ins)
                    ins = nc.vector.tensor_tensor(stats_n[:, c:c + 1], stats_n[:, c:c + 1],
                                                  cur[:, V_NSINK + i:V_NSINK + i + 1], ALU.min)
                ins.then_inc(max_done, 1)

        def combine(l, it):
            b, i = ITEMS[it]
            nn = keys_of(b, i)[1]
            c = unit_col(i)
            su = 16 * b + c
            dve.wait_ge(exp_done, N_SU * l + su + 2)
            link(l, nc.vector.reciprocal(stats_r[:, c:c + 1], stats_s[:, c + 1:c + 2]))
            link(l, nc.vector.scalar_tensor_tensor(stats_r[:, c + 1:c + 2], stats_r[:, c:c + 1],
                                                   cur[:, V_NLAM:V_NLAM + 1], stats_s[:, c:c + 1],
                                                   ALU.mult, ALU.mult))
            nc.vector.scalar_tensor_tensor(e_buf[su % 6][:, 0:nn], e_buf[(su + 1) % 6][:, 0:nn],
                                           stats_r[:, c + 1:c + 2], e_buf[su % 6][:, 0:nn],
                                           ALU.mult, ALU.add).then_inc(comb_done, 1)

        def y_ab_out(l, b):
            dve.wait_ge(pv_done, N_IT * l + 12 * b + 8)
            dve.wait_ge(sink_done, 4 * NT * l + 4 * b + 4)
            nc.vector.tensor_tensor(stats_f[:, 0:4], stats_s[:, 0:4], stats_e[:], ALU.add)
            link(l, nc.vector.tensor_copy(stats_f[:, 4:8], stats_s[:, 4:8]))
            link(l, nc.vector.reciprocal(stats_f[:, 0:8], stats_f[:, 0:8]))
            nc.vector.tensor_tensor(y_ab[:, b].rearrange("p (h e) -> p h e", h=8),
                                    ps[4][:].rearrange("p (h e) -> p h e", h=8),
                                    stats_f[:, 0:8].unsqueeze(2).broadcast_to([P, 8, HD]), ALU.mult
                                    ).then_inc(y_out, 1)

        def y_c_out(l, b):
            dve.wait_ge(pv_done, N_IT * l + 12 * b + 12)
            link(l, nc.vector.reciprocal(stats_f[:, 8:12], stats_s[:, 8:16:2]))
            nc.vector.tensor_tensor(y_c[:, b].rearrange("p (h e) -> p h e", h=4),
                                    ps[5][:].rearrange("p (h e) -> p h e", h=4),
                                    stats_f[:, 8:12].unsqueeze(2).broadcast_to([P, 4, P]), ALU.mult
                                    ).then_inc(y_out, 1)
            dve.wait_ge(y_out, 2 * NT * l + 2 * b + 2)
            link(l, nc.vector.tensor_tensor(c_sq[:], y_c[:, b], y_c[:, b], ALU.mult))
            ins = nc.vector.tensor_reduce(c_ss[:, 4 * b:4 * b + 4],
                                          c_sq[:].rearrange("p (h e) -> p h e", h=4), AX.X, ALU.add)
            if b == NT - 1:
                ins.then_inc(css_done, 1)

        def attention(l):
            for it, (b, i) in enumerate(ITEMS):
                maxima(l, it)
                if it in LATE_ROUNDS:
                    topk(l, *LATE_ROUNDS[it])
                if it and ITEMS[it - 1][1] >= 8:
                    combine(l, it - 1)
                if i == 11:
                    y_ab_out(l, b)
                if i == 3 and b:
                    y_c_out(l, b - 1)
            combine(l, N_IT - 1)
            y_c_out(l, NT - 1)
            dve.wait_ge(csd_done, l + 1)
            link(l, nc.vector.reciprocal(c_rs[:], c_rs[:]))
            for b in range(NT):
                yb = y_c[:, b].rearrange("p (h e) -> p h e", h=4)
                nc.vector.tensor_tensor(yb, yb, c_rs[:, 4 * b:4 * b + 4].unsqueeze(2)
                                        .broadcast_to([P, 4, P]), ALU.mult).then_inc(cn_done, 1)
            for n in range(2 * NT):
                b, c = n // 2, n % 2
                dve.wait_ge(yhi_done, 2 * NT * l + n + 1)
                hi, lo = (h[:, 4 * c:4 * c + 4, b * P:(b + 1) * P] for h in (h_hi, h_lo))
                src = ps[n][:].rearrange("p (t s) -> p t s", s=P)
                if c:
                    for t in range(4):
                        ins = nc.vector.scalar_tensor_tensor(lo[:, t], src[:, t],
                                                             cur[:, V_SUBG:V_SUBG + 1],
                                                             hi[:, t].bitcast(F32),
                                                             ALU.mult, ALU.subtract)
                else:
                    ins = nc.vector.tensor_tensor(lo, src, hi.bitcast(F32), ALU.subtract)
                ins.then_inc(ylo_done, 1)

        dve.wait_ge(start_act, 8)
        with dve.Fori(0, DEPTH) as l:
            nc.vector.tensor_copy(cur[:], at_col(lay, l)).then_inc(cur_done, 1)
            dve.wait_ge(cur_done, l + 1)
            split_lo(l, 0)
            norm(l, 0)
            ffn(l, 0)
            norm(l, 1)
            mixer_projections(l)
            attention(l)
            assert chain[0] == CHAIN, chain

            def out_step(i, p, prepared):
                split_lo(l, prepared, i)
                x_update(used(l, OUT_0 + p) + 2 * i, p, 2 * i + p, 1)

            run_segment(dve, OUT_0, KD // 2, out_step)
            norm(l, 2)
            ffn(l, 1)

        dve.wait_ge(sq_done, KD * (NORMS * DEPTH + 1))
        for k in range(KD):
            nc.vector.tensor_scalar(x_t[:, k], x_t[:, k], lay[:, 0, V_FIN + k:V_FIN + k + 1], None,
                                    ALU.mult).then_inc(fin_done, 1)
        dve.wait_ge(sd_done, NORMS * DEPTH + 1)
        nc.vector.reciprocal(rstd[:], sd[:]).then_inc(rstd_done, 1)
        dve.wait_ge(rstd_done, NORMS * DEPTH + 1)
        for n in range(1, 2 * NT, 2):
            dve.wait_ge(ftr_done, n + 1)
            nc.vector.tensor_scalar(out_nat[:, n // 2, S:2 * S], ps[n % 4][:],
                                    rstd[:, n // 2:n // 2 + 1], None, ALU.mult).then_inc(fout_b, 1)

    @block.gpsimd
    def _(pool):
        with pool.Fori(0, NORMS * DEPTH + 1) as v:
            for k in range(KD - 1):
                pool.wait_ge(sq_done, KD * v + k + 1)
                fence(pool)
                if k == 0:
                    ins = nc.gpsimd.tensor_copy(sq_sum[:], sq[0][:])
                else:
                    pool.wait_ge(sq_added, (KD - 1) * v + k)
                    fence(pool)
                    ins = nc.gpsimd.tensor_tensor(sq_sum[:], sq_sum[:], sq[k % 2][:], ALU.add)
                ins.then_inc(sq_added, 1)

    @block.tensor
    def _(pe):
        def product(dst, w, h, first, last):
            nc.tensor.matmul(dst, w[0], h[1], start=first, stop=False, skip_group_check=True)
            nc.tensor.matmul(dst, w[1], h[0], start=False, stop=False, skip_group_check=True)
            return nc.tensor.matmul(dst, w[0], h[0], start=False, stop=last, skip_group_check=True)

        def sum_squares(v):
            pe.wait_ge(sq_added, (KD - 1) * (v + 1))
            pe.wait_ge(sq_done, KD * (v + 1))
            for t in range(NT):
                for src in (sq_sum, sq[(KD - 1) % 2]):
                    ins = nc.tensor.matmul(ps[SUM][:, t:t + 1], src[:, t * P:(t + 1) * P],
                                           ones[:, 0:1], start=src is sq_sum,
                                           stop=src is not sq_sum)
            ins.then_inc(sum_done, 1)

        def spread(v):
            for t in range(NT):
                pe.wait_ge(diag_done, NT * v + t + 1)
                ins = nc.tensor.matmul(ps[SUM][:, t * P:(t + 1) * P], ones, diag[:, t],
                                       start=True, stop=True)
            ins.then_inc(spread_done, 1)

        def module_sum(l, q):
            pe.wait_ge(wm_used, 72 * l + 8 * q + 8 + CREDIT)
            par = q % N_MOD % 2
            for t in range(KD):
                ins = nc.tensor.matmul(ps[MISC[par]][:, t:t + 1],
                                       macc[par][:, t * P:(t + 1) * P], ones[:, 0:1],
                                       start=True, stop=True)
            ins.then_inc(mod_sum, 1)

        def ffn(l, which):
            for kind, half, pairs, module, s0, step, f0 in walk(which):
                nf = HALVES[half][1]
                v = NORMS * l + 2 * which

                def body(i, p):
                    pe.wait_ge(lo_done, BLOCKS * l + s0 + p + 2 * i + 1 + CREDIT)
                    if kind == "in":
                        w = [wb[p][:].rearrange("p (k g f) -> p k g f", k=KD, g=2)
                             for wb in (w_hi, w_lo)]
                        for k in range(KD):
                            if half == 0 and step == 0 and p == 0:
                                pe.wait_ge(hlo_done, KD * v + k + 1)
                            for g in range(2):
                                ins = product(ps[2 * p + g][:], [t[:, k, g] for t in w],
                                              (h_hi[:, k], h_lo[:, k]), k == 0, k == KD - 1)
                    else:
                        w = [wb[p][:, 0:nf * P].rearrange("p (f n) -> p f n", n=P)
                             for wb in (w_hi, w_lo)]
                        for f in range(nf):
                            if f in (0, nf - 1):
                                pe.wait_ge(alo_done, 2 * F_TILES * l + f0 - (1 if f == 0 else 0))
                            ins = product(ps[2 * p][:], [t[:, f] for t in w],
                                          (a_hi[:, f], a_lo[:, f]), f == 0, f == nf - 1)
                    ins.then_inc(blk_done, 1)

                with pe.Fori(0, pairs) as i:
                    for p in range(2):
                        body(i, p)
                if module is not None:
                    module_sum(l, module)
            sum_squares(NORMS * l + 1 + 2 * which)

        pe.sem_inc(blk_done, CREDIT)
        pe.wait_ge(const_in, 16)
        pe.wait_ge(vec_in, 16 * VEC_DMAS)
        for l in range(DEPTH):
            nc.tensor.transpose(ps[6 + l][:, 0:N_VEC], vec_rows[0:N_VEC, l],
                                ident[0:N_VEC, 0:N_VEC]).then_inc(tr_done, 1)
        pe.wait_ge(x_in, 16 * 2)
        for k in range(KD):
            if k >= 4:
                pe.wait_ge(x_done, k - 3)
            for t in range(NT):
                ins = nc.tensor.transpose(ps[k % 4][:, t * P:(t + 1) * P],
                                          x_nat[:, t, k * P:(k + 1) * P], ident)
            ins.then_inc(tr_done, 1)
        module_sum(0, 0)
        sum_squares(0)
        module_sum(0, 1)

        def swap(l, u):
            r = ROPED.index(u)
            pe.wait_ge(unit_out, N_U * l + u + 1)
            if r >= 2:
                pe.wait_ge(rope_done, N_R * l + r - 1)
            if UNITS[u][1] == "i32":
                ins = nc.tensor.matmul(ps[6 + r % 2][:], const[:, C_P32:C_P32 + P], q_raw[r % 2][:],
                                       start=True, stop=True)
            else:
                for t in range(NT):
                    ins = nc.tensor.transpose(ps[6 + r % 2][:, t * P:(t + 1) * P],
                                              q_raw[r % 2][:, t * P:(t + 1) * P], ident)
            ins.then_inc(swap_done, 1)
            if u == UNIT_IK:
                for t in range(NT):
                    ins = nc.tensor.transpose(ps[5][:, 4 * t:4 * t + 4],
                                              iw_raw[96:100, t * P:(t + 1) * P],
                                              ident[96:100, 96:100])
                ins.then_inc(iw_turned, 1)

        def project(l, u):
            n, kind, dst = UNITS[u]
            p = n % 2
            bank = ps[u % 4]
            if u >= 4:
                pe.wait_ge(unit_out, N_U * l + u - 3)
            first = u == 0 or UNITS[u - 1][0] != n
            if n == KV_UP:
                pe.wait_ge(kvn_lo_done, l + 1)
                if kind == "k64":
                    ins = product(bank[:], (w_hi[p][:, 0:P], w_lo[p][:, 0:P]),
                                  (kvn_hi[:], kvn_lo[:]), True, True)
                else:
                    for t in range(NT):
                        tok = slice(t * P, (t + 1) * P)
                        ins = product(bank[:, t * HD:(t + 1) * HD],
                                      (kvn_hi[:, tok], kvn_lo[:, tok]),
                                      (w_hi[p][:, P:P + HD], w_lo[p][:, P:P + HD]), True, True)
            else:
                cols = 100 if n == INDEX_KEYS else 256
                w = [wb[p][:, 0:KD * cols].rearrange("p (k n) -> p k n", n=cols)
                     for wb in (w_hi, w_lo)]
                c0, width = 0 if first else P, min(cols, P)
                for k in range(KD):
                    if u == 0:
                        pe.wait_ge(hlo_done, KD * (NORMS * l + 1) + k + 1)
                    ins = product(bank[0:width, :], [x[:, k, c0:c0 + width] for x in w],
                                  (h_hi[:, k], h_lo[:, k]), k == 0, k == KD - 1)
            ins.then_inc(unit_done, 1)
            return ins

        def mixer_projections(l):
            raw = None
            pe.wait_ge(mod_out, N_MOD * l + 8)
            for n in range(MIX_BLOCKS):
                pe.wait_ge(lo_done, BLOCKS * l + MIX_0 + n + 1 + CREDIT)
                for u in range(N_U):
                    if UNITS[u][0] != n:
                        continue
                    project(l, u)
                    if u == 1:
                        pe.wait_ge(kv_act, 2 * l + 1)
                        nc.tensor.matmul(ps[SUM][:], ones, rel[0][:], start=True, stop=True
                                         ).then_inc(kv_sum, 1)
                    if raw is not None:
                        swap(l, raw)
                    raw = u if u in MOVED else None
                    for x in IDX_AFTER.get(u, ()):
                        b, h = IDX_ITEMS[x]
                        if x == 0:
                            pe.wait_ge(rope_done, N_R * l + 2)
                            pe.wait_ge(kv_act, 2 * l + 2)
                            pe.wait_ge(iw_done, l + 1)
                        if x >= 2:
                            pe.wait_ge(relu_done, N_I * l + x - 1)
                        rows = slice(IDX * h, IDX * h + IDX)
                        nc.tensor.matmul(ps[4 + x % 2][:, 0:P * (b + 1)], iq[rows, b * P:(b + 1) * P],
                                         ik[rows, 0:P * (b + 1)], start=True, stop=True
                                         ).then_inc(idx_done, 1)
            swap(l, raw)

        def logits(l, it):
            b, i = ITEMS[it]
            k0, nn = keys_of(b, i)
            tok = slice(b * P, (b + 1) * P)
            for j in range(2 if i >= 8 else 1):
                su = 16 * b + unit_col(i, j)
                if su >= 4:
                    pe.wait_ge(exp_done, N_SU * l + su - 3)
                h = i % 4
                half = j if i >= 8 else h % 2
                rows = slice(64 * half, 64 * half + 64)
                if i < 4:
                    q, k = aq[rows, h // 2, tok], (ak if h // 2 == half else akx)[rows, k0:k0 + nn]
                elif i < 8:
                    q, k = bq[rows, h // 2, tok], bk[rows, k0:k0 + nn]
                else:
                    q, k = cq[rows, h, tok], ck[rows, h, k0:k0 + nn]
                bank = ps[su % 4]
                nc.tensor.matmul(bank[:, 0:nn], q, k, start=True, stop=False, skip_group_check=True)
                if i < 4 and b:
                    cols, mask = slice(0, nn), mask_bf[:]
                elif 4 <= i < 8 and b:
                    if i == 4:
                        pe.wait_ge(sel_done, 3 * l + SEL_ORDER.index(b) + 1)
                    cols, mask = slice(0, nn), sel_bf[:, score_at[b]:score_at[b] + nn]
                else:
                    cols, mask = slice(nn - 64, nn), mask_bf[:, 192:256]
                nc.tensor.matmul(bank[:, cols], id_bf[:], mask, start=False, stop=True,
                                 skip_group_check=True).then_inc(sc_done, 1)

        def turn_over(l, it):
            b, i = ITEMS[it]
            su = 16 * b + unit_col(i)
            if i >= 8:
                pe.wait_ge(comb_done, 4 * NT * l + 4 * b + (i - 8) + 1)
            else:
                pe.wait_ge(exp_done, N_SU * l + su + 1)
            if it >= 2:
                pe.wait_ge(pt_done, N_IT * l + it - 1)
            for j in range(keys_of(b, i)[1] // P):
                ins = nc.tensor.transpose(ps[6 + it % 2][:, j * P:(j + 1) * P],
                                          e_buf[su % 6][:, j * P:(j + 1) * P], ident)
            ins.then_inc(pt_psum, 1)

        def weigh(l, it):
            b, i = ITEMS[it]
            k0, nn = keys_of(b, i)
            pe.wait_ge(pt_done, N_IT * l + it + 1)
            if b and i in (0, 8):
                pe.wait_ge(y_out, 2 * NT * l + 2 * (b - 1) + (1 if i == 0 else 2))
            for j in range(nn // P):
                t = k0 // P + j
                h = i % 4
                if i < 4:
                    dst, v = ps[4][:, i * HD:(i + 1) * HD], av[:, t, (h // 2) * HD:(h // 2 + 1) * HD]
                elif i < 8:
                    dst, v = ps[4][:, i * HD:(i + 1) * HD], bv[:, t]
                else:
                    dst, v = ps[5][:, h * P:(h + 1) * P], cv[:, t, h * P:(h + 1) * P]
                ins = nc.tensor.matmul(dst, p_t[it % 2][:, j * P:(j + 1) * P], v, start=(j == 0),
                                       stop=(j == nn // P - 1), skip_group_check=True)
            ins.then_inc(pv_done, 1)

        def attention(l):
            pe.wait_ge(unit_out, N_U * (l + 1))
            pe.wait_ge(rope_done, N_R * (l + 1))
            pe.wait_ge(akx_done, 2 * l + 2)
            pe.wait_ge(relu_done, N_I * (l + 1))
            for it in range(N_IT + 3):
                if it < N_IT:
                    logits(l, it)
                if 2 <= it < N_IT + 2:
                    turn_over(l, it - 2)
                if it >= 3:
                    weigh(l, it - 3)
            for n in range(2 * NT):
                b, c = n // 2, n % 2
                if n == 0:
                    pe.wait_ge(y_out, 2 * NT * (l + 1))
                    pe.wait_ge(pt_done, N_IT * (l + 1))
                if c:
                    pe.wait_ge(cn_done, NT * l + b + 1)
                src = y_c if c else y_ab
                for t in range(4):
                    ins = nc.tensor.transpose(ps[n][:, t * P:(t + 1) * P],
                                              src[:, b, t * P:(t + 1) * P], ident)
                ins.then_inc(yt_done, 1)

        def output_projection(l):
            def body(i, p):
                pe.wait_ge(lo_done, BLOCKS * l + OUT_0 + p + 2 * i + 1 + CREDIT)
                w = [wb[p][:, 0:KD * P].rearrange("p (k n) -> p k n", n=P) for wb in (w_hi, w_lo)]
                for k in range(KD):
                    ins = product(ps[2 * p][:], [t[:, k] for t in w], (h_hi[:, k], h_lo[:, k]),
                                  k == 0, k == KD - 1)
                ins.then_inc(blk_done, 1)

            pe.wait_ge(ylo_done, 2 * NT * (l + 1))
            fence(pe)
            with pe.Fori(0, KD // 2) as i:
                for p in range(2):
                    body(i, p)
            sum_squares(NORMS * l + 2)

        with pe.Fori(0, DEPTH) as l:
            spread(NORMS * l)
            ffn(l, 0)
            spread(NORMS * l + 1)
            mixer_projections(l)
            attention(l)
            output_projection(l)
            spread(NORMS * l + 2)
            ffn(l, 1)

        for n in range(2 * NT):
            t, g = n // 2, n % 2
            pe.wait_ge(fin_done, 4 * g + 4 if t == 0 else KD)
            if n >= 4:
                pe.wait_ge(fout_b if g else fout_a, n // 2 - 1)
            for j in range(4):
                ins = nc.tensor.transpose(ps[n % 4][:, j * P:(j + 1) * P],
                                          x_t[:, 4 * g + j, t * P:(t + 1) * P], ident)
            ins.then_inc(ftr_done, 1)

    ctx.close()


INPUTS = ["x", "c", "positions", "w_mod", "b_mod", "norm_ffn1", "w_ffn1_in", "w_ffn1_out", "norm_mix",
          "w_in", "a_sinks", "b_kv_norm", "w_kv_up", "c_lambda_q1", "c_lambda_k1", "c_lambda_q2",
          "c_lambda_k2", "c_subln", "w_out", "norm_ffn2", "w_ffn2_in", "w_ffn2_out", "final_norm"]


def kernel(**inputs):
    import concourse.bacc as bacc
    from concourse.bass_utils import run_bass_kernel_spmd

    nc = bacc.Bacc("TRN2", target_bir_lowering=False, num_devices=1)
    arrays = {f"in_{name}": np.ascontiguousarray(inputs[name]) for name in INPUTS}
    arrays["in_consts"] = constants()
    a = {name[3:]: nc.dram_tensor(name, v.shape, mybir.dt.from_np(v.dtype), kind="ExternalInput").ap()
         for name, v in arrays.items()}
    out = nc.dram_tensor("out", (1, S, D), F32, kind="ExternalOutput").ap()
    trunk(nc, a, out)
    r = run_bass_kernel_spmd(nc, [arrays], core_ids=[0])
    return r.results[0]["out"]
```

```python
import math
from contextlib import ExitStack

import numpy as np
import concourse.bass as bass
from concourse import mybir
from concourse.alu_op_type import AluOpType as ALU

F32 = mybir.dt.float32
F32R = mybir.dt.float32r
BF16 = mybir.dt.bfloat16
I32 = mybir.dt.int32
ACT = mybir.ActivationFunctionType
AX = mybir.AxisListType

P = 128
S, D, DEPTH = 512, 1024, 2
KD = D // P
NT = S // P
D_FF = 2816
N_MOD = 9
HALVES = ((0, 12), (12, 10))
HD, CH, IDX = 64, 64, 32
TOPK = min(256, S // 4)
EPS = 1e-6
BIG = 1e30

A_Q, A_K, A_V, B_Q, B_KV, I_Q, I_K, I_W, C_Q, C_K, C_V, D_IN = (
    0, 256, 384, 512, 768, 896, 1024, 1056, 1060, 1572, 2084, 2596)

FFN_BLOCKS = sum(n for _, n in HALVES) + KD * len(HALVES)
MIX_BLOCKS = 12
FFN1_0 = 0
MIX_0 = FFN_BLOCKS
OUT_0 = MIX_0 + MIX_BLOCKS
FFN2_0 = OUT_0 + KD
BLOCKS = FFN2_0 + FFN_BLOCKS
F_TILES = D_FF // P
CREDIT = 2

C_ID, C_P64, C_P32, C_ONE, C_MASK, C_INV, C_EPS, C_HPI, C_LI, C_1LI = (
    0, 128, 256, 384, 512, 768, 770, 771, 772, 774)
N_CONST = 776
V_B, V_N1, V_NM, V_N2, V_FIN, V_KV, V_SUB, V_C = 0, 72, 80, 88, 96, 104, 105, 106
N_VEC = 114
V_SINK, V_NSINK, V_NLAM, V_SUBG, N_LAY = 114, 118, 122, 123, 124

TWO_PI = 2 * math.pi
PI_A = 6.28125
PI_B = float(np.float32(np.round((TWO_PI - PI_A) * 2 ** 17) / 2 ** 17))
PI_C = float(np.float32(TWO_PI - PI_A - PI_B))
ROUND = 12582912.0
PI_LO = 3.1415925


def constants():
    c = np.zeros((P, N_CONST), np.float32)
    c[:, C_ID:C_ID + P] = np.eye(P)
    for at, half in ((C_P64, HD // 2), (C_P32, IDX // 2)):
        for m in range(P):
            low = m % (2 * half) < half
            c[m + half if low else m - half, at + m] = -1.0 if low else 1.0
    c[:, C_ONE:C_ONE + P] = 1.0
    c[:, C_MASK:C_MASK + 64] = -BIG
    c[64:, C_MASK + 64:C_MASK + 128] = -BIG
    c[:64, C_MASK + 192:C_MASK + 256] = -BIG
    for n, dim in enumerate((HD, IDX)):
        inv = (10000.0 ** (-np.arange(0, dim, 2, dtype=np.float64) / dim)).astype(np.float32)
        c[:, C_INV + n] = np.tile(inv, P // (dim // 2))
    c[:, C_EPS] = EPS
    c[:, C_HPI] = math.pi / 2
    for l in range(DEPTH):
        li = 0.8 - 0.6 * math.exp(-0.3 * l)
        c[:, C_LI + l] = li
        c[:, C_1LI + l] = 1.0 - li
    return c


def trunk(nc, a, out):
    ctx = ExitStack()
    base = nc.sbuf_base
    top = [(base + 63) // 64 * 64]

    def place(name, shape, dt, at=None):
        n = int(np.prod(shape[1:])) * (2 if dt == BF16 else 4)
        where = top[0] if at is None else at
        if at is None:
            top[0] += (n + 31) // 32 * 32
        return nc.alloc_sbuf_tensor_at(name, list(shape), dt, offset=where), where

    def sb(name, shape, dt=F32, at=None):
        return place(name, shape, dt, at)[0]

    x_t = sb("x_t", [P, KD, S])
    h_at = top[0]
    h_hi = sb("h_hi", [P, KD, S], F32R)
    h_lo = sb("h_lo", [P, KD, S], F32R)
    region = top[0]
    nf_max = HALVES[0][1]
    a_hi = sb("a_hi", [P, nf_max, S], F32R)
    a_lo = sb("a_lo", [P, nf_max, S], F32R)
    region_end = top[0]
    w_raw = [sb(f"w_raw{p}", [P, 2048]) for p in range(2)]
    w_at = [top[0] + 4 * 2048 * n for n in range(4)]
    w_hi = [sb(f"w_hi{p}", [P, 2048], F32R) for p in range(2)]
    w_lo = [sb(f"w_lo{p}", [P, 2048], F32R) for p in range(2)]
    rot = sb("rot", [P, 4, S])
    wm = [sb(f"wm{p}", [P, D]) for p in range(2)]
    macc_at = top[0]
    macc = [sb(f"macc{p}", [P, D]) for p in range(2)]
    const = sb("const", [P, N_CONST])
    id_bf = sb("id_bf", [P, P], BF16)
    mask_bf = sb("mask_bf", [P, 256], BF16)
    lay = sb("lay", [P, DEPTH, N_LAY])
    cur = sb("cur", [P, N_LAY])
    c_act = sb("c_act", [P, KD])
    modc = sb("modc", [P, N_MOD, KD])
    coef = sb("coef", [P, 3, KD])
    gate = sb("gate", [P, 3, KD])
    temps = top[0]
    sil = [sb(f"sil{p}", [P, S]) for p in range(2)]
    a_f = [sb(f"a_f{p}", [P, S]) for p in range(2)]
    sq = [sb(f"sq{p}", [P, S]) for p in range(2)]
    sq_sum = sb("sq_sum", [P, S])
    sd = sb("sd", [P, NT])
    rstd = sb("rstd", [P, NT])
    diag = sb("diag", [P, NT, P])
    xn = [sb(f"xn{p}", [P, S]) for p in range(3)]
    temps_end = top[0]

    top[0] = region
    aq = sb("aq", [P, 2, S])
    ak = sb("ak", [P, S])
    akx = sb("akx", [P, S])
    bq = sb("bq", [P, 2, S])
    bk = sb("bk", [P, S])
    iq = sb("iq", [P, S])
    ik = sb("ik", [P, S])
    cq = sb("cq", [P, 4, S])
    ck = sb("ck", [P, 4, S])
    cv = sb("cv", [P, NT, S])
    av = sb("av", [P, NT, P])
    bv = sb("bv", [P, NT, HD])
    iw = sb("iw", [P, NT, 4])
    assert top[0] <= region_end
    top[0] = temps
    q_raw = [sb(f"q_raw{p}", [P, S]) for p in range(2)]
    t_cos = [sb(f"t_cos{p}", [P, S]) for p in range(2)]
    t_sin = [sb(f"t_sin{p}", [P, S]) for p in range(2)]
    kv_raw = sb("kv_raw", [P, S])
    kvn_hi = sb("kvn_hi", [P, S], F32R)
    kvn_lo = sb("kvn_lo", [P, S], F32R)
    rel = [sb(f"rel{p}", [P, S]) for p in range(2)]
    iw_raw = rel[0]
    mix_proj_end = top[0]
    score_at = [0, 0, 256, 640]
    score = sb("score", [P, 1152])
    sel_bf = sb("sel_bf", [P, 1152], BF16)
    top8 = sb("top8", [P, 8])
    stats_n = sb("stats_n", [P, 2, 16])
    stats_s = sb("stats_s", [P, 2, 16])
    stats_x = sb("stats_x", [P, 2, 4])
    stats_e = sb("stats_e", [P, 2, 4])
    stats_r = sb("stats_r", [P, 16])
    stats_f = sb("stats_f", [P, 16])
    c_ss = sb("c_ss", [P, 16])
    c_rs = sb("c_rs", [P, 16])
    mixer_top = top[0]
    top[0] = temps
    e_buf = [sb(f"e_buf{p}", [P, S]) for p in range(4)] + [iq, ik]
    p_t = [sb(f"p_t{p}", [P, S]) for p in range(2)]
    c_sq = sb("c_sq", [P, S])
    y_c = sb("y_c", [P, NT, S])
    assert top[0] <= mix_proj_end
    y_ab = sb("y_ab", [P, NT, S], at=macc_at)
    high = max(temps_end, mixer_top)
    assert high <= nc.sbuf_usable_end, (high, nc.sbuf_usable_end)
    top[0] = region
    x_nat = sb("x_nat", [P, NT, D])
    vec_rows = sb("vec_rows", [P, DEPTH, P])
    pos_i = sb("pos_i", [P, S], I32)
    pos_f = sb("pos_f", [P, S])
    ang = [sb(f"ang{n}", [P, S]) for n in range(2)]
    lam_v = sb("lam_v", [P, 4, DEPTH, HD])
    lam_p = sb("lam_p", [P, 2, DEPTH, HD])
    lam_s = sb("lam_s", [P, 2, DEPTH])
    boot_wm = [sb(f"boot_wm{j}", [P, 2, D], at=h_at + 8 * D * j) for j in range(4)]
    boot_wm += [sb(f"boot_wm{j}", [P, 2, D]) for j in (4, 5)]
    assert top[0] <= region_end
    boot_wm += [sb(f"boot_wm{j}", [P, 2, D], at=at) for j, at in ((6, w_at[1]), (7, w_at[3]))]
    out_nat = sb("out_nat", [P, NT, D], at=region)

    ps = [ctx.enter_context(nc.psum_tensor(f"ps{b}", [P, S], F32)) for b in range(8)]
    SUM, MISC = 4, (5, 7)

    ident = const[:, C_ID:C_ID + P]
    ones = const[:, C_ONE:C_ONE + P]

    def sem(name):
        return ctx.enter_context(nc.semaphore(name))

    const_in = sem("const_in")
    vec_in = sem("vec_in")
    boot_in = [sem(f"boot_in{j}") for j in range(KD)]
    lam_in = sem("lam_in")
    x_in = sem("x_in")
    pos_in = sem("pos_in")
    raw_in = [sem(f"raw_in{p}") for p in range(2)]
    hi_done = sem("hi_done")
    lo_done = sem("lo_done")
    blk_done = sem("blk_done")
    wm_in = [sem(f"wm_in{p}") for p in range(2)]
    wm_used = sem("wm_used")
    acc_zero = sem("acc_zero")
    mod_sum = sem("mod_sum")
    mod_out = sem("mod_out")
    silu_done = sem("silu_done")
    mul_done = sem("mul_done")
    ahi_done = sem("ahi_done")
    alo_done = sem("alo_done")
    x_done = sem("x_done")
    sq_done = sem("sq_done")
    sq_added = sem("sq_added")
    sum_done = sem("sum_done")
    sd_done = sem("sd_done")
    rstd_done = sem("rstd_done")
    diag_done = sem("diag_done")
    spread_done = sem("spread_done")
    xn_done = sem("xn_done")
    hhi_done = sem("hhi_done")
    hlo_done = sem("hlo_done")
    cur_done = sem("cur_done")
    mod_step = sem("mod_step")
    passed = sem("passed")
    tr_done = sem("tr_done")
    boot_step = sem("boot_step")
    start_act = sem("start_act")
    start_dve = sem("start_dve")
    unit_done = sem("unit_done")
    unit_out = sem("unit_out")
    swap_done = sem("swap_done")
    rope_done = sem("rope_done")
    kv_act = sem("kv_act")
    kv_sum = sem("kv_sum")
    kvn_done = sem("kvn_done")
    kvn_hi_done = sem("kvn_hi_done")
    kvn_lo_done = sem("kvn_lo_done")
    akx_done = sem("akx_done")
    iw_turned = sem("iw_turned")
    iw_done = sem("iw_done")
    idx_done = sem("idx_done")
    relu_done = sem("relu_done")
    idx_acc = sem("idx_acc")
    dve_step = sem("dve_step")
    sel_done = sem("sel_done")
    sc_done = sem("sc_done")
    max_done = sem("max_done")
    exp_done = sem("exp_done")
    sink_in = sem("sink_in")
    sink_done = sem("sink_done")
    comb_done = sem("comb_done")
    pt_psum = sem("pt_psum")
    pt_done = sem("pt_done")
    pv_done = sem("pv_done")
    y_out = sem("y_out")
    css_done = sem("css_done")
    csd_done = sem("csd_done")
    cn_done = sem("cn_done")
    yt_done = sem("yt_done")
    yhi_done = sem("yhi_done")
    ylo_done = sem("ylo_done")
    fin_done = sem("fin_done")
    ftr_done = sem("ftr_done")
    fout_a = sem("fout_a")
    fout_b = sem("fout_b")
    stored = sem("stored")

    FFN1 = [("in", 0, [(2, 2), (2, 3), (2, None)]), ("out", 0, [(2, 4), (2, None)]),
            ("in", 1, [(2, 5), (2, 6), (1, None)]), ("out", 1, [(2, 7), (2, None)])]
    FFN2 = [("in", 0, [(2, 8), (4, None)]), ("out", 0, [(4, None)]),
            ("in", 1, [(2, 9), (2, 10), (1, None)]), ("out", 1, [(4, None)])]

    def walk(which):
        s, f = (FFN1_0, FFN2_0)[which], F_TILES * which
        for kind, half, segments in (FFN1, FFN2)[which]:
            step = 0
            for pairs, module in segments:
                yield kind, half, pairs, module, s, step, f
                s += 2 * pairs
                step += 2 * pairs
                if kind == "in":
                    f += 2 * pairs

    MIX = [(B_KV, 256), (I_K, 36), (A_Q, 256), (A_K, 256), (B_Q, 256), None,
           (C_Q, 256), (C_Q + 256, 256), (C_K, 256), (C_K + 256, 256), (C_V, 256), (C_V + 256, 256)]
    KV_UP, INDEX_KEYS = 5, 1
    UNITS = [(0, "kv", kv_raw[:]), (0, "i32", iq[:]), (1, "i32", ik[:]),
             (2, "q64", aq[:, 0]), (2, "q64", aq[:, 1]), (3, "k64", ak[:]), (3, "turn", av[:]),
             (4, "q64", bq[:, 0]), (4, "q64", bq[:, 1]), (5, "k64", bk[:]), (5, "nat", bv),
             (6, "q64", cq[:, 0]), (6, "q64", cq[:, 1]), (7, "q64", cq[:, 2]), (7, "q64", cq[:, 3]),
             (8, "k64", ck[:, 0]), (8, "k64", ck[:, 1]), (9, "k64", ck[:, 2]), (9, "k64", ck[:, 3]),
             *[(10 + h // 2, "turn", cv[:, :, h * P:(h + 1) * P]) for h in range(4)]]
    ROPED = [u for u, (_, kind, _) in enumerate(UNITS) if kind in ("i32", "q64", "k64", "turn")]
    MOVED = [u for u in ROPED if UNITS[u][1] in ("i32", "turn")]
    UNIT_IK, UNIT_AK = 2, 5
    N_U, N_R, N_M = len(UNITS), len(ROPED), len(MOVED)
    IDX_ITEMS = [(b, h) for b in (1, 2, 3) for h in range(4)]
    N_I = len(IDX_ITEMS)
    IDX_AFTER = {u: (2 * j, 2 * j + 1) for j, u in enumerate(range(5, 5 + N_I // 2))}
    TK = TOPK // 8
    TOPK_PLAN = {4: [(1, 0, 4)], 5: [(1, 4, 8)], 6: [(1, 8, 12)], 7: [(1, 12, 16)],
                 8: [(2, 0, 3)], 9: [(2, 3, 6)], 10: [(2, 6, 12)], 11: [(2, 12, 16), (3, 0, 2)]}
    LATE_ROUNDS = {1 + j: (3, r) for j, r in enumerate(range(2, TK))}
    SEL_ORDER = [1, 2, 3]
    def keys_of(b, fam):
        return (max(b - 1, 0) * P, P * min(b + 1, 2)) if fam == "A" else (0, P * (b + 1))

    ITEMS = []
    N_SU = 0
    for b in range(NT):
        for fam in "ABC":
            per = S // keys_of(b, fam)[1]
            if fam != "C":
                per = min(per, 2)
            heads = range(4) if fam == "C" else (0, 2, 1, 3)
            for m in range(0, 4, per):
                maps = [(h, j) for j in range(2 if fam == "C" else 1) for h in heads[m:m + per]]
                ITEMS.append((b, fam, maps, per, N_SU))
                N_SU += len(maps) // per
    N_IT, N_C = len(ITEMS), sum(item[1] == "C" for item in ITEMS)

    def stat(fam, m):
        return 8 + 2 * m[0] + m[1] if fam == "C" else m[0] + (4 if fam == "B" else 0)

    def banks_of(it):
        _, _, maps, per, su = ITEMS[it]
        return [(su + n, maps[n * per:(n + 1) * per]) for n in range(len(maps) // per)]

    def heads_of(it):
        return sorted({h for h, _ in ITEMS[it][2]})

    def items_through(b, fam):
        return 1 + max(n for n, item in enumerate(ITEMS) if item[:2] == (b, fam))

    NORMS = 3
    VEC_DMAS = 8
    CHAIN = N_R - sum(kind == "turn" for _, kind, _ in UNITS) + 1 + 3 + 3 * 2 * TK + sum(item[1] == "A" for item in ITEMS) \
        + 2 * sum(item[1] == "C" for item in ITEMS) + 2 * NT + 2 * NT + 1

    def used(l, s):
        return (BLOCKS - MIX_BLOCKS) * l + (s if s <= MIX_0 + 1 else s - MIX_BLOCKS)

    def units_through(n):
        return sum(unit[0] <= n for unit in UNITS)

    def fence(eng):
        eng.sem_inc(passed, 1)

    def at_col(t, k):
        return t[:, bass.ds(k, 1)].rearrange("p a s -> p (a s)")

    def block_len(s):
        if MIX_0 <= s < OUT_0:
            cols = MIX[s - MIX_0]
            return KD * cols[1] if cols else P
        if OUT_0 <= s < FFN2_0:
            return KD * P
        r = s - FFN1_0 if s < MIX_0 else s - FFN2_0
        for _, nf in HALVES:
            if r < nf:
                return 2 * KD * P
            if r < nf + KD:
                return nf * P
            r -= nf + KD
        return None

    def split_views(s, p):
        if s == MIX_0 + INDEX_KEYS:
            raw = w_raw[p][:, 0:KD * 36].rearrange("p (k n) -> p k n", n=36)
            hi, lo = (w[p][:, 0:KD * 100].rearrange("p (k n) -> p k n", n=100) for w in (w_hi, w_lo))
            return [(raw[:, :, 0:n], hi[:, :, at:at + n], lo[:, :, at:at + n])
                    for at, n in ((0, IDX), (IDX, IDX), (2 * IDX, IDX + 4))]
        if s == MIX_0 + KV_UP:
            return [(w_raw[p][:, 0:64], w_hi[p][:, 0:64], w_lo[p][:, 0:64]),
                    (w_raw[p][:, 0:128], w_hi[p][:, 64:192], w_lo[p][:, 64:192])]
        n = block_len(s)
        return [(w_raw[p][:, 0:n], w_hi[p][:, 0:n], w_lo[p][:, 0:n])]

    def run_segment(eng, s0, pairs, body):
        sizes = [block_len(s0 + 1 + j) for j in range(2 * pairs)]
        whole = pairs if len(set(sizes)) == 1 and s0 + 2 * pairs not in (MIX_0, BLOCKS) else pairs - 1
        if whole:
            with eng.Fori(0, whole) as i:
                for p in range(2):
                    body(i, p, s0 + p + 1)
        if whole < pairs:
            body(pairs - 1, 0, s0 + 1)
            nxt = s0 + 2 * pairs
            body(pairs - 1, 1, None if nxt == BLOCKS else nxt - 2 * (pairs - 1))

    w_mod = a["w_mod"].rearrange("l (k p) n -> l p k n", p=P)

    def load_chunk(eng, source_l, l, q, k, p):
        eng.wait_ge(wm_used, 72 * l + 8 * q + k + 1)
        fence(eng)
        m = q % N_MOD
        eng.dma_start(wm[p][:], w_mod[source_l, :, bass.ds(k, 1), m * D:(m + 1) * D]
                      .rearrange("p a n -> p (a n)")).then_inc(wm_in[p], 16)

    def vec_src(name):
        return a[name].rearrange("l (r c) -> r l c", c=P)

    def load_vec(eng, row, src):
        eng.dma_start(vec_rows[row:row + src.shape[0]], src).then_inc(vec_in, 16)

    block = ctx.enter_context(nc.Block())

    @block.sync
    def _(sp):
        sp.dma_start(const[:], a["consts"]).then_inc(const_in, 16)
        load_vec(sp, V_B, vec_src("b_mod"))
        load_vec(sp, V_N1, vec_src("norm_ffn1"))
        load_vec(sp, V_FIN, a["final_norm"].rearrange("(r c) -> r c", c=P).unsqueeze(1)
                 .broadcast_to([KD, DEPTH, P]))
        for n, name in enumerate(("c_lambda_q1", "c_lambda_k1", "c_lambda_q2", "c_lambda_k2")):
            sp.dma_start(lam_v[:, n], a[name].unsqueeze(0).broadcast_to([P, DEPTH, HD])
                         ).then_inc(lam_in, 16)
        load_vec(sp, V_C, a["c"].rearrange("b (r c) -> (b r) c", c=P).unsqueeze(1)
                 .broadcast_to([KD, DEPTH, P]))
        x_rows = a["x"].rearrange("b (t p) d -> (b p) t d", p=P)
        w_in_r = a["w_in"].rearrange("l (k p) n -> l p k n", p=P)
        w_out_r = a["w_out"].rearrange("l (k p) n -> l p k n", p=P)

        def load_block(s, p, parts):
            sp.wait_ge(lo_done, s + 1)
            fence(sp)
            for dst, src in parts:
                sp.dma_start(dst, src).then_inc(raw_in[p], 16)

        def slot(p, n):
            return lambda tiles: w_raw[p][:, 0:tiles * n].rearrange("p (k n) -> p k n", n=n)

        def ffn(l, which):
            w_up, w_down = (("w_ffn1_in", "w_ffn1_out"), ("w_ffn2_in", "w_ffn2_out"))[which]
            up = a[w_up].rearrange("l (k p) (g f) -> l p k g f", p=P, g=2)
            down = a[w_down].rearrange("l (f p) n -> l p f n", p=P)
            for kind, half, pairs, module, s0, step, _ in walk(which):
                f0, nf = HALVES[half]
                with sp.Fori(0, pairs) as i:
                    for p in range(2):
                        s = BLOCKS * l + s0 + p + 2 * i
                        if kind == "in":
                            dst = w_raw[p][:].rearrange("p (k g f) -> p k g f", k=KD, g=2)
                            col = bass.ds(i * 2 * P + (f0 + step + p) * P, P)
                            load_block(s, p, [(dst[:, :, g], up[l, :, :, g, col]) for g in range(2)])
                        else:
                            dst = slot(p, P)(nf)
                            col = bass.ds(i * 2 * P + (step + p) * P, P)
                            cut = (slice(0, nf // 2), slice(nf // 2, nf))
                            load_block(s, p, [(dst[:, c], down[l, :, f0 + c.start:f0 + c.stop, col])
                                              for c in cut])

        sp.wait_ge(vec_in, 16 * VEC_DMAS)
        for q in range(2):
            for j in range(4):
                sp.dma_start(boot_wm[4 * q + j][:], w_mod[0, :, 2 * j:2 * j + 2, q * D:(q + 1) * D]
                             ).then_inc(boot_in[4 * q + j], 16)
            if q == 0:
                for t in (0, 2):
                    sp.dma_start(x_nat[:, t:t + 2], x_rows[:, t:t + 2]).then_inc(x_in, 16)
        with sp.Fori(0, DEPTH) as l:
            ffn(l, 0)
            for n, cols in enumerate(MIX):
                p = n % 2
                if cols is None:
                    parts = [(w_raw[p][:, g:g + 64], a["w_kv_up"][l, :, g:g + 64]) for g in (0, 64)]
                else:
                    dst = slot(p, cols[1])(KD)
                    parts = [(dst[:, g:g + 4], w_in_r[l, :, g:g + 4, cols[0]:sum(cols)])
                             for g in (0, 4)]
                load_block(BLOCKS * l + MIX_0 + n, p, parts)
            with sp.Fori(0, KD // 2) as i:
                for p in range(2):
                    dst = slot(p, P)(KD)
                    load_block(BLOCKS * l + OUT_0 + p + 2 * i, p,
                               [(dst[:, g:g + 4], w_out_r[l, :, g:g + 4, bass.ds(i * 2 * P + p * P, P)])
                                for g in (0, 4)])
            ffn(l, 1)

        o_rows = out.rearrange("b (t p) d -> (b p) t d", p=P)
        for t in range(NT):
            sp.wait_ge(fout_a, t + 1)
            sp.wait_ge(fout_b, t + 1)
            sp.dma_start(o_rows[:, t], out_nat[:, t]).then_inc(stored, 16)
        sp.wait_ge(stored, 16 * NT)

    @block.scalar
    def _(act):
        def split_hi(l, s, i=0):
            p = s % 2
            act.wait_ge(raw_in[p], 32 * (BLOCKS // 2) * l + 32 * (s // 2) + 32 * i + 32)
            if MIX_0 + 2 <= s <= OUT_0:
                act.wait_ge(unit_done, N_U * l + units_through(s - 2 - MIX_0))
            else:
                act.wait_ge(blk_done, used(l, s) + 2 * i + 1)
            for raw, hi, _ in split_views(s + 2 * i if isinstance(i, int) else s, p):
                ins = nc.scalar.activation(hi, raw, ACT.Copy)
            ins.then_inc(hi_done, 1)

        def square(x_n, l, m, i, j, p):
            k = 2 * i + j
            act.wait_ge(x_done, x_n + 1)
            act.wait_ge(sq_added, (KD - 1) * NORMS * l + 2 * i + ((KD - 1) * m + j - 1))
            nc.scalar.activation(sq[p][:], at_col(x_t, k), ACT.Square).then_inc(sq_done, 1)

        def root_of_mean(dst, src, n):
            return nc.scalar.activation(dst, src, ACT.Sqrt, scale=1.0 / n,
                                        bias=const[:, C_EPS:C_EPS + 1])

        def norm(l, n):
            v = NORMS * l + n
            act.wait_ge(sum_done, v + 1)
            root_of_mean(sd[:], ps[SUM][:, 0:NT], D).then_inc(sd_done, 1)
            act.wait_ge(mod_out, N_MOD * l + 3 * n + 2)
            for k in range(KD):
                act.wait_ge(xn_done, KD * v + k + 1)
                nc.scalar.activation(h_hi[:, k], xn[k % 3][:], ACT.Identity,
                                     bias=modc[:, 3 * n, k:k + 1]).then_inc(hhi_done, 1)

        def ffn(l, which):
            for kind, half, pairs, module, s0, step, f0 in walk(which):
                def body(i, p, prepared):
                    if module is not None:
                        for c in range(2):
                            load_chunk(act, l if module < N_MOD else 1 - l, l, module,
                                       4 * i + (2 * p + c), c)
                    if prepared is not None:
                        split_hi(l, prepared, i)
                    if kind == "in":
                        f = 2 * F_TILES * l + f0 + p + 2 * i
                        act.wait_ge(blk_done, used(l, s0 + p) + 2 * i + 1 + CREDIT)
                        nc.scalar.activation(sil[p][:], ps[2 * p][:], ACT.Silu).then_inc(silu_done, 1)
                        act.wait_ge(mul_done, f + 1)
                        nc.scalar.activation(at_col(a_hi, 2 * i + (step + p)), a_f[p][:], ACT.Copy
                                             ).then_inc(ahi_done, 1)
                    elif half == 1:
                        square(KD + 40 * l + (24 * which + KD + step + p) + 2 * i, l,
                               1 + 2 * which, i, step + p, p)

                run_segment(act, s0, pairs, body)

        for row, name in ((V_NM, "norm_mix"), (V_N2, "norm_ffn2"), (V_KV, "b_kv_norm"),
                          (V_SUB, "c_subln")):
            load_vec(act, row, vec_src(name))
        act.dma_start(pos_i[:], a["positions"].broadcast_to([P, S])).then_inc(pos_in, 16)
        act.dma_start(lay[:, :, V_SINK:V_SINK + 4],
                      a["a_sinks"].unsqueeze(0).broadcast_to([P, DEPTH, 4])).then_inc(lam_in, 16)
        act.wait_ge(const_in, 16)
        act.wait_ge(tr_done, 2)
        for l in range(DEPTH):
            nc.scalar.activation(lay[:, l, 0:N_VEC], ps[6 + l][:, 0:N_VEC], ACT.Copy
                                 ).then_inc(start_act, 1)
        nc.scalar.activation(c_act[:], ps[6][:, V_C:V_C + KD], ACT.Silu).then_inc(start_act, 1)
        act.wait_ge(start_dve, 1)
        nc.scalar.activation(lam_s[:], lam_s[:], ACT.Exp).then_inc(start_act, 1)
        for n in range(2):
            act.wait_ge(start_dve, 2 + n)
            nc.scalar.activation(rot[:, 2 * n + 1], ang[n][:], ACT.Sin).then_inc(start_act, 1)
            nc.scalar.activation(rot[:, 2 * n], rot[:, 2 * n], ACT.Sin, scale=-1.0,
                                 bias=const[:, C_HPI:C_HPI + 1]).then_inc(start_act, 1)
        for k in range(KD):
            if k >= 2:
                act.wait_ge(sq_added, k - 1)
            act.wait_ge(x_done, k + 1)
            nc.scalar.activation(sq[k % 2][:], x_t[:, k], ACT.Square).then_inc(sq_done, 1)

        def evac(l, u):
            _, kind, dst = UNITS[u]
            act.wait_ge(unit_done, N_U * l + u + 1)
            src = ps[u % 4][:]
            if kind == "kv":
                nc.scalar.activation(dst, src, ACT.Copy).then_inc(unit_out, 1)
                nc.scalar.activation(rel[0][:], src, ACT.Square).then_inc(kv_act, 1)
                act.wait_ge(kv_sum, l + 1)
                root_of_mean(rel[1][:], ps[SUM][:], P).then_inc(kv_act, 1)
            elif u in ROPED:
                r = ROPED.index(u)
                scale = HD ** -0.5 if kind == "q64" else 1.0
                if r >= 2:
                    act.wait_ge(rope_done, N_R * l + r - 1)
                rows = 96 if u == UNIT_IK else P
                ins = nc.scalar.activation(q_raw[r % 2][0:rows, :], src[0:rows], ACT.Copy, scale=scale)
                if u == UNIT_IK:
                    nc.scalar.activation(q_raw[r % 2][96:128, :], src[0:IDX], ACT.Copy)
                    ins = nc.scalar.activation(iw_raw[96:100, :], src[96:100], ACT.Copy)
                if kind in ("q64", "k64"):
                    for g in range(4):
                        ins = nc.scalar.activation(t_sin[r % 2][32 * g:32 * g + 32, :],
                                                   src[32 * (g ^ 1):32 * (g ^ 1) + 32], ACT.Copy,
                                                   scale=scale if g % 2 else -scale)
                ins.then_inc(unit_out, 1)
            else:
                n = dst.shape[2]
                nc.scalar.activation(dst[:], src[:, 0:NT * n].rearrange("p (t n) -> p t n", n=n),
                                     ACT.Copy).then_inc(unit_out, 1)

        def mixer_projections(l):
            def outs(n, last):
                for u in [u for u in range(N_U) if UNITS[u][0] == n][slice(1, 9) if last else slice(1)]:
                    evac(l, u)
                    for x in IDX_AFTER.get(u, ()):
                        nn = P * (IDX_ITEMS[x][0] + 1)
                        act.wait_ge(idx_done, N_I * l + x + 1)
                        if x >= 2:
                            act.wait_ge(idx_acc, N_I * l + x - 1)
                        nc.scalar.activation(rel[x % 2][:, 0:nn], ps[4 + x % 2][:, 0:nn], ACT.Relu
                                             ).then_inc(relu_done, 1)

            for n in range(MIX_BLOCKS):
                split_hi(l, MIX_0 + n + 1)
                outs(n - 1, True)
                outs(n, False)
                if n == 3:
                    act.wait_ge(kvn_done, l + 1)
                    nc.scalar.activation(kvn_hi[:], kv_raw[:], ACT.Copy).then_inc(kvn_hi_done, 1)
                if n == 4:
                    act.wait_ge(rope_done, N_R * l + ROPED.index(UNIT_AK) + 1)
                    nc.scalar.activation(akx[0:64, :], ak[64:128, :], ACT.Copy).then_inc(akx_done, 1)
                    nc.scalar.activation(akx[64:128, :], ak[0:64, :], ACT.Copy).then_inc(akx_done, 1)
            outs(MIX_BLOCKS - 1, True)

        def exps(l, it):
            b, fam, _, _, _ = ITEMS[it]
            nn = keys_of(b, fam)[1]
            par = b % 2
            if b >= 2 and items_through(b - 1, "C") == it:
                act.wait_ge(y_out, 2 * NT * l + 2 * (b - 1))
            for su, maps in banks_of(it):
                act.wait_ge(max_done, N_SU * l + su + 1)
                for n, m in enumerate(maps):
                    c = stat(fam, m)
                    cols = slice(n * nn, (n + 1) * nn)
                    ins = nc.scalar.activation(e_buf[su % 6][:, cols], ps[su % 4][:, cols], ACT.Exp,
                                               bias=stats_n[:, par, c:c + 1],
                                               accum_out=stats_s[:, par, c:c + 1])
                ins.then_inc(exp_done, 1)
            if it + 1 == items_through(b, "A"):
                act.wait_ge(sink_in, NT * l + b + 1)
                nc.scalar.activation(stats_e[:, par], stats_x[:, par], ACT.Exp).then_inc(sink_done, 1)

        def evac_p(l, it):
            b, fam, _, _, _ = ITEMS[it]
            nn = keys_of(b, fam)[1] * len(heads_of(it))
            act.wait_ge(pt_psum, N_IT * l + it + 1)
            if it >= 2:
                act.wait_ge(pv_done, N_IT * l + it - 1)
            nc.scalar.activation(p_t[it % 2][:, 0:nn], ps[6 + it % 2][:, 0:nn], ACT.Copy
                                 ).then_inc(pt_done, 1)

        def attention(l):
            act.wait_ge(rope_done, N_R * (l + 1))
            act.wait_ge(kvn_lo_done, l + 1)
            for it in range(N_IT):
                exps(l, it)
                if it >= 2:
                    evac_p(l, it - 2)
            for it in (N_IT - 2, N_IT - 1):
                evac_p(l, it)
            for n in range(2 * NT):
                b, c = n % NT, n // NT
                if n == NT:
                    act.wait_ge(css_done, l + 1)
                    nc.scalar.activation(c_rs[:], c_ss[:], ACT.Sqrt, scale=1.0 / P,
                                         bias=const[:, C_EPS:C_EPS + 1]).then_inc(csd_done, 1)
                act.wait_ge(yt_done, 2 * NT * l + n + 1)
                nc.scalar.activation(h_hi[:, 4 * c:4 * c + 4, b * P:(b + 1) * P],
                                     ps[n][:].rearrange("p (t s) -> p t s", s=P), ACT.Copy,
                                     scale=cur[:, V_SUBG:V_SUBG + 1] if c else 1.0
                                     ).then_inc(yhi_done, 1)

        with act.Fori(0, DEPTH) as l:
            split_hi(l, 0)
            norm(l, 0)
            ffn(l, 0)
            norm(l, 1)
            mixer_projections(l)
            attention(l)

            def out_step(i, p, prepared):
                split_hi(l, prepared, i)
                square(KD + 40 * l + 2 * KD + p + 2 * i, l, 2, i, p, p)

            run_segment(act, OUT_0, KD // 2, out_step)
            norm(l, 2)
            ffn(l, 1)

        act.wait_ge(sum_done, NORMS * DEPTH + 1)
        root_of_mean(sd[:], ps[SUM][:, 0:NT], D).then_inc(sd_done, 1)
        act.wait_ge(rstd_done, NORMS * DEPTH + 1)
        for n in range(0, 2 * NT, 2):
            act.wait_ge(ftr_done, n + 1)
            nc.scalar.activation(out_nat[:, n // 2, 0:S], ps[n % 4][:], ACT.Copy,
                                 scale=rstd[:, n // 2:n // 2 + 1]).then_inc(fout_a, 1)

    @block.vector
    def _(dve):
        def split_lo(l, s, i=0):
            dve.wait_ge(hi_done, BLOCKS * l + s + 2 * i + 1)
            for raw, hi, lo in split_views(s + 2 * i if isinstance(i, int) else s, s % 2):
                ins = nc.vector.tensor_tensor(lo, raw, hi.bitcast(F32), ALU.subtract)
            ins.then_inc(lo_done, 1)

        def clear(l, q):
            nc.vector.memset(macc[q % N_MOD % 2][:], 0.0).then_inc(acc_zero, 1)
            dve.wait_ge(acc_zero, N_MOD * l + q - 1)
            fence(dve)

        def chunk(l, q, k, p):
            acc = macc[q % N_MOD % 2][:]
            dve.wait_ge(wm_in[p], 16 * 36 * l + 16 * 4 * (q - 2) + 8 * (k - p) + 16)
            dve.wait_ge(wm_used, 72 * l + 8 * q + k + CREDIT)
            nc.vector.scalar_tensor_tensor(acc, wm[p][:], c_act[:, bass.ds(k, 1)], acc,
                                           ALU.mult, ALU.add).then_inc(wm_used, 1)

        def module_out(l, q, src):
            m = q % N_MOD
            n, par = m // 3, m % 2
            dve.wait_ge(mod_sum, N_MOD * l + q + 1)
            fence(dve)
            ins = nc.vector.tensor_tensor(modc[:, m], ps[MISC[par]][:, 0:8],
                                          src[:, V_B + 8 * m:V_B + 8 * m + 8], ALU.add)
            if m % 3:
                ins.then_inc(mod_step, 1)
                dve.wait_ge(mod_step, 6 * l + q - q // 3)
                if m % 3 == 1:
                    g = (V_N1, V_NM, V_N2)[n]
                    ins = nc.vector.scalar_tensor_tensor(coef[:, n], modc[:, m], 1.0,
                                                         src[:, g:g + KD], ALU.add, ALU.mult)
                else:
                    ins = nc.vector.tensor_scalar(gate[:, n], modc[:, m], 1.0 if n == 1 else 0.5,
                                                  None, ALU.mult)
            ins.then_inc(mod_out, 1)
            dve.wait_ge(mod_out, N_MOD * l + q + 1)
            fence(dve)

        def norm(l, n):
            v = NORMS * l + n
            dve.wait_ge(sd_done, v + 1)
            nc.vector.reciprocal(rstd[:], sd[:]).then_inc(rstd_done, 1)
            dve.wait_ge(rstd_done, v + 1)
            for t in range(NT):
                fence(dve)
                nc.vector.tensor_scalar(diag[:, t], ident, rstd[:, t:t + 1], None, ALU.mult
                                        ).then_inc(diag_done, 1)

            def rest(k):
                dve.wait_ge(hhi_done, KD * v + k + 1)
                nc.vector.scalar_tensor_tensor(h_lo[:, k], xn[k % 3][:], modc[:, 3 * n, k:k + 1],
                                               h_hi[:, k].bitcast(F32), ALU.add, ALU.subtract
                                               ).then_inc(hlo_done, 1)

            dve.wait_ge(spread_done, v + 1)
            for k in range(KD):
                if k >= 3:
                    dve.wait_ge(hlo_done, KD * v + k - 2)
                nc.vector.scalar_tensor_tensor(xn[k % 3][:], x_t[:, k], coef[:, n, k:k + 1],
                                               ps[SUM][:], ALU.mult, ALU.mult).then_inc(xn_done, 1)
                if k:
                    rest(k - 1)
            rest(KD - 1)

        def x_update(s, p, k, g):
            dve.wait_ge(blk_done, s + 1 + CREDIT)
            xk = at_col(x_t, k)
            nc.vector.scalar_tensor_tensor(xk, ps[2 * p][:], gate[:, g, bass.ds(k, 1)], xk,
                                           ALU.mult, ALU.add).then_inc(x_done, 1)

        def ffn(l, which):
            for kind, half, pairs, module, s0, step, f0 in walk(which):
                if module is not None:
                    clear(l, module)

                def body(i, p, prepared):
                    if prepared is not None:
                        split_lo(l, prepared, i)
                    if module is not None:
                        for c in range(2):
                            chunk(l, module, 4 * i + (2 * p + c), c)
                    if kind == "in":
                        f = 2 * F_TILES * l + f0 + p + 2 * i
                        dve.wait_ge(silu_done, f + 1)
                        nc.vector.tensor_tensor(a_f[p][:], ps[2 * p + 1][:], sil[p][:], ALU.mult
                                                ).then_inc(mul_done, 1)
                        dve.wait_ge(ahi_done, f + 1)
                        k = 2 * i + (step + p)
                        nc.vector.tensor_tensor(at_col(a_lo, k), a_f[p][:],
                                                at_col(a_hi, k).bitcast(F32), ALU.subtract
                                                ).then_inc(alo_done, 1)
                    else:
                        x_update(used(l, s0 + p) + 2 * i, p, 2 * i + (step + p), 2 * which)

                run_segment(dve, s0, pairs, body)
                if module is not None:
                    src = cur if module < N_MOD else lay[:, bass.ds(1 - l, 1)].rearrange(
                        "p a n -> p (a n)")
                    module_out(l, module, src)

        boots = [0]

        def boot(ins):
            boots[0] += 1
            ins.then_inc(boot_step, 1)
            dve.wait_ge(boot_step, boots[0])

        dve.sem_inc(lo_done, CREDIT)
        dve.sem_inc(wm_used, CREDIT)
        dve.wait_ge(const_in, 16)
        nc.vector.tensor_copy(id_bf[:], ident)
        nc.vector.tensor_copy(mask_bf[:], const[:, C_MASK:C_MASK + 256])
        dve.wait_ge(lam_in, 16 * 5)
        boot(nc.vector.tensor_tensor(lam_p[:], lam_v[:, 0:4:2], lam_v[:, 1:4:2], ALU.mult))
        nc.vector.tensor_reduce(lam_s[:], lam_p[:], AX.X, ALU.add).then_inc(start_dve, 1)
        dve.wait_ge(pos_in, 16)
        boot(nc.vector.tensor_copy(pos_f[:], pos_i[:]))
        for n in range(2):
            turn = rot[:, 2 * n]
            boot(nc.vector.tensor_scalar(ang[n][:], pos_f[:], const[:, C_INV + n:C_INV + n + 1], None,
                                         ALU.mult))
            boot(nc.vector.tensor_scalar(turn, ang[n][:], 1.0 / TWO_PI, ROUND, ALU.mult, ALU.add))
            boot(nc.vector.tensor_scalar(turn, turn, ROUND, None, ALU.subtract))
            for part in (PI_A, PI_B, PI_C):
                boot(nc.vector.scalar_tensor_tensor(ang[n][:], turn, -part, ang[n][:],
                                                    ALU.mult, ALU.add))
            boot(nc.vector.tensor_scalar(ang[n][:], ang[n][:], PI_LO, -PI_LO, ALU.min, ALU.max))
            nc.vector.scalar_tensor_tensor(turn, ang[n][:], -1.0, ang[n][:], ALU.mult, ALU.max
                                           ).then_inc(start_dve, 1)
        dve.wait_ge(start_act, 4)
        nc.vector.tensor_scalar(lay[:, :, V_NSINK:V_NSINK + 4], lay[:, :, V_SINK:V_SINK + 4], -1.0,
                                None, ALU.mult)
        boot(nc.vector.tensor_tensor(lam_s[:, 0], lam_s[:, 1], lam_s[:, 0], ALU.subtract))
        nc.vector.tensor_tensor(lay[:, :, V_NLAM], lam_s[:, 0], const[:, C_LI:C_LI + DEPTH],
                                ALU.subtract)
        boot(nc.vector.tensor_tensor(lay[:, :, V_SUBG], lay[:, :, V_SUB],
                                     const[:, C_1LI:C_1LI + DEPTH], ALU.mult))
        for q in range(2):
            for k in range(KD):
                src = boot_wm[4 * q + k // 2][:, k % 2]
                dve.wait_ge(boot_in[4 * q + k // 2], 16)
                if k == 0:
                    ins = nc.vector.tensor_scalar(macc[q][:], src, c_act[:, k:k + 1], None, ALU.mult)
                else:
                    dve.wait_ge(wm_used, 8 * q + k + CREDIT)
                    ins = nc.vector.scalar_tensor_tensor(macc[q][:], src, c_act[:, k:k + 1],
                                                         macc[q][:], ALU.mult, ALU.add)
                ins.then_inc(wm_used, 1)
            if q == 0:
                for k in range(KD):
                    dve.wait_ge(tr_done, 3 + k)
                    nc.vector.tensor_copy(x_t[:, k], ps[k % 4][:]).then_inc(x_done, 1)
        for q in range(2):
            module_out(0, q, lay[:, 0])

        chain = [0]

        def link(l, ins):
            chain[0] += 1
            ins.then_inc(dve_step, 1)
            dve.wait_ge(dve_step, CHAIN * l + chain[0])

        def mark(ins):
            chain[0] += 1
            ins.then_inc(dve_step, 1)
            return chain[0]

        def need(l, number):
            dve.wait_ge(dve_step, CHAIN * l + number)

        def rope(l, u):
            kind, dst = UNITS[u][1:]
            r = ROPED.index(u)
            if u in MOVED:
                dve.wait_ge(swap_done, N_M * l + MOVED.index(u) + 1)
            if kind == "turn":
                nc.vector.tensor_copy(dst, ps[6 + r % 2][:].rearrange("p (t n) -> p t n", n=P)
                                      ).then_inc(rope_done, 1)
                return
            t = 2 if kind == "i32" else 0
            dve.wait_ge(unit_out, N_U * l + u + 1)
            nc.vector.tensor_tensor(t_cos[r % 2][:], q_raw[r % 2][:], rot[:, t], ALU.mult)
            swapped = ps[6 + r % 2][:] if kind == "i32" else t_sin[r % 2][:]
            link(l, nc.vector.tensor_tensor(t_sin[r % 2][:], swapped, rot[:, t + 1], ALU.mult))
            nc.vector.tensor_tensor(dst, t_cos[r % 2][:], t_sin[r % 2][:], ALU.add
                                    ).then_inc(rope_done, 1)

        def index_score(l, x):
            b, h = IDX_ITEMS[x]
            nn = P * (b + 1)
            dst = score[:, score_at[b]:score_at[b] + nn]
            dve.wait_ge(relu_done, N_I * l + x + 1)
            w = iw[:, b, h:h + 1]
            if h:
                ins = nc.vector.scalar_tensor_tensor(dst, rel[x % 2][:, 0:nn], w, dst,
                                                     ALU.mult, ALU.add)
            else:
                ins = nc.vector.tensor_scalar(dst, rel[x % 2][:, 0:nn], w, 0.0, ALU.mult, ALU.add)
            ins.then_inc(idx_acc, 1)
            dve.wait_ge(idx_acc, N_I * l + x + 1)
            if h == 3:
                link(l, nc.vector.memset(score[0:64, score_at[b] + nn - 64:score_at[b] + nn], -BIG))

        def topk(l, b, r0, r1, between=None):
            nn = P * (b + 1)
            work = score[:, score_at[b]:score_at[b] + nn]
            for r in range(r0, r1):
                if between is None:
                    fence(dve)
                    link(l, nc.vector.max(top8[:], work))
                    fence(dve)
                    link(l, nc.vector.match_replace(work, top8[:], work, -3e38))
                else:
                    number = mark(nc.vector.max(top8[:], work))
                    between()
                    need(l, number)
                    fence(dve)
                    number = mark(nc.vector.match_replace(work, top8[:], work, -3e38))
            if r1 == TK:
                if between is not None:
                    need(l, number)
                nc.vector.tensor_scalar(sel_bf[:, score_at[b]:score_at[b] + nn], work, -2e38, -BIG,
                                        ALU.is_gt, ALU.mult).then_inc(sel_done, 1)
            return None if between is None else number

        def mixer_projections(l):
            def outs(n, last):
                for u in [u for u in range(N_U) if UNITS[u][0] == n][slice(1, 9) if last else slice(1)]:
                    if u in ROPED:
                        rope(l, u)
                    for x in IDX_AFTER.get(u, ()):
                        index_score(l, x)

            for n in range(MIX_BLOCKS):
                split_lo(l, MIX_0 + n + 1)
                outs(n - 1, True)
                if n == 2:
                    dve.wait_ge(iw_turned, l + 1)
                    nc.vector.tensor_copy(iw[:], ps[5][:, 0:NT * 4].rearrange("p (t n) -> p t n", n=4)
                                          ).then_inc(iw_done, 1)
                    dve.wait_ge(kv_act, 2 * l + 2)
                    link(l, nc.vector.reciprocal(rel[1][:], rel[1][:]))
                    nc.vector.scalar_tensor_tensor(kv_raw[:], kv_raw[:], cur[:, V_KV:V_KV + 1],
                                                   rel[1][:], ALU.mult, ALU.mult).then_inc(kvn_done, 1)
                    dve.wait_ge(iw_done, l + 1)
                    fence(dve)
                if n == 4:
                    dve.wait_ge(kvn_hi_done, l + 1)
                    nc.vector.tensor_tensor(kvn_lo[:], kv_raw[:], kvn_hi[:].bitcast(F32),
                                            ALU.subtract).then_inc(kvn_lo_done, 1)
                for part in TOPK_PLAN.get(n, []):
                    topk(l, *part)
                outs(n, False)
            outs(MIX_BLOCKS - 1, True)

        def maxima(l, it):
            b, fam, _, _, _ = ITEMS[it]
            nn = keys_of(b, fam)[1]
            par = b % 2
            for su, maps in banks_of(it):
                c, n = stat(fam, maps[0]), len(maps)
                neg = stats_n[:, par, c:c + 2 * n - 1:2]
                dve.wait_ge(sc_done, N_SU * l + su + 1)
                ins = nc.vector.tensor_reduce(neg, ps[su % 4][:, 0:n * nn].rearrange(
                    "p (m k) -> p m k", m=n), AX.X, ALU.max, negate=True)
                if fam == "A":
                    link(l, ins)
                    ins = nc.vector.tensor_tensor(neg, neg, cur[:, V_NSINK + c:V_NSINK + c + 2 * n - 1:2],
                                                  ALU.min)
                ins.then_inc(max_done, 1)

        def sinks(l, b):
            dve.wait_ge(max_done, N_SU * l + max(su for su, _ in banks_of(items_through(b, "A") - 1)) + 1)
            nc.vector.tensor_tensor(stats_x[:, b % 2], cur[:, V_SINK:V_SINK + 4],
                                    stats_n[:, b % 2, 0:4], ALU.add).then_inc(sink_in, 1)

        def combine(l, it):
            b, fam, maps, per, su0 = ITEMS[it]
            nn = keys_of(b, fam)[1]
            heads = heads_of(it)
            c, end = stat(fam, maps[0]), stat(fam, maps[-1]) + 1
            sums = stats_s[:, b % 2]
            dve.wait_ge(exp_done, N_SU * l + banks_of(it)[-1][0] + 1)
            link(l, nc.vector.reciprocal(stats_r[:, c:end:2], sums[:, c + 1:end:2]))
            link(l, nc.vector.scalar_tensor_tensor(stats_r[:, c + 1:end:2], stats_r[:, c:end:2],
                                                   cur[:, V_NLAM:V_NLAM + 1], sums[:, c:end:2],
                                                   ALU.mult, ALU.mult))
            for n in range(len(heads)):
                e0, e1 = (e_buf[(su0 + j) % 6][:, n * nn:(n + 1) * nn] for j in range(2))
                ins = nc.vector.scalar_tensor_tensor(e0, e1, stats_r[:, c + 2 * n + 1:c + 2 * n + 2],
                                                     e0, ALU.mult, ALU.add)
            ins.then_inc(comb_done, 1)

        def y_ab_out(l, b):
            par = b % 2
            dve.wait_ge(pv_done, N_IT * l + items_through(b, "B"))
            dve.wait_ge(sink_done, NT * l + b + 1)
            nc.vector.tensor_tensor(stats_f[:, 0:4], stats_s[:, par, 0:4], stats_e[:, par], ALU.add)
            link(l, nc.vector.tensor_copy(stats_f[:, 4:8], stats_s[:, par, 4:8]))
            link(l, nc.vector.reciprocal(stats_f[:, 0:8], stats_f[:, 0:8]))
            nc.vector.tensor_tensor(y_ab[:, b].rearrange("p (h e) -> p h e", h=8),
                                    ps[4][:].rearrange("p (h e) -> p h e", h=8),
                                    stats_f[:, 0:8].unsqueeze(2).broadcast_to([P, 8, HD]), ALU.mult
                                    ).then_inc(y_out, 1)

        def y_c_out(l, b):
            dve.wait_ge(pv_done, N_IT * l + items_through(b, "C"))
            link(l, nc.vector.reciprocal(stats_f[:, 8:12], stats_s[:, b % 2, 8:16:2]))
            nc.vector.tensor_tensor(y_c[:, b].rearrange("p (h e) -> p h e", h=4),
                                    ps[5][:].rearrange("p (h e) -> p h e", h=4),
                                    stats_f[:, 8:12].unsqueeze(2).broadcast_to([P, 4, P]), ALU.mult
                                    ).then_inc(y_out, 1)
            dve.wait_ge(y_out, 2 * NT * l + 2 * b + 2)
            link(l, nc.vector.tensor_tensor(c_sq[:], y_c[:, b], y_c[:, b], ALU.mult))
            ins = nc.vector.tensor_reduce(c_ss[:, 4 * b:4 * b + 4],
                                          c_sq[:].rearrange("p (h e) -> p h e", h=4), AX.X, ALU.add)
            if b == NT - 1:
                ins.then_inc(css_done, 1)

        def norm_c(l):
            dve.wait_ge(csd_done, l + 1)
            link(l, nc.vector.reciprocal(c_rs[:], c_rs[:]))
            for b in range(NT):
                yb = y_c[:, b].rearrange("p (h e) -> p h e", h=4)
                nc.vector.tensor_tensor(yb, yb, c_rs[:, 4 * b:4 * b + 4].unsqueeze(2)
                                        .broadcast_to([P, 4, P]), ALU.mult).then_inc(cn_done, 1)

        def attention(l):
            for it in range(N_IT + 4):
                b, fam = ITEMS[min(it, N_IT - 1)][:2]

                def now():
                    if it < N_IT:
                        maxima(l, it)
                        if it + 1 == items_through(b, "A"):
                            sinks(l, b)
                    if 1 <= it <= N_IT and ITEMS[it - 1][1] == "C":
                        combine(l, it - 1)

                if it in LATE_ROUNDS:
                    if it - 1 in LATE_ROUNDS:
                        need(l, last)
                        fence(dve)
                    kt, rnd = LATE_ROUNDS[it]
                    last = topk(l, kt, rnd, rnd + 1, now)
                else:
                    now()
                for t in range(NT):
                    if it == items_through(t, "B") + 3:
                        y_ab_out(l, t)
                    if it == items_through(t, "C") + 3:
                        y_c_out(l, t)
            for n in range(2 * NT):
                b, c = n % NT, n // NT
                if n == NT:
                    norm_c(l)
                dve.wait_ge(yhi_done, 2 * NT * l + n + 1)
                hi, lo = (h[:, 4 * c:4 * c + 4, b * P:(b + 1) * P] for h in (h_hi, h_lo))
                src = ps[n][:].rearrange("p (t s) -> p t s", s=P)
                if c:
                    for t in range(4):
                        ins = nc.vector.scalar_tensor_tensor(lo[:, t], src[:, t],
                                                             cur[:, V_SUBG:V_SUBG + 1],
                                                             hi[:, t].bitcast(F32),
                                                             ALU.mult, ALU.subtract)
                else:
                    ins = nc.vector.tensor_tensor(lo, src, hi.bitcast(F32), ALU.subtract)
                ins.then_inc(ylo_done, 1)

        dve.wait_ge(start_act, 8)
        with dve.Fori(0, DEPTH) as l:
            nc.vector.tensor_copy(cur[:], at_col(lay, l)).then_inc(cur_done, 1)
            dve.wait_ge(cur_done, l + 1)
            split_lo(l, 0)
            norm(l, 0)
            ffn(l, 0)
            norm(l, 1)
            mixer_projections(l)
            attention(l)
            assert chain[0] == CHAIN, chain

            def out_step(i, p, prepared):
                split_lo(l, prepared, i)
                x_update(used(l, OUT_0 + p) + 2 * i, p, 2 * i + p, 1)

            run_segment(dve, OUT_0, KD // 2, out_step)
            norm(l, 2)
            ffn(l, 1)

        dve.wait_ge(sq_done, KD * (NORMS * DEPTH + 1))
        for k in range(KD):
            nc.vector.tensor_scalar(x_t[:, k], x_t[:, k], lay[:, 0, V_FIN + k:V_FIN + k + 1], None,
                                    ALU.mult).then_inc(fin_done, 1)
        dve.wait_ge(sd_done, NORMS * DEPTH + 1)
        nc.vector.reciprocal(rstd[:], sd[:]).then_inc(rstd_done, 1)
        dve.wait_ge(rstd_done, NORMS * DEPTH + 1)
        for n in range(1, 2 * NT, 2):
            dve.wait_ge(ftr_done, n + 1)
            nc.vector.tensor_scalar(out_nat[:, n // 2, S:2 * S], ps[n % 4][:],
                                    rstd[:, n // 2:n // 2 + 1], None, ALU.mult).then_inc(fout_b, 1)

    @block.gpsimd
    def _(pool):
        with pool.Fori(0, NORMS * DEPTH + 1) as v:
            for k in range(KD - 1):
                pool.wait_ge(sq_done, KD * v + k + 1)
                fence(pool)
                if k == 0:
                    ins = nc.gpsimd.tensor_copy(sq_sum[:], sq[0][:])
                else:
                    pool.wait_ge(sq_added, (KD - 1) * v + k)
                    fence(pool)
                    ins = nc.gpsimd.tensor_tensor(sq_sum[:], sq_sum[:], sq[k % 2][:], ALU.add)
                ins.then_inc(sq_added, 1)

    @block.tensor
    def _(pe):
        def product(dst, w, h, first, last):
            nc.tensor.matmul(dst, w[0], h[1], start=first, stop=False, skip_group_check=True)
            nc.tensor.matmul(dst, w[1], h[0], start=False, stop=False, skip_group_check=True)
            return nc.tensor.matmul(dst, w[0], h[0], start=False, stop=last, skip_group_check=True)

        def sum_squares(v):
            pe.wait_ge(sq_added, (KD - 1) * (v + 1))
            pe.wait_ge(sq_done, KD * (v + 1))
            for t in range(NT):
                for src in (sq_sum, sq[(KD - 1) % 2]):
                    ins = nc.tensor.matmul(ps[SUM][:, t:t + 1], src[:, t * P:(t + 1) * P],
                                           ones[:, 0:1], start=src is sq_sum,
                                           stop=src is not sq_sum)
            ins.then_inc(sum_done, 1)

        def spread(v):
            for t in range(NT):
                pe.wait_ge(diag_done, NT * v + t + 1)
                ins = nc.tensor.matmul(ps[SUM][:, t * P:(t + 1) * P], ones, diag[:, t],
                                       start=True, stop=True)
            ins.then_inc(spread_done, 1)

        def module_sum(l, q):
            pe.wait_ge(wm_used, 72 * l + 8 * q + 8 + CREDIT)
            par = q % N_MOD % 2
            for t in range(KD):
                ins = nc.tensor.matmul(ps[MISC[par]][:, t:t + 1],
                                       macc[par][:, t * P:(t + 1) * P], ones[:, 0:1],
                                       start=True, stop=True)
            ins.then_inc(mod_sum, 1)

        def ffn(l, which):
            for kind, half, pairs, module, s0, step, f0 in walk(which):
                nf = HALVES[half][1]
                v = NORMS * l + 2 * which

                def body(i, p):
                    pe.wait_ge(lo_done, BLOCKS * l + s0 + p + 2 * i + 1 + CREDIT)
                    if kind == "in":
                        w = [wb[p][:].rearrange("p (k g f) -> p k g f", k=KD, g=2)
                             for wb in (w_hi, w_lo)]
                        for k in range(KD):
                            if half == 0 and step == 0 and p == 0:
                                pe.wait_ge(hlo_done, KD * v + k + 1)
                            for g in range(2):
                                ins = product(ps[2 * p + g][:], [t[:, k, g] for t in w],
                                              (h_hi[:, k], h_lo[:, k]), k == 0, k == KD - 1)
                    else:
                        w = [wb[p][:, 0:nf * P].rearrange("p (f n) -> p f n", n=P)
                             for wb in (w_hi, w_lo)]
                        for f in range(nf):
                            if f in (0, nf - 1):
                                pe.wait_ge(alo_done, 2 * F_TILES * l + f0 - (1 if f == 0 else 0))
                            ins = product(ps[2 * p][:], [t[:, f] for t in w],
                                          (a_hi[:, f], a_lo[:, f]), f == 0, f == nf - 1)
                    ins.then_inc(blk_done, 1)

                with pe.Fori(0, pairs) as i:
                    for p in range(2):
                        body(i, p)
                if module is not None:
                    module_sum(l, module)
            sum_squares(NORMS * l + 1 + 2 * which)

        pe.sem_inc(blk_done, CREDIT)
        pe.wait_ge(const_in, 16)
        pe.wait_ge(vec_in, 16 * VEC_DMAS)
        for l in range(DEPTH):
            nc.tensor.transpose(ps[6 + l][:, 0:N_VEC], vec_rows[0:N_VEC, l],
                                ident[0:N_VEC, 0:N_VEC]).then_inc(tr_done, 1)
        pe.wait_ge(x_in, 16 * 2)
        for k in range(KD):
            if k >= 4:
                pe.wait_ge(x_done, k - 3)
            for t in range(NT):
                ins = nc.tensor.transpose(ps[k % 4][:, t * P:(t + 1) * P],
                                          x_nat[:, t, k * P:(k + 1) * P], ident)
            ins.then_inc(tr_done, 1)
        module_sum(0, 0)
        sum_squares(0)
        module_sum(0, 1)

        def swap(l, u):
            r = ROPED.index(u)
            pe.wait_ge(unit_out, N_U * l + u + 1)
            if r >= 2:
                pe.wait_ge(rope_done, N_R * l + r - 1)
            if UNITS[u][1] == "i32":
                ins = nc.tensor.matmul(ps[6 + r % 2][:], const[:, C_P32:C_P32 + P], q_raw[r % 2][:],
                                       start=True, stop=True)
            else:
                for t in range(NT):
                    ins = nc.tensor.transpose(ps[6 + r % 2][:, t * P:(t + 1) * P],
                                              q_raw[r % 2][:, t * P:(t + 1) * P], ident)
            ins.then_inc(swap_done, 1)
            if u == UNIT_IK:
                for t in range(NT):
                    ins = nc.tensor.transpose(ps[5][:, 4 * t:4 * t + 4],
                                              iw_raw[96:100, t * P:(t + 1) * P],
                                              ident[96:100, 96:100])
                ins.then_inc(iw_turned, 1)

        def project(l, u):
            n, kind, dst = UNITS[u]
            p = n % 2
            bank = ps[u % 4]
            if u >= 4:
                pe.wait_ge(unit_out, N_U * l + u - 3)
            first = u == 0 or UNITS[u - 1][0] != n
            if n == KV_UP:
                pe.wait_ge(kvn_lo_done, l + 1)
                if kind == "k64":
                    ins = product(bank[:], (w_hi[p][:, 0:P], w_lo[p][:, 0:P]),
                                  (kvn_hi[:], kvn_lo[:]), True, True)
                else:
                    for t in range(NT):
                        tok = slice(t * P, (t + 1) * P)
                        ins = product(bank[:, t * HD:(t + 1) * HD],
                                      (kvn_hi[:, tok], kvn_lo[:, tok]),
                                      (w_hi[p][:, P:P + HD], w_lo[p][:, P:P + HD]), True, True)
            else:
                cols = 100 if n == INDEX_KEYS else 256
                w = [wb[p][:, 0:KD * cols].rearrange("p (k n) -> p k n", n=cols)
                     for wb in (w_hi, w_lo)]
                c0, width = 0 if first else P, min(cols, P)
                for k in range(KD):
                    if u == 0:
                        pe.wait_ge(hlo_done, KD * (NORMS * l + 1) + k + 1)
                    ins = product(bank[0:width, :], [x[:, k, c0:c0 + width] for x in w],
                                  (h_hi[:, k], h_lo[:, k]), k == 0, k == KD - 1)
            ins.then_inc(unit_done, 1)
            return ins

        def mixer_projections(l):
            raw = None
            pe.wait_ge(mod_out, N_MOD * l + 8)
            for n in range(MIX_BLOCKS):
                pe.wait_ge(lo_done, BLOCKS * l + MIX_0 + n + 1 + CREDIT)
                for u in range(N_U):
                    if UNITS[u][0] != n:
                        continue
                    project(l, u)
                    if u == 1:
                        pe.wait_ge(kv_act, 2 * l + 1)
                        nc.tensor.matmul(ps[SUM][:], ones, rel[0][:], start=True, stop=True
                                         ).then_inc(kv_sum, 1)
                    if raw is not None:
                        swap(l, raw)
                    raw = u if u in MOVED else None
                    for x in IDX_AFTER.get(u, ()):
                        b, h = IDX_ITEMS[x]
                        if x == 0:
                            pe.wait_ge(rope_done, N_R * l + 2)
                            pe.wait_ge(kv_act, 2 * l + 2)
                            pe.wait_ge(iw_done, l + 1)
                        if x >= 2:
                            pe.wait_ge(relu_done, N_I * l + x - 1)
                        rows = slice(IDX * h, IDX * h + IDX)
                        nc.tensor.matmul(ps[4 + x % 2][:, 0:P * (b + 1)], iq[rows, b * P:(b + 1) * P],
                                         ik[rows, 0:P * (b + 1)], start=True, stop=True
                                         ).then_inc(idx_done, 1)
            swap(l, raw)

        def logits(l, it):
            b, fam, _, _, _ = ITEMS[it]
            k0, nn = keys_of(b, fam)
            tok = slice(b * P, (b + 1) * P)
            for su, maps in banks_of(it):
                if su >= 4:
                    pe.wait_ge(exp_done, N_SU * l + su - 3)
                for n, (h, j) in enumerate(maps):
                    half = j if fam == "C" else h % 2
                    rows = slice(64 * half, 64 * half + 64)
                    if fam == "A":
                        q, k = aq[rows, h // 2, tok], (ak if h // 2 == half else akx)[rows, k0:k0 + nn]
                    elif fam == "B":
                        q, k = bq[rows, h // 2, tok], bk[rows, k0:k0 + nn]
                    else:
                        q, k = cq[rows, h, tok], ck[rows, h, k0:k0 + nn]
                    bank = ps[su % 4][:, n * nn:(n + 1) * nn]
                    nc.tensor.matmul(bank, q, k, start=True, stop=False, skip_group_check=True)
                    if fam == "A" and b:
                        cols, mask = slice(0, nn), mask_bf[:]
                    elif fam == "B" and b:
                        if h == 0:
                            pe.wait_ge(sel_done, 3 * l + SEL_ORDER.index(b) + 1)
                        cols, mask = slice(0, nn), sel_bf[:, score_at[b]:score_at[b] + nn]
                    else:
                        cols, mask = slice(nn - 64, nn), mask_bf[:, 192:256]
                    ins = nc.tensor.matmul(bank[:, cols], id_bf[:], mask, start=False, stop=True,
                                           skip_group_check=True)
                ins.then_inc(sc_done, 1)

        def turn_over(l, it):
            b, fam, _, per, su = ITEMS[it]
            nn = keys_of(b, fam)[1]
            if fam == "C":
                before = sum(item[1] == "C" for item in ITEMS[:it])
                pe.wait_ge(comb_done, N_C * l + before + 1)
            else:
                pe.wait_ge(exp_done, N_SU * l + su + 1)
            if it >= 2:
                pe.wait_ge(pt_done, N_IT * l + it - 1)
            for n in range(len(heads_of(it))):
                for j in range(nn // P):
                    ins = nc.tensor.transpose(ps[6 + it % 2][:, n * nn + j * P:n * nn + (j + 1) * P],
                                              e_buf[su % 6][:, n * nn + j * P:n * nn + (j + 1) * P], ident)
            ins.then_inc(pt_psum, 1)

        def weigh(l, it):
            b, fam, _, _, _ = ITEMS[it]
            k0, nn = keys_of(b, fam)
            pe.wait_ge(pt_done, N_IT * l + it + 1)
            if b and it == items_through(b - 1, "C"):
                pe.wait_ge(y_out, 2 * NT * l + 2 * (b - 1) + 1)
            if b and it == items_through(b, "B"):
                pe.wait_ge(y_out, 2 * NT * l + 2 * (b - 1) + 2)
            for n, h in enumerate(heads_of(it)):
                for j in range(nn // P):
                    t = k0 // P + j
                    if fam == "A":
                        dst, v = ps[4][:, h * HD:(h + 1) * HD], av[:, t, (h // 2) * HD:(h // 2 + 1) * HD]
                    elif fam == "B":
                        dst, v = ps[4][:, (4 + h) * HD:(5 + h) * HD], bv[:, t]
                    else:
                        dst, v = ps[5][:, h * P:(h + 1) * P], cv[:, t, h * P:(h + 1) * P]
                    ins = nc.tensor.matmul(dst, p_t[it % 2][:, n * nn + j * P:n * nn + (j + 1) * P],
                                           v, start=(j == 0), stop=(j == nn // P - 1),
                                           skip_group_check=True)
            ins.then_inc(pv_done, 1)

        def attention(l):
            pe.wait_ge(unit_out, N_U * (l + 1))
            pe.wait_ge(rope_done, N_R * (l + 1))
            pe.wait_ge(akx_done, 2 * l + 2)
            pe.wait_ge(relu_done, N_I * (l + 1))
            for it in range(N_IT + 3):
                if it < N_IT:
                    logits(l, it)
                if 2 <= it < N_IT + 2:
                    turn_over(l, it - 2)
                if it >= 3:
                    weigh(l, it - 3)
            for n in range(2 * NT):
                b, c = n % NT, n // NT
                if n == 0:
                    pe.wait_ge(y_out, 2 * NT * (l + 1) - 1)
                    pe.wait_ge(exp_done, N_SU * (l + 1))
                if c:
                    pe.wait_ge(cn_done, NT * l + b + 1)
                src = y_c if c else y_ab
                for t in range(4):
                    ins = nc.tensor.transpose(ps[n][:, t * P:(t + 1) * P],
                                              src[:, b, t * P:(t + 1) * P], ident)
                ins.then_inc(yt_done, 1)

        def output_projection(l):
            def body(i, p):
                pe.wait_ge(lo_done, BLOCKS * l + OUT_0 + p + 2 * i + 1 + CREDIT)
                w = [wb[p][:, 0:KD * P].rearrange("p (k n) -> p k n", n=P) for wb in (w_hi, w_lo)]
                for k in range(KD):
                    ins = product(ps[2 * p][:], [t[:, k] for t in w], (h_hi[:, k], h_lo[:, k]),
                                  k == 0, k == KD - 1)
                ins.then_inc(blk_done, 1)

            pe.wait_ge(ylo_done, 2 * NT * (l + 1))
            fence(pe)
            with pe.Fori(0, KD // 2) as i:
                for p in range(2):
                    body(i, p)
            sum_squares(NORMS * l + 2)

        with pe.Fori(0, DEPTH) as l:
            spread(NORMS * l)
            ffn(l, 0)
            spread(NORMS * l + 1)
            mixer_projections(l)
            attention(l)
            output_projection(l)
            spread(NORMS * l + 2)
            ffn(l, 1)

        for n in range(2 * NT):
            t, g = n // 2, n % 2
            pe.wait_ge(fin_done, 4 * g + 4 if t == 0 else KD)
            if n >= 4:
                pe.wait_ge(fout_b if g else fout_a, n // 2 - 1)
            for j in range(4):
                ins = nc.tensor.transpose(ps[n % 4][:, j * P:(j + 1) * P],
                                          x_t[:, 4 * g + j, t * P:(t + 1) * P], ident)
            ins.then_inc(ftr_done, 1)

    ctx.close()


INPUTS = ["x", "c", "positions", "w_mod", "b_mod", "norm_ffn1", "w_ffn1_in", "w_ffn1_out", "norm_mix",
          "w_in", "a_sinks", "b_kv_norm", "w_kv_up", "c_lambda_q1", "c_lambda_k1", "c_lambda_q2",
          "c_lambda_k2", "c_subln", "w_out", "norm_ffn2", "w_ffn2_in", "w_ffn2_out", "final_norm"]


def kernel(**inputs):
    import concourse.bacc as bacc
    from concourse.bass_utils import run_bass_kernel_spmd

    nc = bacc.Bacc("TRN2", target_bir_lowering=False, num_devices=1)
    arrays = {f"in_{name}": np.ascontiguousarray(inputs[name]) for name in INPUTS}
    arrays["in_consts"] = constants()
    a = {name[3:]: nc.dram_tensor(name, v.shape, mybir.dt.from_np(v.dtype), kind="ExternalInput").ap()
         for name, v in arrays.items()}
    out = nc.dram_tensor("out", (1, S, D), F32, kind="ExternalOutput").ap()
    trunk(nc, a, out)
    r = run_bass_kernel_spmd(nc, [arrays], core_ids=[0])
    return r.results[0]["out"]
```

```python
import math
from contextlib import ExitStack

import numpy as np
import concourse.bass as bass
from concourse import mybir
from concourse.alu_op_type import AluOpType as ALU

F32 = mybir.dt.float32
F32R = mybir.dt.float32r
BF16 = mybir.dt.bfloat16
I32 = mybir.dt.int32
ACT = mybir.ActivationFunctionType
AX = mybir.AxisListType

P = 128
S, D, DEPTH = 512, 1024, 2
KD = D // P
NT = S // P
D_FF = 2816
N_MOD = 9
HALVES = ((0, 12), (12, 10))
HD, CH, IDX = 64, 64, 32
TOPK = min(256, S // 4)
EPS = 1e-6
BIG = 1e30

A_Q, A_K, A_V, B_Q, B_KV, I_Q, I_K, I_W, C_Q, C_K, C_V, D_IN = (
    0, 256, 384, 512, 768, 896, 1024, 1056, 1060, 1572, 2084, 2596)

FFN_BLOCKS = sum(n for _, n in HALVES) + KD * len(HALVES)
MIX_BLOCKS = 12
FFN1_0 = 0
MIX_0 = FFN_BLOCKS
OUT_0 = MIX_0 + MIX_BLOCKS
FFN2_0 = OUT_0 + KD
BLOCKS = FFN2_0 + FFN_BLOCKS
F_TILES = D_FF // P
CREDIT = 2

C_ID, C_P32, C_ONE, C_MASK, C_INV, C_EPS, C_HPI, C_LI, C_1LI = (
    0, 128, 256, 384, 640, 642, 643, 644, 646)
N_CONST = 648
V_B, V_N1, V_NM, V_N2, V_FIN, V_KV, V_SUB, V_C = 0, 72, 80, 88, 96, 104, 105, 106
N_VEC = 114
V_SINK, V_NSINK, V_NLAM, V_SUBG, N_LAY = 114, 118, 122, 123, 124

TWO_PI = 2 * math.pi
PI_A = 6.28125
PI_B = float(np.float32(np.round((TWO_PI - PI_A) * 2 ** 17) / 2 ** 17))
PI_C = float(np.float32(TWO_PI - PI_A - PI_B))
ROUND = 12582912.0
PI_LO = 3.1415925


def constants():
    c = np.zeros((P, N_CONST), np.float32)
    c[:, C_ID:C_ID + P] = np.eye(P)
    half = IDX // 2
    for m in range(P):
        low = m % IDX < half
        c[m + half if low else m - half, C_P32 + m] = -1.0 if low else 1.0
    c[:, C_ONE:C_ONE + P] = 1.0
    c[:, C_MASK:C_MASK + 64] = -BIG
    c[64:, C_MASK + 64:C_MASK + 128] = -BIG
    c[:64, C_MASK + 192:C_MASK + 256] = -BIG
    for n, dim in enumerate((HD, IDX)):
        inv = (10000.0 ** (-np.arange(0, dim, 2, dtype=np.float64) / dim)).astype(np.float32)
        c[:, C_INV + n] = np.tile(inv, P // (dim // 2))
    c[:, C_EPS] = EPS
    c[:, C_HPI] = math.pi / 2
    for l in range(DEPTH):
        li = 0.8 - 0.6 * math.exp(-0.3 * l)
        c[:, C_LI + l] = li
        c[:, C_1LI + l] = 1.0 - li
    return c


def trunk(nc, a, out):
    ctx = ExitStack()
    base = nc.sbuf_base
    top = [(base + 63) // 64 * 64]

    def place(name, shape, dt, at=None):
        n = int(np.prod(shape[1:])) * (2 if dt == BF16 else 4)
        where = top[0] if at is None else at
        if at is None:
            top[0] += (n + 31) // 32 * 32
        return nc.alloc_sbuf_tensor_at(name, list(shape), dt, offset=where), where

    def sb(name, shape, dt=F32, at=None):
        return place(name, shape, dt, at)[0]

    x_t = sb("x_t", [P, KD, S])
    h_at = top[0]
    h_hi = sb("h_hi", [P, KD, S], F32R)
    h_lo = sb("h_lo", [P, KD, S], F32R)
    region = top[0]
    nf_max = HALVES[0][1]
    a_hi = sb("a_hi", [P, nf_max, S], F32R)
    a_lo = sb("a_lo", [P, nf_max, S], F32R)
    region_end = top[0]
    w_raw = [sb(f"w_raw{p}", [P, 2048]) for p in range(2)]
    w_at = [top[0] + 4 * 2048 * n for n in range(4)]
    w_hi = [sb(f"w_hi{p}", [P, 2048], F32R) for p in range(2)]
    w_lo = [sb(f"w_lo{p}", [P, 2048], F32R) for p in range(2)]
    rot = sb("rot", [P, 4, S])
    wm = [sb(f"wm{p}", [P, D]) for p in range(2)]
    macc_at = top[0]
    macc = [sb(f"macc{p}", [P, D]) for p in range(2)]
    const = sb("const", [P, N_CONST])
    id_bf = sb("id_bf", [P, P], BF16)
    mask_bf = sb("mask_bf", [P, 256], BF16)
    lay = sb("lay", [P, DEPTH, N_LAY])
    cur = sb("cur", [P, N_LAY])
    c_act = sb("c_act", [P, KD])
    modc = sb("modc", [P, N_MOD, KD])
    coef = sb("coef", [P, 3, KD])
    gate = sb("gate", [P, 3, KD])
    scrap = sb("scrap", [P, 2])
    temps = top[0]
    sil = [sb(f"sil{p}", [P, S]) for p in range(2)]
    a_f = [sb(f"a_f{p}", [P, S]) for p in range(2)]
    sq = [sb(f"sq{p}", [P, S]) for p in range(2)]
    sq_sum = sb("sq_sum", [P, S])
    sd = sb("sd", [P, NT])
    rstd = sb("rstd", [P, NT])
    diag = sb("diag", [P, NT, P])
    xn = [sb(f"xn{p}", [P, S]) for p in range(3)]
    temps_end = top[0]

    top[0] = region
    aq = sb("aq", [P, 2, S])
    ak = sb("ak", [P, S])
    akx = sb("akx", [P, S])
    bq = sb("bq", [P, 2, S])
    bk = sb("bk", [P, S])
    iq = sb("iq", [P, S])
    ik = sb("ik", [P, S])
    cq = sb("cq", [P, 4, S])
    ck = sb("ck", [P, 4, S])
    cv = sb("cv", [P, NT, S])
    av = sb("av", [P, NT, P])
    bv = sb("bv", [P, NT, HD])
    iw = sb("iw", [P, NT, 4])
    assert top[0] <= region_end
    top[0] = temps
    q_raw = [sb(f"q_raw{p}", [P, S]) for p in range(2)]
    t_cos = [sb(f"t_cos{p}", [P, S]) for p in range(2)]
    t_sin = [sb(f"t_sin{p}", [P, S]) for p in range(2)]
    kv_raw = sb("kv_raw", [P, S])
    kvn_hi = sb("kvn_hi", [P, S], F32R)
    kvn_lo = sb("kvn_lo", [P, S], F32R)
    rel = [sb(f"rel{p}", [P, S]) for p in range(2)]
    mix_proj_end = top[0]
    score_at = [0, 0, 256, 640]
    score = sb("score", [P, 1152])
    iw_raw = score
    sel_bf = sb("sel_bf", [P, 1152], BF16)
    top8 = sb("top8", [P, 8])
    stats_n = sb("stats_n", [P, 2, 16])
    stats_s = sb("stats_s", [P, 2, 16])
    stats_x = sb("stats_x", [P, 2, 4])
    stats_e = sb("stats_e", [P, 2, 4])
    stats_r = sb("stats_r", [P, 16])
    stats_f = sb("stats_f", [P, 16])
    c_ss = sb("c_ss", [P, 16])
    c_rs = sb("c_rs", [P, 16])
    mixer_top = top[0]
    top[0] = temps
    e_low = [sb(f"e_buf{p}", [P, S]) for p in range(4)]
    e_buf = [iq, ik, *e_low[2:], *e_low[:2]]
    p_t = [sb(f"p_t{p}", [P, S]) for p in range(2)]
    c_sq = sb("c_sq", [P, S])
    y_c = sb("y_c", [P, NT, S])
    assert top[0] <= mix_proj_end
    y_ab = sb("y_ab", [P, NT, S], at=macc_at)
    high = max(temps_end, mixer_top)
    assert high <= nc.sbuf_usable_end, (high, nc.sbuf_usable_end)
    top[0] = region
    x_nat = sb("x_nat", [P, NT, D])
    vec_rows = sb("vec_rows", [P, DEPTH, P])
    pos_i = sb("pos_i", [P, S], I32)
    pos_f = sb("pos_f", [P, S])
    ang = [sb(f"ang{n}", [P, S]) for n in range(2)]
    lam_v = sb("lam_v", [P, 4, DEPTH, HD])
    lam_p = sb("lam_p", [P, 2, DEPTH, HD])
    lam_s = sb("lam_s", [P, 2, DEPTH])
    boot_wm = [sb(f"boot_wm{j}", [P, 2, D], at=h_at + 8 * D * j) for j in range(4)]
    boot_wm += [sb(f"boot_wm{j}", [P, 2, D]) for j in (4, 5)]
    assert top[0] <= region_end
    boot_wm += [sb(f"boot_wm{j}", [P, 2, D], at=at) for j, at in ((6, w_at[1]), (7, w_at[3]))]
    out_nat = sb("out_nat", [P, NT, D], at=region)

    ps = [ctx.enter_context(nc.psum_tensor(f"ps{b}", [P, S], F32)) for b in range(8)]
    SUM, MISC = 4, (5, 7)

    ident = const[:, C_ID:C_ID + P]
    ones = const[:, C_ONE:C_ONE + P]

    def sem(name):
        return ctx.enter_context(nc.semaphore(name))

    const_in = sem("const_in")
    vec_in = sem("vec_in")
    boot_in = [sem(f"boot_in{j}") for j in range(KD)]
    lam_in = sem("lam_in")
    x_in = sem("x_in")
    pos_in = sem("pos_in")
    raw_in = [sem(f"raw_in{p}") for p in range(2)]
    hi_done = sem("hi_done")
    lo_done = sem("lo_done")
    blk_done = sem("blk_done")
    wm_in = [sem(f"wm_in{p}") for p in range(2)]
    wm_used = sem("wm_used")
    acc_zero = sem("acc_zero")
    mod_sum = sem("mod_sum")
    mod_out = sem("mod_out")
    silu_done = sem("silu_done")
    mul_done = sem("mul_done")
    ahi_done = sem("ahi_done")
    alo_done = sem("alo_done")
    x_done = sem("x_done")
    sq_done = sem("sq_done")
    sq_added = sem("sq_added")
    sum_done = sem("sum_done")
    sd_done = sem("sd_done")
    rstd_done = sem("rstd_done")
    diag_done = sem("diag_done")
    spread_done = sem("spread_done")
    xn_done = sem("xn_done")
    hhi_done = sem("hhi_done")
    hlo_done = sem("hlo_done")
    cur_done = sem("cur_done")
    mod_step = sem("mod_step")
    passed = sem("passed")
    tr_done = sem("tr_done")
    boot_step = sem("boot_step")
    start_act = sem("start_act")
    start_dve = sem("start_dve")
    unit_done = sem("unit_done")
    unit_out = sem("unit_out")
    swap_done = sem("swap_done")
    rope_done = sem("rope_done")
    turn_done = sem("turn_done")
    kv_act = sem("kv_act")
    kv_sum = sem("kv_sum")
    kvn_done = sem("kvn_done")
    kvn_hi_done = sem("kvn_hi_done")
    kvn_lo_done = sem("kvn_lo_done")
    akx_done = sem("akx_done")
    iw_turned = sem("iw_turned")
    iw_done = sem("iw_done")
    idx_done = sem("idx_done")
    relu_done = sem("relu_done")
    idx_acc = sem("idx_acc")
    dve_step = sem("dve_step")
    sel_done = sem("sel_done")
    sc_done = sem("sc_done")
    max_done = sem("max_done")
    exp_done = sem("exp_done")
    sink_in = sem("sink_in")
    sink_done = sem("sink_done")
    comb_done = sem("comb_done")
    pt_psum = sem("pt_psum")
    pt_done = sem("pt_done")
    pv_done = sem("pv_done")
    y_out = sem("y_out")
    css_done = sem("css_done")
    csd_done = sem("csd_done")
    cn_done = sem("cn_done")
    yt_done = sem("yt_done")
    yhi_done = sem("yhi_done")
    ylo_done = sem("ylo_done")
    fin_done = sem("fin_done")
    ftr_done = sem("ftr_done")
    fout_a = sem("fout_a")
    fout_b = sem("fout_b")
    stored = sem("stored")

    FFN1 = [("in", 0, [(2, 2), (2, 3), (2, None)]), ("out", 0, [(4, 4)]),
            ("in", 1, [(2, 5), (2, 6), (1, None)]), ("out", 1, [(2, 7), (2, None)])]
    FFN2 = [("in", 0, [(4, 8), (2, None)]), ("out", 0, [(4, 9)]),
            ("in", 1, [(4, 10), (1, None)]), ("out", 1, [(4, None)])]

    NEXT_LAYER = (N_MOD, N_MOD + 1)

    def walk(which):
        s, f = (FFN1_0, FFN2_0)[which], F_TILES * which
        for kind, half, segments in (FFN1, FFN2)[which]:
            step = 0
            for pairs, module in segments:
                yield kind, half, pairs, module, s, step, f
                s += 2 * pairs
                step += 2 * pairs
                if kind == "in":
                    f += 2 * pairs

    MIX = [(B_KV, 256), (I_K, 36), (A_Q, 256), (A_K, 256), (B_Q, 256), None,
           (C_Q, 256), (C_Q + 256, 256), (C_K, 256), (C_K + 256, 256), (C_V, 256), (C_V + 256, 256)]
    KV_UP, INDEX_KEYS = 5, 1
    UNITS = [(0, "kv", kv_raw[:]), (0, "i32", iq[:]), (1, "i32", ik[:]),
             (2, "q64", aq[:, 0]), (2, "q64", aq[:, 1]), (3, "k64", ak[:]), (3, "turn", av[:]),
             (4, "q64", bq[:, 0]), (4, "q64", bq[:, 1]), (5, "k64", bk[:]), (5, "nat", bv),
             (6, "q64", cq[:, 0]), (6, "q64", cq[:, 1]), (7, "q64", cq[:, 2]), (7, "q64", cq[:, 3]),
             (8, "k64", ck[:, 0]), (8, "k64", ck[:, 1]), (9, "k64", ck[:, 2]), (9, "k64", ck[:, 3]),
             *[(10 + h // 2, "turn", cv[:, :, h * P:(h + 1) * P]) for h in range(4)]]
    ROPED = [u for u, (_, kind, _) in enumerate(UNITS) if kind in ("i32", "q64", "k64", "turn")]
    MOVED = [u for u in ROPED if UNITS[u][1] in ("i32", "turn")]
    UNIT_IK, UNIT_AK = 2, 5
    TURNED = [u for u in ROPED if UNITS[u][1] == "turn"]
    N_U, N_M, N_T = len(UNITS), len(MOVED), len(TURNED)
    N_R = len(ROPED) - N_T

    def wait_in_place(eng, l, r):
        u = ROPED[r]
        if u in TURNED:
            eng.wait_ge(turn_done, N_T * l + TURNED.index(u) + 1)
        else:
            eng.wait_ge(rope_done, N_R * l + sum(v not in TURNED for v in ROPED[:r]) + 1)
    IDX_ITEMS = [(b, h) for b in (1, 2, 3) for h in range(4)]
    N_I = len(IDX_ITEMS)
    IDX_AFTER = {u: (2 * j, 2 * j + 1) for j, u in enumerate(range(5, 5 + N_I // 2))}
    TK = TOPK // 8
    TOPK_PLAN = {4: [(1, 0, 4)], 5: [(1, 4, 8)], 6: [(1, 8, 12)], 7: [(1, 12, 16)],
                 8: [(2, 0, 4)], 9: [(2, 4, 8)], 10: [(2, 8, 16)], 11: [(3, 0, 2)]}
    LATE_ROUNDS = {j: (3, j + 2) for j in range(TK - 2)}
    SEL_ORDER = [1, 2, 3]
    def keys_of(b, fam):
        return (max(b - 1, 0) * P, P * min(b + 1, 2)) if fam == "A" else (0, P * (b + 1))

    ITEMS = []
    N_SU = 0
    for b in range(NT):
        for fam in "ABC":
            per = S // keys_of(b, fam)[1]
            if fam != "C":
                per = min(per, 2)
            heads = range(4) if fam == "C" else (0, 2, 1, 3)
            for m in range(0, 4, per):
                maps = [(h, j) for j in range(2 if fam == "C" else 1) for h in heads[m:m + per]]
                ITEMS.append((b, fam, maps, per, N_SU))
                N_SU += len(maps) // per
    Y_BANKS = (0, 1, 2, 3, 4, 6, 7, 5)
    N_IT, N_C = len(ITEMS), sum(item[1] == "C" for item in ITEMS)

    def stat(fam, m):
        return 8 + 2 * m[0] + m[1] if fam == "C" else m[0] + (4 if fam == "B" else 0)

    def banks_of(it):
        _, _, maps, per, su = ITEMS[it]
        return [(su + n, maps[n * per:(n + 1) * per]) for n in range(len(maps) // per)]

    def heads_of(it):
        return sorted({h for h, _ in ITEMS[it][2]})

    def items_through(b, fam):
        return 1 + max(n for n, item in enumerate(ITEMS) if item[:2] == (b, fam))

    NORMS = 3
    X_TILES = 5 * KD
    VEC_DMAS = 8
    CHAIN = (N_R + 1 + 3 + 3 * 2 * TK + sum(item[1] == "A" for item in ITEMS)
             + 2 * sum(item[1] == "C" for item in ITEMS) + 2 * NT + 2 * NT + 2)

    def used(l, s):
        return (BLOCKS - MIX_BLOCKS) * l + (s if s <= MIX_0 + 1 else s - MIX_BLOCKS)

    def units_through(n):
        return sum(unit[0] <= n for unit in UNITS)

    def fence(eng):
        eng.sem_inc(passed, 1)

    def at_col(t, k):
        return t[:, bass.ds(k, 1)].rearrange("p a s -> p (a s)")

    def block_len(s):
        if MIX_0 <= s < OUT_0:
            cols = MIX[s - MIX_0]
            return KD * cols[1] if cols else P
        if OUT_0 <= s < FFN2_0:
            return KD * P
        r = s - FFN1_0 if s < MIX_0 else s - FFN2_0
        for _, nf in HALVES:
            if r < nf:
                return 2 * KD * P
            if r < nf + KD:
                return nf * P
            r -= nf + KD
        return None

    def split_views(s, p):
        if s == MIX_0 + INDEX_KEYS:
            raw = w_raw[p][:, 0:KD * 36].rearrange("p (k n) -> p k n", n=36)
            hi, lo = (w[p][:, 0:KD * 100].rearrange("p (k n) -> p k n", n=100) for w in (w_hi, w_lo))
            return [(raw[:, :, 0:n], hi[:, :, at:at + n], lo[:, :, at:at + n])
                    for at, n in ((0, IDX), (IDX, IDX), (2 * IDX, IDX + 4))]
        if s == MIX_0 + KV_UP:
            return [(w_raw[p][:, 0:64], w_hi[p][:, 0:64], w_lo[p][:, 0:64]),
                    (w_raw[p][:, 0:128], w_hi[p][:, 64:192], w_lo[p][:, 64:192])]
        n = block_len(s)
        return [(w_raw[p][:, 0:n], w_hi[p][:, 0:n], w_lo[p][:, 0:n])]

    def run_segment(eng, s0, pairs, body):
        sizes = [block_len(s0 + 1 + j) for j in range(2 * pairs)]
        whole = pairs if len(set(sizes)) == 1 and s0 + 2 * pairs not in (MIX_0, BLOCKS) else pairs - 1
        if whole:
            with eng.Fori(0, whole) as i:
                for p in range(2):
                    body(i, p, s0 + p + 1)
        if whole < pairs:
            body(pairs - 1, 0, s0 + 1)
            nxt = s0 + 2 * pairs
            body(pairs - 1, 1, None if nxt == BLOCKS else nxt - 2 * (pairs - 1))

    def chunks_of(pairs, i, p):
        if pairs == 4:
            return [(2 * i + p, p)]
        return [(4 * i + (2 * p + c), c) for c in range(2)]

    w_mod = a["w_mod"].rearrange("l (k p) n -> l p k n", p=P)

    def load_chunk(eng, source_l, l, q, k, p):
        eng.wait_ge(wm_used, KD * N_MOD * l + KD * q + k + 1)
        fence(eng)
        m = q % N_MOD
        eng.dma_start(wm[p][:], w_mod[source_l, :, bass.ds(k, 1), m * D:(m + 1) * D]
                      .rearrange("p a n -> p (a n)")).then_inc(wm_in[p], 16)

    def vec_src(name):
        return a[name].rearrange("l (r c) -> r l c", c=P)

    def load_vec(eng, row, src):
        eng.dma_start(vec_rows[row:row + src.shape[0]], src).then_inc(vec_in, 16)

    block = ctx.enter_context(nc.Block())

    @block.sync
    def _(sp):
        sp.dma_start(const[:], a["consts"]).then_inc(const_in, 16)
        load_vec(sp, V_B, vec_src("b_mod"))
        load_vec(sp, V_N1, vec_src("norm_ffn1"))
        load_vec(sp, V_FIN, a["final_norm"].rearrange("(r c) -> r c", c=P).unsqueeze(1)
                 .broadcast_to([KD, DEPTH, P]))
        for n, name in enumerate(("c_lambda_q1", "c_lambda_k1", "c_lambda_q2", "c_lambda_k2")):
            sp.dma_start(lam_v[:, n], a[name].unsqueeze(0).broadcast_to([P, DEPTH, HD])
                         ).then_inc(lam_in, 16)
        load_vec(sp, V_C, a["c"].rearrange("b (r c) -> (b r) c", c=P).unsqueeze(1)
                 .broadcast_to([KD, DEPTH, P]))
        x_rows = a["x"].rearrange("b (t p) d -> (b p) t d", p=P)
        w_in_r = a["w_in"].rearrange("l (k p) n -> l p k n", p=P)
        w_out_r = a["w_out"].rearrange("l (k p) n -> l p k n", p=P)

        def load_block(s, p, parts):
            sp.wait_ge(lo_done, s + 1)
            fence(sp)
            for dst, src in parts:
                sp.dma_start(dst, src).then_inc(raw_in[p], 16)

        def slot(p, n):
            return lambda tiles: w_raw[p][:, 0:tiles * n].rearrange("p (k n) -> p k n", n=n)

        def ffn(l, which):
            w_up, w_down = (("w_ffn1_in", "w_ffn1_out"), ("w_ffn2_in", "w_ffn2_out"))[which]
            up = a[w_up].rearrange("l (k p) (g f) -> l p k g f", p=P, g=2)
            down = a[w_down].rearrange("l (f p) n -> l p f n", p=P)
            for kind, half, pairs, module, s0, step, _ in walk(which):
                f0, nf = HALVES[half]
                with sp.Fori(0, pairs) as i:
                    for p in range(2):
                        s = BLOCKS * l + s0 + p + 2 * i
                        if kind == "in":
                            dst = w_raw[p][:].rearrange("p (k g f) -> p k g f", k=KD, g=2)
                            col = bass.ds(i * 2 * P + (f0 + step + p) * P, P)
                            load_block(s, p, [(dst[:, :, g], up[l, :, :, g, col]) for g in range(2)])
                        else:
                            dst = slot(p, P)(nf)
                            col = bass.ds(i * 2 * P + (step + p) * P, P)
                            cut = (slice(0, nf // 2), slice(nf // 2, nf))
                            load_block(s, p, [(dst[:, c], down[l, :, f0 + c.start:f0 + c.stop, col])
                                              for c in cut])

        sp.wait_ge(vec_in, 16 * VEC_DMAS)
        for q in range(2):
            for j in range(4):
                sp.dma_start(boot_wm[4 * q + j][:], w_mod[0, :, 2 * j:2 * j + 2, q * D:(q + 1) * D]
                             ).then_inc(boot_in[4 * q + j], 16)
            if q == 0:
                for t in (0, 2):
                    sp.dma_start(x_nat[:, t:t + 2], x_rows[:, t:t + 2]).then_inc(x_in, 16)
        with sp.Fori(0, DEPTH) as l:
            ffn(l, 0)
            for n, cols in enumerate(MIX):
                p = n % 2
                if cols is None:
                    parts = [(w_raw[p][:, g:g + 64], a["w_kv_up"][l, :, g:g + 64]) for g in (0, 64)]
                else:
                    dst = slot(p, cols[1])(KD)
                    parts = [(dst[:, g:g + 4], w_in_r[l, :, g:g + 4, cols[0]:sum(cols)])
                             for g in (0, 4)]
                load_block(BLOCKS * l + MIX_0 + n, p, parts)
            with sp.Fori(0, KD // 2) as i:
                for p in range(2):
                    dst = slot(p, P)(KD)
                    load_block(BLOCKS * l + OUT_0 + p + 2 * i, p,
                               [(dst[:, g:g + 4], w_out_r[l, :, g:g + 4, bass.ds(i * 2 * P + p * P, P)])
                                for g in (0, 4)])
            ffn(l, 1)

        o_rows = out.rearrange("b (t p) d -> (b p) t d", p=P)
        for t in range(NT):
            sp.wait_ge(fout_a, t + 1)
            sp.wait_ge(fout_b, t + 1)
            sp.dma_start(o_rows[:, t], out_nat[:, t]).then_inc(stored, 16)
        sp.wait_ge(stored, 16 * NT)

    @block.scalar
    def _(act):
        def split_hi(l, s, i=0):
            p = s % 2
            act.wait_ge(raw_in[p], 32 * (BLOCKS // 2) * l + 32 * (s // 2) + 32 * i + 32)
            if MIX_0 + 2 <= s <= OUT_0:
                act.wait_ge(unit_done, N_U * l + units_through(s - 2 - MIX_0))
            else:
                act.wait_ge(blk_done, used(l, s) + 2 * i + 1)
            for raw, hi, _ in split_views(s + 2 * i if isinstance(i, int) else s, p):
                ins = nc.scalar.activation(hi, raw, ACT.Copy)
            ins.then_inc(hi_done, 1)

        def square(x_n, l, m, i, j, p):
            k = 2 * i + j
            act.wait_ge(x_done, x_n + 1)
            act.wait_ge(sq_added, (KD - 1) * NORMS * l + 2 * i + ((KD - 1) * m + j - 1))
            nc.scalar.activation(sq[p][:], at_col(x_t, k), ACT.Square).then_inc(sq_done, 1)

        def root_of_mean(dst, src, n):
            return nc.scalar.activation(dst, src, ACT.Sqrt, scale=1.0 / n,
                                        bias=const[:, C_EPS:C_EPS + 1])

        def have_table(func, at):
            nc.scalar.activation(scrap[:, at:at + 1], const[:, C_EPS:C_EPS + 1], func)

        def norm(l, n):
            v = NORMS * l + n
            act.wait_ge(sum_done, v + 1)
            root_of_mean(sd[:], ps[SUM][:, 0:NT], D).then_inc(sd_done, 1)
            if n == 0:
                split_hi(l, 0)
            if n != 1:
                have_table(ACT.Silu, 0)
            act.wait_ge(mod_out, N_MOD * l + 3 * n + 2)
            for k in range(KD):
                act.wait_ge(xn_done, KD * v + k + 1)
                nc.scalar.activation(h_hi[:, k], xn[k % 3][:], ACT.Identity,
                                     bias=modc[:, 3 * n, k:k + 1]).then_inc(hhi_done, 1)

        def ffn(l, which):
            for kind, half, pairs, module, s0, step, f0 in walk(which):
                def body(i, p, prepared):
                    if prepared is not None:
                        split_hi(l, prepared, i)
                    if module is not None:
                        for k, slot in chunks_of(pairs, i, p):
                            load_chunk(act, l if module < N_MOD else 1 - l, l, module, k, slot)
                    if kind == "in":
                        f = 2 * F_TILES * l + f0 + p + 2 * i
                        act.wait_ge(blk_done, used(l, s0 + p) + 2 * i + 1 + CREDIT)
                        nc.scalar.activation(sil[p][:], ps[2 * p][:], ACT.Silu).then_inc(silu_done, 1)
                        act.wait_ge(mul_done, f + 1)
                        nc.scalar.activation(at_col(a_hi, 2 * i + (step + p)), a_f[p][:], ACT.Copy
                                             ).then_inc(ahi_done, 1)
                    elif half == 1:
                        if isinstance(i, int) and p == 1:
                            have_table(ACT.Sqrt, 1)
                        square(KD + X_TILES * l + (3 * KD * which + KD + step + p) + 2 * i, l,
                               1 + 2 * which, i, step + p, p)

                run_segment(act, s0, pairs, body)

        for row, name in ((V_NM, "norm_mix"), (V_N2, "norm_ffn2"), (V_KV, "b_kv_norm"),
                          (V_SUB, "c_subln")):
            load_vec(act, row, vec_src(name))
        act.dma_start(pos_i[:], a["positions"].broadcast_to([P, S])).then_inc(pos_in, 16)
        act.dma_start(lay[:, :, V_SINK:V_SINK + 4],
                      a["a_sinks"].unsqueeze(0).broadcast_to([P, DEPTH, 4])).then_inc(lam_in, 16)
        act.wait_ge(const_in, 16)
        act.wait_ge(tr_done, 2)
        for l in range(DEPTH):
            nc.scalar.activation(lay[:, l, 0:N_VEC], ps[6 + l][:, 0:N_VEC], ACT.Copy
                                 ).then_inc(start_act, 1)
        nc.scalar.activation(c_act[:], ps[6][:, V_C:V_C + KD], ACT.Silu).then_inc(start_act, 1)
        act.wait_ge(start_dve, 1)
        nc.scalar.activation(lam_s[:], lam_s[:], ACT.Exp).then_inc(start_act, 1)
        for n in range(2):
            act.wait_ge(start_dve, 2 + n)
            nc.scalar.activation(rot[:, 2 * n + 1], ang[n][:], ACT.Sin).then_inc(start_act, 1)
            nc.scalar.activation(rot[:, 2 * n], rot[:, 2 * n], ACT.Sin, scale=-1.0,
                                 bias=const[:, C_HPI:C_HPI + 1]).then_inc(start_act, 1)
        for k in range(KD):
            act.wait_ge(tr_done, 3 + k)
            nc.scalar.activation(x_t[:, k], ps[k % 4][:], ACT.Copy).then_inc(x_done, 1)
            if k >= 2:
                act.wait_ge(sq_added, k - 1)
            act.wait_ge(x_done, k + 1)
            nc.scalar.activation(sq[k % 2][:], x_t[:, k], ACT.Square).then_inc(sq_done, 1)

        def turned(l, u):
            act.wait_ge(swap_done, N_M * l + MOVED.index(u) + 1)
            nc.scalar.activation(UNITS[u][2], ps[6 + ROPED.index(u) % 2][:].rearrange(
                "p (t n) -> p t n", n=P), ACT.Copy).then_inc(turn_done, 1)

        def evac(l, u):
            _, kind, dst = UNITS[u]
            act.wait_ge(unit_done, N_U * l + u + 1)
            src = ps[u % 4][:]
            if kind == "kv":
                nc.scalar.activation(dst, src, ACT.Copy).then_inc(unit_out, 1)
                nc.scalar.activation(rel[0][:], src, ACT.Square).then_inc(kv_act, 1)
            elif u in ROPED:
                r = ROPED.index(u)
                scale = HD ** -0.5 if kind == "q64" else 1.0
                if r >= 2:
                    wait_in_place(act, l, r - 2)
                rows = 96 if u == UNIT_IK else P
                ins = nc.scalar.activation(q_raw[r % 2][0:rows, :], src[0:rows], ACT.Copy, scale=scale)
                if u == UNIT_IK:
                    nc.scalar.activation(q_raw[r % 2][96:128, :], src[0:IDX], ACT.Copy)
                    ins = nc.scalar.activation(iw_raw[96:100, 0:S], src[96:100], ACT.Copy)
                if kind in ("q64", "k64"):
                    for g in range(4):
                        ins = nc.scalar.activation(t_sin[r % 2][32 * g:32 * g + 32, :],
                                                   src[32 * (g ^ 1):32 * (g ^ 1) + 32], ACT.Copy,
                                                   scale=scale if g % 2 else -scale)
                ins.then_inc(unit_out, 1)
            else:
                n = dst.shape[2]
                nc.scalar.activation(dst[:], src[:, 0:NT * n].rearrange("p (t n) -> p t n", n=n),
                                     ACT.Copy).then_inc(unit_out, 1)

        def mixer_projections(l):
            def outs(n, last):
                for u in [u for u in range(N_U) if UNITS[u][0] == n][slice(1, 9) if last else slice(1)]:
                    evac(l, u)
                    if u - 1 in TURNED:
                        turned(l, u - 1)
                    for x in IDX_AFTER.get(u, ()):
                        nn = P * (IDX_ITEMS[x][0] + 1)
                        act.wait_ge(idx_done, N_I * l + x + 1)
                        if x >= 2:
                            act.wait_ge(idx_acc, N_I * l + x - 1)
                        nc.scalar.activation(rel[x % 2][:, 0:nn], ps[4 + x % 2][:, 0:nn], ACT.Relu
                                             ).then_inc(relu_done, 1)

            for n in range(MIX_BLOCKS):
                split_hi(l, MIX_0 + n + 1)
                if n == MIX_BLOCKS - 1:
                    have_table(ACT.Exp, 0)
                outs(n - 1, True)
                outs(n, False)
                if n == 1:
                    act.wait_ge(kv_sum, l + 1)
                    root_of_mean(rel[1][:], ps[SUM][:], P).then_inc(kv_act, 1)
                if n == 3:
                    act.wait_ge(kvn_done, l + 1)
                    nc.scalar.activation(kvn_hi[:], kv_raw[:], ACT.Copy).then_inc(kvn_hi_done, 1)
                if n == 4:
                    wait_in_place(act, l, ROPED.index(UNIT_AK))
                    nc.scalar.activation(akx[0:64, :], ak[64:128, :], ACT.Copy).then_inc(akx_done, 1)
                    nc.scalar.activation(akx[64:128, :], ak[0:64, :], ACT.Copy).then_inc(akx_done, 1)
            outs(MIX_BLOCKS - 1, True)

        def exps(l, it):
            b, fam, _, _, _ = ITEMS[it]
            nn = keys_of(b, fam)[1]
            par = b % 2
            if b >= 2 and items_through(b - 1, "C") == it:
                act.wait_ge(y_out, 2 * NT * l + 2 * (b - 1))
            for su, maps in banks_of(it):
                act.wait_ge(max_done, N_SU * l + su + 1)
                for n, m in enumerate(maps):
                    c = stat(fam, m)
                    cols = slice(n * nn, (n + 1) * nn)
                    ins = nc.scalar.activation(e_buf[su % 6][:, cols], ps[su % 4][:, cols], ACT.Exp,
                                               bias=stats_n[:, par, c:c + 1],
                                               accum_out=stats_s[:, par, c:c + 1])
                ins.then_inc(exp_done, 1)
            if it + 1 == items_through(b, "A"):
                act.wait_ge(sink_in, NT * l + b + 1)
                nc.scalar.activation(stats_e[:, par], stats_x[:, par], ACT.Exp).then_inc(sink_done, 1)

        def evac_p(l, it):
            b, fam, _, _, _ = ITEMS[it]
            nn = keys_of(b, fam)[1] * len(heads_of(it))
            act.wait_ge(pt_psum, N_IT * l + it + 1)
            if it >= 2:
                act.wait_ge(pv_done, N_IT * l + it - 1)
            nc.scalar.activation(p_t[it % 2][:, 0:nn], ps[6 + it % 2][:, 0:nn], ACT.Copy
                                 ).then_inc(pt_done, 1)

        def root_c(l, last):
            cols = slice(4 * (NT - 1), 4 * NT) if last else slice(0, 4 * (NT - 1))
            act.wait_ge(css_done, NT * l + (NT if last else NT - 1))
            nc.scalar.activation(c_rs[:, cols], c_ss[:, cols], ACT.Sqrt, scale=1.0 / P,
                                 bias=const[:, C_EPS:C_EPS + 1]).then_inc(csd_done, 1)

        def attention(l):
            act.wait_ge(kvn_lo_done, l + 1)
            act.wait_ge(rope_done, N_R * (l + 1))
            turned(l, N_U - 1)
            for it in range(N_IT):
                exps(l, it)
                if it >= 2:
                    evac_p(l, it - 2)
            evac_p(l, N_IT - 2)
            root_c(l, 0)
            evac_p(l, N_IT - 1)
            for n in range(2 * NT):
                b, c = n % NT, n // NT
                if n == NT:
                    root_c(l, 1)
                act.wait_ge(yt_done, 2 * NT * l + n + 1)
                nc.scalar.activation(h_hi[:, 4 * c:4 * c + 4, b * P:(b + 1) * P],
                                     ps[Y_BANKS[n]][:].rearrange("p (t s) -> p t s", s=P), ACT.Copy,
                                     scale=cur[:, V_SUBG:V_SUBG + 1] if c else 1.0
                                     ).then_inc(yhi_done, 1)

        with act.Fori(0, DEPTH) as l:
            norm(l, 0)
            ffn(l, 0)
            norm(l, 1)
            mixer_projections(l)
            attention(l)

            def out_step(i, p, prepared):
                split_hi(l, prepared, i)
                if isinstance(i, int) and p == 1:
                    have_table(ACT.Sqrt, 1)
                square(KD + X_TILES * l + 2 * KD + p + 2 * i, l, 2, i, p, p)

            run_segment(act, OUT_0, KD // 2, out_step)
            norm(l, 2)
            ffn(l, 1)

        act.wait_ge(sum_done, NORMS * DEPTH + 1)
        root_of_mean(sd[:], ps[SUM][:, 0:NT], D).then_inc(sd_done, 1)
        act.wait_ge(rstd_done, NORMS * DEPTH + 1)
        for n in range(0, 2 * NT, 2):
            act.wait_ge(ftr_done, n + 1)
            nc.scalar.activation(out_nat[:, n // 2, 0:S], ps[n % 4][:], ACT.Copy,
                                 scale=rstd[:, n // 2:n // 2 + 1]).then_inc(fout_a, 1)

    @block.vector
    def _(dve):
        def split_lo(l, s, i=0):
            dve.wait_ge(hi_done, BLOCKS * l + s + 2 * i + 1)
            for raw, hi, lo in split_views(s + 2 * i if isinstance(i, int) else s, s % 2):
                ins = nc.vector.tensor_tensor(lo, raw, hi.bitcast(F32), ALU.subtract)
            ins.then_inc(lo_done, 1)

        def clear(l, q):
            nc.vector.memset(macc[q % N_MOD % 2][:], 0.0).then_inc(acc_zero, 1)
            dve.wait_ge(acc_zero, N_MOD * l + q - 1)
            fence(dve)

        def chunk(l, q, k, p):
            acc = macc[q % N_MOD % 2][:]
            dve.wait_ge(wm_in[p], 16 * (KD // 2) * N_MOD * l + 16 * (KD // 2) * (q - 2)
                        + 8 * (k - p) + 16)
            dve.wait_ge(wm_used, KD * N_MOD * l + KD * q + k + CREDIT)
            nc.vector.scalar_tensor_tensor(acc, wm[p][:], c_act[:, bass.ds(k, 1)], acc,
                                           ALU.mult, ALU.add).then_inc(wm_used, 1)

        def module_out(l, q):
            m = q % N_MOD
            n, par = m // 3, m % 2
            dve.wait_ge(mod_sum, N_MOD * l + q + 1)
            fence(dve)
            ins = nc.vector.tensor_tensor(modc[:, m], ps[MISC[par]][:, 0:8],
                                          cur[:, V_B + 8 * m:V_B + 8 * m + 8], ALU.add)
            if m % 3:
                ins.then_inc(mod_step, 1)
                dve.wait_ge(mod_step, 2 * NORMS * l + q - q // 3)
                if m % 3 == 1:
                    g = (V_N1, V_NM, V_N2)[n]
                    ins = nc.vector.scalar_tensor_tensor(coef[:, n], modc[:, m], 1.0,
                                                         cur[:, g:g + KD], ALU.add, ALU.mult)
                else:
                    ins = nc.vector.tensor_scalar(gate[:, n], modc[:, m], 1.0 if n == 1 else 0.5,
                                                  None, ALU.mult)
            ins.then_inc(mod_out, 1)
            dve.wait_ge(mod_out, N_MOD * l + q + 1)
            fence(dve)

        def norm(l, n):
            v = NORMS * l + n
            dve.wait_ge(sd_done, v + 1)
            nc.vector.reciprocal(rstd[:], sd[:]).then_inc(rstd_done, 1)
            dve.wait_ge(rstd_done, v + 1)
            for t in range(NT):
                fence(dve)
                nc.vector.tensor_scalar(diag[:, t], ident, rstd[:, t:t + 1], None, ALU.mult
                                        ).then_inc(diag_done, 1)
            if n == 0:
                split_lo(l, 0)
                for q in range(2):
                    module_out(l, q)

            def rest(k):
                dve.wait_ge(hhi_done, KD * v + k + 1)
                nc.vector.scalar_tensor_tensor(h_lo[:, k], xn[k % 3][:], modc[:, 3 * n, k:k + 1],
                                               h_hi[:, k].bitcast(F32), ALU.add, ALU.subtract
                                               ).then_inc(hlo_done, 1)

            dve.wait_ge(spread_done, v + 1)
            for k in range(KD):
                if k >= 3:
                    dve.wait_ge(hlo_done, KD * v + k - 2)
                nc.vector.scalar_tensor_tensor(xn[k % 3][:], x_t[:, k], coef[:, n, k:k + 1],
                                               ps[SUM][:], ALU.mult, ALU.mult).then_inc(xn_done, 1)
                if k:
                    rest(k - 1)
            rest(KD - 1)

        def x_update(s, p, k, g):
            dve.wait_ge(blk_done, s + 1 + CREDIT)
            xk = at_col(x_t, k)
            nc.vector.scalar_tensor_tensor(xk, ps[2 * p][:], gate[:, g, bass.ds(k, 1)], xk,
                                           ALU.mult, ALU.add).then_inc(x_done, 1)

        def ffn(l, which):
            before = None
            for kind, half, pairs, module, s0, step, f0 in walk(which):
                if module is not None:
                    clear(l, module)

                def body(i, p, prepared):
                    if prepared is not None:
                        split_lo(l, prepared, i)
                    if kind == "out":
                        x_update(used(l, s0 + p) + 2 * i, p, 2 * i + (step + p), 2 * which)
                    if module is not None:
                        for k, slot in chunks_of(pairs, i, p):
                            chunk(l, module, k, slot)
                    if kind == "in":
                        f = 2 * F_TILES * l + f0 + p + 2 * i
                        dve.wait_ge(silu_done, f + 1)
                        nc.vector.tensor_tensor(a_f[p][:], ps[2 * p + 1][:], sil[p][:], ALU.mult
                                                ).then_inc(mul_done, 1)
                        dve.wait_ge(ahi_done, f + 1)
                        k = 2 * i + (step + p)
                        nc.vector.tensor_tensor(at_col(a_lo, k), a_f[p][:],
                                                at_col(a_hi, k).bitcast(F32), ALU.subtract
                                                ).then_inc(alo_done, 1)

                run_segment(dve, s0, pairs, body)
                if before is not None:
                    module_out(l, before)
                before = module if module not in NEXT_LAYER else None
            if before is not None:
                module_out(l, before)

        boots = [0]

        def boot(ins):
            boots[0] += 1
            ins.then_inc(boot_step, 1)
            dve.wait_ge(boot_step, boots[0])

        dve.sem_inc(lo_done, CREDIT)
        dve.sem_inc(wm_used, CREDIT)
        dve.wait_ge(const_in, 16)
        nc.vector.tensor_copy(id_bf[:], ident)
        nc.vector.tensor_copy(mask_bf[:], const[:, C_MASK:C_MASK + 256])
        dve.wait_ge(lam_in, 16 * 5)
        boot(nc.vector.tensor_tensor(lam_p[:], lam_v[:, 0:4:2], lam_v[:, 1:4:2], ALU.mult))
        nc.vector.tensor_reduce(lam_s[:], lam_p[:], AX.X, ALU.add).then_inc(start_dve, 1)
        dve.wait_ge(pos_in, 16)
        boot(nc.vector.tensor_copy(pos_f[:], pos_i[:]))
        for n in range(2):
            turn = rot[:, 2 * n]
            boot(nc.vector.tensor_scalar(ang[n][:], pos_f[:], const[:, C_INV + n:C_INV + n + 1], None,
                                         ALU.mult))
            boot(nc.vector.tensor_scalar(turn, ang[n][:], 1.0 / TWO_PI, ROUND, ALU.mult, ALU.add))
            boot(nc.vector.tensor_scalar(turn, turn, ROUND, None, ALU.subtract))
            for part in (PI_A, PI_B, PI_C):
                boot(nc.vector.scalar_tensor_tensor(ang[n][:], turn, -part, ang[n][:],
                                                    ALU.mult, ALU.add))
            boot(nc.vector.tensor_scalar(ang[n][:], ang[n][:], PI_LO, -PI_LO, ALU.min, ALU.max))
            nc.vector.scalar_tensor_tensor(turn, ang[n][:], -1.0, ang[n][:], ALU.mult, ALU.max
                                           ).then_inc(start_dve, 1)
        dve.wait_ge(start_act, 4)
        nc.vector.tensor_scalar(lay[:, :, V_NSINK:V_NSINK + 4], lay[:, :, V_SINK:V_SINK + 4], -1.0,
                                None, ALU.mult)
        boot(nc.vector.tensor_tensor(lam_s[:, 0], lam_s[:, 1], lam_s[:, 0], ALU.subtract))
        nc.vector.tensor_tensor(lay[:, :, V_NLAM], lam_s[:, 0], const[:, C_LI:C_LI + DEPTH],
                                ALU.subtract)
        boot(nc.vector.tensor_tensor(lay[:, :, V_SUBG], lay[:, :, V_SUB],
                                     const[:, C_1LI:C_1LI + DEPTH], ALU.mult))
        for q in range(2):
            for k in range(KD):
                src = boot_wm[4 * q + k // 2][:, k % 2]
                dve.wait_ge(boot_in[4 * q + k // 2], 16)
                if k == 0:
                    ins = nc.vector.tensor_scalar(macc[q][:], src, c_act[:, k:k + 1], None, ALU.mult)
                else:
                    dve.wait_ge(wm_used, 8 * q + k + CREDIT)
                    ins = nc.vector.scalar_tensor_tensor(macc[q][:], src, c_act[:, k:k + 1],
                                                         macc[q][:], ALU.mult, ALU.add)
                ins.then_inc(wm_used, 1)

        chain = [0]

        def link(l, ins):
            chain[0] += 1
            ins.then_inc(dve_step, 1)
            dve.wait_ge(dve_step, CHAIN * l + chain[0])

        def mark(ins):
            chain[0] += 1
            ins.then_inc(dve_step, 1)
            return chain[0]

        def need(l, number):
            dve.wait_ge(dve_step, CHAIN * l + number)

        def rope(l, u):
            kind, dst = UNITS[u][1:]
            r = ROPED.index(u)
            if u in MOVED:
                dve.wait_ge(swap_done, N_M * l + MOVED.index(u) + 1)
            t = 2 if kind == "i32" else 0
            dve.wait_ge(unit_out, N_U * l + u + 1)
            nc.vector.tensor_tensor(t_cos[r % 2][:], q_raw[r % 2][:], rot[:, t], ALU.mult)
            swapped = ps[6 + r % 2][:] if kind == "i32" else t_sin[r % 2][:]
            link(l, nc.vector.tensor_tensor(t_sin[r % 2][:], swapped, rot[:, t + 1], ALU.mult))
            nc.vector.tensor_tensor(dst, t_cos[r % 2][:], t_sin[r % 2][:], ALU.add
                                    ).then_inc(rope_done, 1)

        def index_score(l, x):
            b, h = IDX_ITEMS[x]
            nn = P * (b + 1)
            dst = score[:, score_at[b]:score_at[b] + nn]
            dve.wait_ge(relu_done, N_I * l + x + 1)
            w = iw[:, b, h:h + 1]
            if h:
                ins = nc.vector.scalar_tensor_tensor(dst, rel[x % 2][:, 0:nn], w, dst,
                                                     ALU.mult, ALU.add)
            else:
                ins = nc.vector.tensor_scalar(dst, rel[x % 2][:, 0:nn], w, 0.0, ALU.mult, ALU.add)
            ins.then_inc(idx_acc, 1)
            dve.wait_ge(idx_acc, N_I * l + x + 1)
            if h == 3:
                link(l, nc.vector.memset(score[0:64, score_at[b] + nn - 64:score_at[b] + nn], -BIG))

        def topk(l, b, r0, r1, between=None):
            nn = P * (b + 1)
            work = score[:, score_at[b]:score_at[b] + nn]
            for r in range(r0, r1):
                if between is None:
                    fence(dve)
                    link(l, nc.vector.max(top8[:], work))
                    fence(dve)
                    link(l, nc.vector.match_replace(work, top8[:], work, -3e38))
                else:
                    number = mark(nc.vector.max(top8[:], work))
                    between()
                    need(l, number)
                    fence(dve)
                    number = mark(nc.vector.match_replace(work, top8[:], work, -3e38))
            if r1 == TK:
                if between is not None:
                    need(l, number)
                nc.vector.tensor_scalar(sel_bf[:, score_at[b]:score_at[b] + nn], work, -2e38, -BIG,
                                        ALU.is_gt, ALU.mult).then_inc(sel_done, 1)
            return None if between is None else number

        def mixer_projections(l):
            def outs(n, last):
                for u in [u for u in range(N_U) if UNITS[u][0] == n][slice(1, 9) if last else slice(1)]:
                    if u in ROPED and u not in TURNED:
                        rope(l, u)
                    for x in IDX_AFTER.get(u, ()):
                        index_score(l, x)

            for n in range(MIX_BLOCKS):
                split_lo(l, MIX_0 + n + 1)
                outs(n - 1, True)
                if n == 2:
                    dve.wait_ge(iw_turned, l + 1)
                    nc.vector.tensor_copy(iw[:], ps[5][:, 0:NT * 4].rearrange("p (t n) -> p t n", n=4)
                                          ).then_inc(iw_done, 1)
                    dve.wait_ge(kv_act, 2 * l + 2)
                    link(l, nc.vector.reciprocal(rel[1][:], rel[1][:]))
                    nc.vector.scalar_tensor_tensor(kv_raw[:], kv_raw[:], cur[:, V_KV:V_KV + 1],
                                                   rel[1][:], ALU.mult, ALU.mult).then_inc(kvn_done, 1)
                    dve.wait_ge(iw_done, l + 1)
                    fence(dve)
                if n == 4:
                    dve.wait_ge(kvn_hi_done, l + 1)
                    nc.vector.tensor_tensor(kvn_lo[:], kv_raw[:], kvn_hi[:].bitcast(F32),
                                            ALU.subtract).then_inc(kvn_lo_done, 1)
                for part in TOPK_PLAN.get(n, []):
                    topk(l, *part)
                outs(n, False)
            outs(MIX_BLOCKS - 1, True)

        def maxima(l, it):
            b, fam, _, _, _ = ITEMS[it]
            nn = keys_of(b, fam)[1]
            par = b % 2
            for su, maps in banks_of(it):
                c, n = stat(fam, maps[0]), len(maps)
                neg = stats_n[:, par, c:c + 2 * n - 1:2]
                dve.wait_ge(sc_done, N_SU * l + su + 1)
                ins = nc.vector.tensor_reduce(neg, ps[su % 4][:, 0:n * nn].rearrange(
                    "p (m k) -> p m k", m=n), AX.X, ALU.max, negate=True)
                if fam == "A":
                    link(l, ins)
                    sink = V_NSINK + c
                    ins = nc.vector.tensor_tensor(neg, neg, cur[:, sink:sink + 2 * n - 1:2], ALU.min)
                ins.then_inc(max_done, 1)

        def sinks(l, b):
            last_bank = banks_of(items_through(b, "A") - 1)[-1][0]
            dve.wait_ge(max_done, N_SU * l + last_bank + 1)
            nc.vector.tensor_tensor(stats_x[:, b % 2], cur[:, V_SINK:V_SINK + 4],
                                    stats_n[:, b % 2, 0:4], ALU.add).then_inc(sink_in, 1)

        def combine(l, it):
            b, fam, maps, per, su0 = ITEMS[it]
            nn = keys_of(b, fam)[1]
            heads = heads_of(it)
            c, end = stat(fam, maps[0]), stat(fam, maps[-1]) + 1
            sums = stats_s[:, b % 2]
            dve.wait_ge(exp_done, N_SU * l + banks_of(it)[-1][0] + 1)
            link(l, nc.vector.reciprocal(stats_r[:, c:end:2], sums[:, c + 1:end:2]))
            link(l, nc.vector.scalar_tensor_tensor(stats_r[:, c + 1:end:2], stats_r[:, c:end:2],
                                                   cur[:, V_NLAM:V_NLAM + 1], sums[:, c:end:2],
                                                   ALU.mult, ALU.mult))
            for n in range(len(heads)):
                e0, e1 = (e_buf[(su0 + j) % 6][:, n * nn:(n + 1) * nn] for j in range(2))
                ins = nc.vector.scalar_tensor_tensor(e0, e1, stats_r[:, c + 2 * n + 1:c + 2 * n + 2],
                                                     e0, ALU.mult, ALU.add)
            ins.then_inc(comb_done, 1)

        def y_ab_out(l, b):
            par = b % 2
            dve.wait_ge(pv_done, N_IT * l + items_through(b, "B"))
            dve.wait_ge(sink_done, NT * l + b + 1)
            nc.vector.tensor_tensor(stats_f[:, 0:4], stats_s[:, par, 0:4], stats_e[:, par], ALU.add)
            link(l, nc.vector.tensor_copy(stats_f[:, 4:8], stats_s[:, par, 4:8]))
            link(l, nc.vector.reciprocal(stats_f[:, 0:8], stats_f[:, 0:8]))
            nc.vector.tensor_tensor(y_ab[:, b].rearrange("p (h e) -> p h e", h=8),
                                    ps[4][:].rearrange("p (h e) -> p h e", h=8),
                                    stats_f[:, 0:8].unsqueeze(2).broadcast_to([P, 8, HD]), ALU.mult
                                    ).then_inc(y_out, 1)

        def y_c_out(l, b):
            dve.wait_ge(pv_done, N_IT * l + items_through(b, "C"))
            link(l, nc.vector.reciprocal(stats_f[:, 8:12], stats_s[:, b % 2, 8:16:2]))
            nc.vector.tensor_tensor(y_c[:, b].rearrange("p (h e) -> p h e", h=4),
                                    ps[5][:].rearrange("p (h e) -> p h e", h=4),
                                    stats_f[:, 8:12].unsqueeze(2).broadcast_to([P, 4, P]), ALU.mult
                                    ).then_inc(y_out, 1)
            dve.wait_ge(y_out, 2 * NT * l + 2 * b + 2)
            link(l, nc.vector.tensor_tensor(c_sq[:], y_c[:, b], y_c[:, b], ALU.mult))
            nc.vector.tensor_reduce(c_ss[:, 4 * b:4 * b + 4], c_sq[:].rearrange(
                "p (h e) -> p h e", h=4), AX.X, ALU.add).then_inc(css_done, 1)

        def norm_c(l, last):
            tiles = range(NT - 1, NT) if last else range(NT - 1)
            cols = c_rs[:, 4 * tiles.start:4 * tiles.stop]
            dve.wait_ge(csd_done, 2 * l + last + 1)
            link(l, nc.vector.reciprocal(cols, cols))
            for b in tiles:
                yb = y_c[:, b].rearrange("p (h e) -> p h e", h=4)
                nc.vector.tensor_tensor(yb, yb, c_rs[:, 4 * b:4 * b + 4].unsqueeze(2)
                                        .broadcast_to([P, 4, P]), ALU.mult).then_inc(cn_done, 1)

        def attention(l):
            last = None
            for it in range(N_IT + 4):
                b, fam = ITEMS[min(it, N_IT - 1)][:2]

                def now():
                    if it < N_IT:
                        maxima(l, it)
                        if it + 1 == items_through(b, "A"):
                            sinks(l, b)
                    if 1 <= it <= N_IT and ITEMS[it - 1][1] == "C":
                        combine(l, it - 1)

                if it in LATE_ROUNDS:
                    if last is not None:
                        need(l, last)
                    fence(dve)
                    kt, rnd = LATE_ROUNDS[it]
                    last = topk(l, kt, rnd, rnd + 1, now)
                else:
                    now()
                for t in range(NT):
                    if it == items_through(t, "B") + 3:
                        y_ab_out(l, t)
                    if it == items_through(t, "C") + 3:
                        if t == NT - 1:
                            norm_c(l, 0)
                        y_c_out(l, t)
            for n in range(2 * NT):
                b, c = n % NT, n // NT
                if n == NT:
                    norm_c(l, 1)
                dve.wait_ge(yhi_done, 2 * NT * l + n + 1)
                hi, lo = (h[:, 4 * c:4 * c + 4, b * P:(b + 1) * P] for h in (h_hi, h_lo))
                src = ps[Y_BANKS[n]][:].rearrange("p (t s) -> p t s", s=P)
                if c:
                    ins = nc.vector.scalar_tensor_tensor(lo, src, cur[:, V_SUBG:V_SUBG + 1],
                                                         hi.bitcast(F32), ALU.mult, ALU.subtract)
                else:
                    ins = nc.vector.tensor_tensor(lo, src, hi.bitcast(F32), ALU.subtract)
                ins.then_inc(ylo_done, 1)

        dve.wait_ge(start_act, 8)
        with dve.Fori(0, DEPTH) as l:
            nc.vector.tensor_copy(cur[:], at_col(lay, l)).then_inc(cur_done, 1)
            dve.wait_ge(cur_done, l + 1)
            norm(l, 0)
            ffn(l, 0)
            norm(l, 1)
            mixer_projections(l)
            attention(l)
            assert chain[0] == CHAIN, chain

            def out_step(i, p, prepared):
                split_lo(l, prepared, i)
                x_update(used(l, OUT_0 + p) + 2 * i, p, 2 * i + p, 1)

            run_segment(dve, OUT_0, KD // 2, out_step)
            norm(l, 2)
            ffn(l, 1)

        dve.wait_ge(sq_done, KD * (NORMS * DEPTH + 1))
        for k in range(KD):
            nc.vector.tensor_scalar(x_t[:, k], x_t[:, k], lay[:, 0, V_FIN + k:V_FIN + k + 1], None,
                                    ALU.mult).then_inc(fin_done, 1)
        dve.wait_ge(sd_done, NORMS * DEPTH + 1)
        nc.vector.reciprocal(rstd[:], sd[:]).then_inc(rstd_done, 1)
        dve.wait_ge(rstd_done, NORMS * DEPTH + 1)
        for n in range(1, 2 * NT, 2):
            dve.wait_ge(ftr_done, n + 1)
            nc.vector.tensor_scalar(out_nat[:, n // 2, S:2 * S], ps[n % 4][:],
                                    rstd[:, n // 2:n // 2 + 1], None, ALU.mult).then_inc(fout_b, 1)

    @block.gpsimd
    def _(pool):
        with pool.Fori(0, NORMS * DEPTH + 1) as v:
            for k in range(KD - 1):
                pool.wait_ge(sq_done, KD * v + k + 1)
                fence(pool)
                if k == 0:
                    ins = nc.gpsimd.tensor_copy(sq_sum[:], sq[0][:])
                else:
                    pool.wait_ge(sq_added, (KD - 1) * v + k)
                    fence(pool)
                    ins = nc.gpsimd.tensor_tensor(sq_sum[:], sq_sum[:], sq[k % 2][:], ALU.add)
                ins.then_inc(sq_added, 1)

    @block.tensor
    def _(pe):
        def product(dst, w, h, first, last):
            nc.tensor.matmul(dst, w[0], h[1], start=first, stop=False, skip_group_check=True)
            nc.tensor.matmul(dst, w[1], h[0], start=False, stop=False, skip_group_check=True)
            return nc.tensor.matmul(dst, w[0], h[0], start=False, stop=last, skip_group_check=True)

        def normed_products(dsts, ws, v, k):
            pe.wait_ge(hhi_done, KD * v + k + 1)
            for dst, w in zip(dsts, ws):
                for part in (1, 0):
                    nc.tensor.matmul(dst, w[part], h_hi[:, k], start=(k == 0 and part == 1),
                                     stop=False, skip_group_check=True)
            pe.wait_ge(hlo_done, KD * v + k + 1)
            return [nc.tensor.matmul(dst, w[0], h_lo[:, k], start=False, stop=(k == KD - 1),
                                     skip_group_check=True) for dst, w in zip(dsts, ws)]

        def sum_squares(v):
            pe.wait_ge(sq_added, (KD - 1) * (v + 1))
            pe.wait_ge(sq_done, KD * (v + 1))
            for t in range(NT):
                for src in (sq_sum, sq[(KD - 1) % 2]):
                    ins = nc.tensor.matmul(ps[SUM][:, t:t + 1], src[:, t * P:(t + 1) * P],
                                           ones[:, 0:1], start=src is sq_sum,
                                           stop=src is not sq_sum)
            ins.then_inc(sum_done, 1)

        def spread(v):
            for t in range(NT):
                pe.wait_ge(diag_done, NT * v + t + 1)
                ins = nc.tensor.matmul(ps[SUM][:, t * P:(t + 1) * P], ones, diag[:, t],
                                       start=True, stop=True)
            ins.then_inc(spread_done, 1)

        def module_sum(l, q):
            pe.wait_ge(wm_used, KD * N_MOD * l + KD * q + 8 + CREDIT)
            par = q % N_MOD % 2
            for t in range(KD):
                ins = nc.tensor.matmul(ps[MISC[par]][:, t:t + 1],
                                       macc[par][:, t * P:(t + 1) * P], ones[:, 0:1],
                                       start=True, stop=True)
            ins.then_inc(mod_sum, 1)

        def ffn(l, which):
            before = None
            for kind, half, pairs, module, s0, step, f0 in walk(which):
                nf = HALVES[half][1]
                v = NORMS * l + 2 * which

                def body(i, p):
                    pe.wait_ge(lo_done, BLOCKS * l + s0 + p + 2 * i + 1 + CREDIT)
                    if kind == "in":
                        w = [wb[p][:].rearrange("p (k g f) -> p k g f", k=KD, g=2)
                             for wb in (w_hi, w_lo)]
                        for k in range(KD):
                            dsts = [ps[2 * p + g][:] for g in range(2)]
                            parts = [[t[:, k, g] for t in w] for g in range(2)]
                            if half == 0 and step == 0 and p == 0:
                                ins = normed_products(dsts, parts, v, k)[-1]
                                continue
                            for dst, part in zip(dsts, parts):
                                ins = product(dst, part, (h_hi[:, k], h_lo[:, k]), k == 0,
                                              k == KD - 1)
                    else:
                        w = [wb[p][:, 0:nf * P].rearrange("p (f n) -> p f n", n=P)
                             for wb in (w_hi, w_lo)]
                        for f in range(nf):
                            if f in (0, nf - 1):
                                pe.wait_ge(alo_done, 2 * F_TILES * l + f0 - (1 if f == 0 else 0))
                            ins = product(ps[2 * p][:], [t[:, f] for t in w],
                                          (a_hi[:, f], a_lo[:, f]), f == 0, f == nf - 1)
                    ins.then_inc(blk_done, 1)

                with pe.Fori(0, pairs) as i:
                    for p in range(2):
                        body(i, p)
                if before is not None:
                    module_sum(l, before)
                before = module if module not in NEXT_LAYER else None
            if before is not None:
                module_sum(l, before)
            sum_squares(NORMS * l + 1 + 2 * which)

        pe.sem_inc(blk_done, CREDIT)
        pe.wait_ge(const_in, 16)
        pe.wait_ge(vec_in, 16 * VEC_DMAS)
        for l in range(DEPTH):
            nc.tensor.transpose(ps[6 + l][:, 0:N_VEC], vec_rows[0:N_VEC, l],
                                ident[0:N_VEC, 0:N_VEC]).then_inc(tr_done, 1)
        pe.wait_ge(x_in, 16 * 2)
        for k in range(KD):
            if k >= 4:
                pe.wait_ge(x_done, k - 3)
            for t in range(NT):
                ins = nc.tensor.transpose(ps[k % 4][:, t * P:(t + 1) * P],
                                          x_nat[:, t, k * P:(k + 1) * P], ident)
            ins.then_inc(tr_done, 1)
        sum_squares(0)

        def swap(l, u):
            r = ROPED.index(u)
            pe.wait_ge(unit_out, N_U * l + u + 1)
            if r >= 2:
                wait_in_place(pe, l, r - 2)
            if UNITS[u][1] == "i32":
                ins = nc.tensor.matmul(ps[6 + r % 2][:], const[:, C_P32:C_P32 + P], q_raw[r % 2][:],
                                       start=True, stop=True)
            else:
                for t in range(NT):
                    ins = nc.tensor.transpose(ps[6 + r % 2][:, t * P:(t + 1) * P],
                                              q_raw[r % 2][:, t * P:(t + 1) * P], ident)
            ins.then_inc(swap_done, 1)
            if u == UNIT_IK:
                for t in range(NT):
                    ins = nc.tensor.transpose(ps[5][:, 4 * t:4 * t + 4],
                                              iw_raw[96:100, t * P:(t + 1) * P],
                                              ident[96:100, 96:100])
                ins.then_inc(iw_turned, 1)

        def project(l, u):
            n, kind, dst = UNITS[u]
            p = n % 2
            bank = ps[u % 4]
            if u >= 4:
                pe.wait_ge(unit_out, N_U * l + u - 3)
            first = u == 0 or UNITS[u - 1][0] != n
            if n == KV_UP:
                pe.wait_ge(kvn_lo_done, l + 1)
                if kind == "k64":
                    ins = product(bank[:], (w_hi[p][:, 0:P], w_lo[p][:, 0:P]),
                                  (kvn_hi[:], kvn_lo[:]), True, True)
                else:
                    for t in range(NT):
                        tok = slice(t * P, (t + 1) * P)
                        ins = product(bank[:, t * HD:(t + 1) * HD],
                                      (kvn_hi[:, tok], kvn_lo[:, tok]),
                                      (w_hi[p][:, P:P + HD], w_lo[p][:, P:P + HD]), True, True)
            else:
                cols = 100 if n == INDEX_KEYS else 256
                w = [wb[p][:, 0:KD * cols].rearrange("p (k n) -> p k n", n=cols)
                     for wb in (w_hi, w_lo)]
                c0, width = 0 if first else P, min(cols, P)
                for k in range(KD):
                    ins = product(bank[0:width, :], [x[:, k, c0:c0 + width] for x in w],
                                  (h_hi[:, k], h_lo[:, k]), k == 0, k == KD - 1)
            ins.then_inc(unit_done, 1)
            return ins

        def first_units(l):
            w = [wb[0][:].rearrange("p (k u n) -> p k u n", k=KD, u=2) for wb in (w_hi, w_lo)]
            for k in range(KD):
                both = normed_products([ps[u][:] for u in range(2)],
                                       [[x[:, k, u] for x in w] for u in range(2)],
                                       NORMS * l + 1, k)
            for ins in both:
                ins.then_inc(unit_done, 1)

        def mixer_projections(l):
            raw = None
            pe.wait_ge(mod_out, N_MOD * l + 8)
            for n in range(MIX_BLOCKS):
                pe.wait_ge(lo_done, BLOCKS * l + MIX_0 + n + 1 + CREDIT)
                for u in range(N_U):
                    if UNITS[u][0] != n:
                        continue
                    if u > 1:
                        project(l, u)
                    elif u == 1:
                        first_units(l)
                    if u == 2:
                        pe.wait_ge(kv_act, 2 * l + 1)
                        nc.tensor.matmul(ps[SUM][:], ones, rel[0][:], start=True, stop=True
                                         ).then_inc(kv_sum, 1)
                    if raw is not None:
                        swap(l, raw)
                    raw = u if u in MOVED else None
                    for x in IDX_AFTER.get(u, ()):
                        b, h = IDX_ITEMS[x]
                        if x == 0:
                            pe.wait_ge(rope_done, N_R * l + 2)
                            pe.wait_ge(kv_act, 2 * l + 2)
                            pe.wait_ge(iw_done, l + 1)
                        if x >= 2:
                            pe.wait_ge(relu_done, N_I * l + x - 1)
                        rows = slice(IDX * h, IDX * h + IDX)
                        nc.tensor.matmul(ps[4 + x % 2][:, 0:P * (b + 1)], iq[rows, b * P:(b + 1) * P],
                                         ik[rows, 0:P * (b + 1)], start=True, stop=True
                                         ).then_inc(idx_done, 1)
        def logits(l, it):
            b, fam, _, per, _ = ITEMS[it]
            k0, nn = keys_of(b, fam)
            tok = slice(b * P, (b + 1) * P)
            for su, _ in banks_of(it):
                if su >= 4:
                    pe.wait_ge(exp_done, N_SU * l + su - 3)
                else:
                    pe.wait_ge(unit_out, N_U * l + max(u for u in range(N_U) if u % 4 == su) + 1)

            def scores(su, n, m):
                h, j = m
                half = j if fam == "C" else h % 2
                rows = slice(64 * half, 64 * half + 64)
                if fam == "A":
                    q, k = aq[rows, h // 2, tok], (ak if h // 2 == half else akx)[rows, k0:k0 + nn]
                elif fam == "B":
                    q, k = bq[rows, h // 2, tok], bk[rows, k0:k0 + nn]
                else:
                    q, k = cq[rows, h, tok], ck[rows, h, k0:k0 + nn]
                nc.tensor.matmul(ps[su % 4][:, n * nn:(n + 1) * nn], q, k, start=True,
                                 stop=False, skip_group_check=True)

            def masked(su, n, m):
                if fam == "A" and b:
                    cols, mask = slice(0, nn), mask_bf[:]
                elif fam == "B" and b:
                    if m[0] == 0:
                        pe.wait_ge(sel_done, 3 * l + SEL_ORDER.index(b) + 1)
                    cols, mask = slice(0, nn), sel_bf[:, score_at[b]:score_at[b] + nn]
                else:
                    cols, mask = slice(nn - 64, nn), mask_bf[:, 192:256]
                ins = nc.tensor.matmul(ps[su % 4][:, n * nn:(n + 1) * nn][:, cols], id_bf[:], mask,
                                       start=False, stop=True, skip_group_check=True)
                if n == per - 1:
                    ins.then_inc(sc_done, 1)

            for su, maps in banks_of(it):
                for n, m in enumerate(maps):
                    scores(su, n, m)
                    if per > 1:
                        masked(su, n, m)
            if per == 1:
                for su, maps in banks_of(it):
                    masked(su, 0, maps[0])

        def turn_over(l, it):
            b, fam, _, per, su = ITEMS[it]
            nn = keys_of(b, fam)[1]
            if fam == "C":
                before = sum(item[1] == "C" for item in ITEMS[:it])
                pe.wait_ge(comb_done, N_C * l + before + 1)
            else:
                pe.wait_ge(exp_done, N_SU * l + su + 1)
            if it >= 2:
                pe.wait_ge(pt_done, N_IT * l + it - 1)
            for n in range(len(heads_of(it))):
                for j in range(nn // P):
                    cols = slice(n * nn + j * P, n * nn + (j + 1) * P)
                    ins = nc.tensor.transpose(ps[6 + it % 2][:, cols], e_buf[su % 6][:, cols], ident)
            ins.then_inc(pt_psum, 1)

        def weigh(l, it):
            b, fam, _, _, _ = ITEMS[it]
            k0, nn = keys_of(b, fam)
            pe.wait_ge(pt_done, N_IT * l + it + 1)
            if b and it == items_through(b - 1, "C"):
                pe.wait_ge(y_out, 2 * NT * l + 2 * (b - 1) + 1)
            if b and it == items_through(b, "B"):
                pe.wait_ge(y_out, 2 * NT * l + 2 * (b - 1) + 2)
            for n, h in enumerate(heads_of(it)):
                for j in range(nn // P):
                    t = k0 // P + j
                    if fam == "A":
                        g = h // 2
                        dst, v = ps[4][:, h * HD:(h + 1) * HD], av[:, t, g * HD:(g + 1) * HD]
                    elif fam == "B":
                        dst, v = ps[4][:, (4 + h) * HD:(5 + h) * HD], bv[:, t]
                    else:
                        dst, v = ps[5][:, h * P:(h + 1) * P], cv[:, t, h * P:(h + 1) * P]
                    ins = nc.tensor.matmul(dst, p_t[it % 2][:, n * nn + j * P:n * nn + (j + 1) * P],
                                           v, start=(j == 0), stop=(j == nn // P - 1),
                                           skip_group_check=True)
            ins.then_inc(pv_done, 1)

        def attention(l):
            pe.wait_ge(rope_done, N_R * (l + 1))
            pe.wait_ge(akx_done, 2 * l + 2)
            pe.wait_ge(relu_done, N_I * (l + 1))
            for it in range(N_IT + 3):
                if it < N_IT:
                    logits(l, it)
                if it == 0:
                    swap(l, N_U - 1)
                if it == 2:
                    pe.wait_ge(turn_done, N_T * (l + 1))
                if 2 <= it < N_IT + 2:
                    turn_over(l, it - 2)
                if it >= 3:
                    weigh(l, it - 3)
            pe.wait_ge(y_out, 2 * NT * (l + 1) - 1)
            pe.wait_ge(exp_done, N_SU * (l + 1))
            for n in range(2 * NT - 1):
                turn_y(l, n)

        def turn_y(l, n):
            b, c = n % NT, n // NT
            if c:
                pe.wait_ge(cn_done, NT * l + b + 1)
            for t in range(4):
                ins = nc.tensor.transpose(ps[Y_BANKS[n]][:, t * P:(t + 1) * P],
                                          (y_c if c else y_ab)[:, b, t * P:(t + 1) * P], ident)
            ins.then_inc(yt_done, 1)

        def output_projection(l):
            def body(i, p, ks=range(KD)):
                pe.wait_ge(lo_done, BLOCKS * l + OUT_0 + p + 2 * i + 1 + CREDIT)
                w = [wb[p][:, 0:KD * P].rearrange("p (k n) -> p k n", n=P) for wb in (w_hi, w_lo)]
                for k in ks:
                    ins = product(ps[2 * p][:], [t[:, k] for t in w], (h_hi[:, k], h_lo[:, k]),
                                  k == 0, k == KD - 1)
                if KD - 1 in ks:
                    ins.then_inc(blk_done, 1)

            pe.wait_ge(ylo_done, 2 * NT * l + NT)
            body(0, 0, range(4))
            turn_y(l, 2 * NT - 1)
            pe.wait_ge(ylo_done, 2 * NT * (l + 1))
            body(0, 0, range(4, KD))
            body(0, 1)
            with pe.Fori(1, KD // 2) as i:
                for p in range(2):
                    body(i, p)
            sum_squares(NORMS * l + 2)

        with pe.Fori(0, DEPTH) as l:
            module_sum(l, 0)
            spread(NORMS * l)
            module_sum(l, 1)
            ffn(l, 0)
            spread(NORMS * l + 1)
            mixer_projections(l)
            attention(l)
            output_projection(l)
            spread(NORMS * l + 2)
            ffn(l, 1)

        for n in range(2 * NT):
            t, g = n // 2, n % 2
            pe.wait_ge(fin_done, 4 * g + 4 if t == 0 else KD)
            if n >= 4:
                pe.wait_ge(fout_b if g else fout_a, n // 2 - 1)
            for j in range(4):
                ins = nc.tensor.transpose(ps[n % 4][:, j * P:(j + 1) * P],
                                          x_t[:, 4 * g + j, t * P:(t + 1) * P], ident)
            ins.then_inc(ftr_done, 1)

    ctx.close()


INPUTS = ["x", "c", "positions", "w_mod", "b_mod", "norm_ffn1", "w_ffn1_in", "w_ffn1_out", "norm_mix",
          "w_in", "a_sinks", "b_kv_norm", "w_kv_up", "c_lambda_q1", "c_lambda_k1", "c_lambda_q2",
          "c_lambda_k2", "c_subln", "w_out", "norm_ffn2", "w_ffn2_in", "w_ffn2_out", "final_norm"]


def kernel(**inputs):
    import concourse.bacc as bacc
    from concourse.bass_utils import run_bass_kernel_spmd

    nc = bacc.Bacc("TRN2", target_bir_lowering=False, num_devices=1)
    arrays = {f"in_{name}": np.ascontiguousarray(inputs[name]) for name in INPUTS}
    arrays["in_consts"] = constants()
    a = {name[3:]: nc.dram_tensor(name, v.shape, mybir.dt.from_np(v.dtype), kind="ExternalInput").ap()
         for name, v in arrays.items()}
    out = nc.dram_tensor("out", (1, S, D), F32, kind="ExternalOutput").ap()
    trunk(nc, a, out)
    r = run_bass_kernel_spmd(nc, [arrays], core_ids=[0])
    return r.results[0]["out"]
```
